# Optimizing a Trainium2 kernel written in Bass

```python
import math
import jax, jax.numpy as jnp
from jax import lax
import numpy as np

D_MODEL = 1024
BATCH = 1
SEQ = 512
DEPTH = 2

HEAD_DIM = 64
NSA_HEADS = 8
NSA_KV_HEADS = 2
NSA_WIDTH = NSA_HEADS * HEAD_DIM
NSA_KV_WIDTH = NSA_KV_HEADS * HEAD_DIM
CMP_BLOCK = 32
CMP_STRIDE = 16
CMP_HIDDEN = 256
SEL_BLOCK = 64
SEL_TOPK = 16
WINDOW = 512
NSA_Q_BLOCK = 64
DIFF_HEADS = 4
DIFF_QK_WIDTH = 2 * DIFF_HEADS * HEAD_DIM
DIFF_V_WIDTH = DIFF_HEADS * 2 * HEAD_DIM
DIFF_Q_BLOCK = 128
D_FF = -(-8 * D_MODEL // (3 * 256)) * 256
ROPE_THETA = 500000.0
ROPE_FRACTION = 4
ALPHA = (2 * DEPTH) ** 0.25
BETA = (8 * DEPTH) ** -0.25
EPS = 1e-5
NEG_INF = -1e30
FORCE_SCORE = 1e9
IN_SIZES = (NSA_WIDTH, NSA_KV_WIDTH, NSA_KV_WIDTH, NSA_KV_WIDTH, NSA_KV_WIDTH,
            NSA_KV_WIDTH, NSA_KV_WIDTH, NSA_HEADS * 3,
            DIFF_QK_WIDTH, DIFF_QK_WIDTH, DIFF_V_WIDTH, 2 * D_MODEL)
IN_COLS = sum(IN_SIZES)

kernel_name = "hybrid_nsa_diffattn_deepnorm_adaln"

def layer_norm(x, g, b):
    x32 = x.astype(jnp.float32)
    mu = jnp.mean(x32, -1, keepdims=True)
    var = jnp.mean(jnp.square(x32 - mu), -1, keepdims=True)
    return ((x32 - mu) * lax.rsqrt(var + EPS) * g + b).astype(x.dtype)

def rope_partial(t, pos):
    rot = t.shape[-1] // ROPE_FRACTION
    half = rot // 2
    inv_freq = ROPE_THETA ** (-jnp.arange(half, dtype=jnp.float32) * 2.0 / rot)
    ang = pos[:, None] * inv_freq[None, :]
    cos = jnp.cos(ang)[:, None, :]
    sin = jnp.sin(ang)[:, None, :]
    t1 = t[..., :half].astype(jnp.float32)
    t2 = t[..., half:rot].astype(jnp.float32)
    r1 = (t1 * cos - t2 * sin).astype(t.dtype)
    r2 = (t2 * cos + t1 * sin).astype(t.dtype)
    return jnp.concatenate([r1, r2, t[..., rot:]], axis=-1)

def masked_softmax(s, mask):
    return jax.nn.softmax(jnp.where(mask, s.astype(jnp.float32), NEG_INF), axis=-1)

def compress(k, pe, w1, w2):
    B, S, G, Dh = k.shape
    nc = (S - CMP_BLOCK) // CMP_STRIDE + 1
    idx = jnp.arange(nc)[:, None] * CMP_STRIDE + jnp.arange(CMP_BLOCK)[None, :]
    blk = k[:, idx] + pe[None, None, :, None, :]
    flat = blk.transpose(0, 1, 3, 2, 4).reshape(B, nc, G, CMP_BLOCK * Dh)
    return jax.nn.gelu(flat @ w1) @ w2

def cmp_to_sel_weights(nc, nb):
    cs = np.arange(nc) * CMP_STRIDE
    bs = np.arange(nb) * SEL_BLOCK
    ov = np.minimum(cs[:, None] + CMP_BLOCK, bs[None, :] + SEL_BLOCK) - np.maximum(cs[:, None], bs[None, :])
    return jnp.asarray(np.clip(ov, 0, None) / CMP_BLOCK, dtype=jnp.float32)

def nsa_attention(q, kc_raw, vc_raw, ks, vs, kw, vw, gates, pe_k, w1_k, w2_k, pe_v, w1_v, w2_v, pos):
    B, S, H, Dh = q.shape
    G = ks.shape[2]
    R = H // G
    C = NSA_Q_BLOCK
    nb = S // SEL_BLOCK
    topk = min(SEL_TOPK, nb)
    NK = topk * SEL_BLOCK
    scale = Dh ** -0.5
    q_rot = rope_partial(q, pos)
    ks = rope_partial(ks, pos)
    kw = rope_partial(kw, pos)
    k_cmp = compress(kc_raw, pe_k, w1_k, w2_k)
    v_cmp = compress(vc_raw, pe_v, w1_v, w2_v)
    nc = k_cmp.shape[1]
    cmp_end = jnp.arange(nc) * CMP_STRIDE + CMP_BLOCK - 1
    ov = cmp_to_sel_weights(nc, nb)
    ks_t = ks.transpose(0, 2, 1, 3)
    vs_t = vs.transpose(0, 2, 1, 3)
    pad = ((0, 0), (WINDOW, 0), (0, 0), (0, 0))
    kw_pad = jnp.pad(kw, pad)
    vw_pad = jnp.pad(vw, pad)
    blk_ids = jnp.arange(nb)
    b_idx = jnp.arange(B)[:, None, None]
    g_idx = jnp.arange(G)[None, :, None]

    def one_block(i):
        t0 = i * C
        t = t0 + jnp.arange(C)
        qb = lax.dynamic_slice_in_dim(q, t0, C, 1).reshape(B, C, G, R, Dh)
        qrb = lax.dynamic_slice_in_dim(q_rot, t0, C, 1).reshape(B, C, G, R, Dh)
        gb = lax.dynamic_slice_in_dim(gates, t0, C, 1).reshape(B, C, G, R, 3)
        valid_c = cmp_end[None, :] <= t[:, None]
        s = jnp.einsum('bcgrd,bngd->bcgrn', qb, k_cmp) * scale
        p_cmp = masked_softmax(s, valid_c[None, :, None, None, :])
        p_cmp = p_cmp * jnp.any(valid_c, -1)[None, :, None, None, None].astype(jnp.float32)
        o_cmp = jnp.einsum('bcgrn,bngd->bcgrd', p_cmp.astype(v_cmp.dtype), v_cmp)
        imp = jnp.einsum('bcgrn,nj->bcgj', p_cmp, ov)
        cur = t // SEL_BLOCK
        future = blk_ids[None, :] > cur[:, None]
        forced = (blk_ids[None, :] == 0) | (blk_ids[None, :] == cur[:, None]) | (blk_ids[None, :] == cur[:, None] - 1)
        imp = jnp.where(future[None, :, None, :], -jnp.inf,
                        jnp.where(forced[None, :, None, :], FORCE_SCORE, imp))
        _, sel = lax.top_k(imp, topk)
        tok = (sel[..., None] * SEL_BLOCK + jnp.arange(SEL_BLOCK)).reshape(B, C, G, NK)
        tok_t = tok.transpose(0, 2, 1, 3).reshape(B, G, C * NK)
        k_g = ks_t[b_idx, g_idx, tok_t].reshape(B, G, C, NK, Dh)
        v_g = vs_t[b_idx, g_idx, tok_t].reshape(B, G, C, NK, Dh)
        s = jnp.einsum('bcgrd,bgcnd->bcgrn', qrb, k_g) * scale
        p = masked_softmax(s, (tok <= t[None, :, None, None])[:, :, :, None, :])
        o_sel = jnp.einsum('bcgrn,bgcnd->bcgrd', p.astype(v_g.dtype), v_g)
        kb = lax.dynamic_slice_in_dim(kw_pad, t0, WINDOW + C, 1)
        vb = lax.dynamic_slice_in_dim(vw_pad, t0, WINDOW + C, 1)
        spos = t0 - WINDOW + jnp.arange(WINDOW + C)
        valid_w = (spos[None, :] <= t[:, None]) & (spos[None, :] > t[:, None] - WINDOW) & (spos[None, :] >= 0)
        s = jnp.einsum('bcgrd,bngd->bcgrn', qrb, kb) * scale
        p = masked_softmax(s, valid_w[None, :, None, None, :])
        o_win = jnp.einsum('bcgrn,bngd->bcgrd', p.astype(vb.dtype), vb)
        out = gb[..., 0:1] * o_cmp + gb[..., 1:2] * o_sel + gb[..., 2:3] * o_win
        return out.reshape(B, C, H * Dh)

    out = lax.map(one_block, jnp.arange(S // C))
    return out.transpose(1, 0, 2, 3).reshape(B, S, H * Dh)

def diff_attention(q, k, v, lam_vec, norm_g, lambda_init, pos):
    B, S, _, Dh = q.shape
    Hd = v.shape[2]
    QB = DIFF_Q_BLOCK
    scale = Dh ** -0.5
    q = rope_partial(q, pos).reshape(B, S, Hd, 2, Dh)
    k = rope_partial(k, pos).reshape(B, S, Hd, 2, Dh)
    lam32 = lam_vec.astype(jnp.float32)
    lam = jnp.exp(jnp.sum(lam32[0] * lam32[1])) - jnp.exp(jnp.sum(lam32[2] * lam32[3])) + lambda_init
    kpos = jnp.arange(S)

    def one_block(i):
        t0 = i * QB
        qb = lax.dynamic_slice_in_dim(q, t0, QB, 1)
        s = jnp.einsum('bqhmd,bkhmd->bhmqk', qb, k) * scale
        mask = kpos[None, :] <= (t0 + jnp.arange(QB))[:, None]
        p = masked_softmax(s, mask[None, None, None])
        a = p[:, :, 0] - lam * p[:, :, 1]
        return jnp.einsum('bhqk,bkhe->bqhe', a.astype(v.dtype), v)

    o = lax.map(one_block, jnp.arange(S // QB))
    o = o.transpose(1, 0, 2, 3, 4).reshape(B, S, Hd, 2 * Dh).astype(jnp.float32)
    o = o * lax.rsqrt(jnp.mean(jnp.square(o), -1, keepdims=True) + EPS) * norm_g * (1.0 - lambda_init)
    return o.reshape(B, S, Hd * 2 * Dh).astype(v.dtype)

def token_mixer(u, w_in, pe_k, w1_k, w2_k, pe_v, w1_v, w2_v, lam_vec, norm_g,
                w_bn, w_bd, w_o, lambda_init):
    B, S, _ = u.shape
    offs = np.cumsum(IN_SIZES)[:-1].tolist()
    (q_n, kc, vc, ksl, vsl, kwn, vwn, g_n, q_d, k_d, v_d, g_m) = jnp.split(u @ w_in, offs, axis=-1)
    pos = jnp.arange(S, dtype=jnp.float32)
    kvh = lambda t: t.reshape(B, S, NSA_KV_HEADS, HEAD_DIM)
    y_nsa = nsa_attention(q_n.reshape(B, S, NSA_HEADS, HEAD_DIM), kvh(kc), kvh(vc), kvh(ksl), kvh(vsl),
                          kvh(kwn), kvh(vwn), jax.nn.sigmoid(g_n).reshape(B, S, NSA_HEADS, 3),
                          pe_k, w1_k, w2_k, pe_v, w1_v, w2_v, pos) @ w_bn
    y_diff = diff_attention(q_d.reshape(B, S, 2 * DIFF_HEADS, HEAD_DIM),
                            k_d.reshape(B, S, 2 * DIFF_HEADS, HEAD_DIM),
                            v_d.reshape(B, S, DIFF_HEADS, 2 * HEAD_DIM),
                            lam_vec, norm_g, lambda_init, pos) @ w_bd
    g_a, g_b = jnp.split(jax.nn.sigmoid(g_m), 2, axis=-1)
    return (g_a * y_nsa + g_b * y_diff) @ w_o

def swiglu(u, w_in, w_out):
    a, b = jnp.split(u @ w_in, 2, axis=-1)
    return (jax.nn.silu(a) * b) @ w_out

def setup_inputs(seed: int = 0) -> dict:
    key = jax.random.key(seed)
    ks = jax.random.split(key, 24)
    nrm = lambda k, shape, s: jax.random.normal(k, shape, jnp.float32) * s
    L = DEPTH
    return {
        "x": nrm(ks[0], (BATCH, SEQ, D_MODEL), 1.0),
        "c": nrm(ks[1], (BATCH, D_MODEL), 1.0),
        "w_ada": nrm(ks[2], (L, D_MODEL, 6 * D_MODEL), 0.1 * D_MODEL ** -0.5),
        "b_ada": nrm(ks[3], (L, 6 * D_MODEL), 0.01),
        "w_in": nrm(ks[4], (L, D_MODEL, IN_COLS), D_MODEL ** -0.5),
        "cmp_pe_k": nrm(ks[5], (L, CMP_BLOCK, HEAD_DIM), 0.1),
        "cmp_w1_k": nrm(ks[6], (L, CMP_BLOCK * HEAD_DIM, CMP_HIDDEN), (CMP_BLOCK * HEAD_DIM) ** -0.5),
        "cmp_w2_k": nrm(ks[7], (L, CMP_HIDDEN, HEAD_DIM), CMP_HIDDEN ** -0.5),
        "cmp_pe_v": nrm(ks[8], (L, CMP_BLOCK, HEAD_DIM), 0.1),
        "cmp_w1_v": nrm(ks[9], (L, CMP_BLOCK * HEAD_DIM, CMP_HIDDEN), (CMP_BLOCK * HEAD_DIM) ** -0.5),
        "cmp_w2_v": nrm(ks[10], (L, CMP_HIDDEN, HEAD_DIM), CMP_HIDDEN ** -0.5),
        "diff_lambda": nrm(ks[11], (L, 4, HEAD_DIM), 0.1),
        "diff_norm_g": 1.0 + nrm(ks[12], (L, 2 * HEAD_DIM), 0.02),
        "w_branch_nsa": nrm(ks[13], (L, NSA_WIDTH, D_MODEL), BETA * NSA_WIDTH ** -0.5),
        "w_branch_diff": nrm(ks[14], (L, DIFF_V_WIDTH, D_MODEL), BETA * DIFF_V_WIDTH ** -0.5),
        "w_out": nrm(ks[15], (L, D_MODEL, D_MODEL), BETA * D_MODEL ** -0.5),
        "ln1_g": 1.0 + nrm(ks[16], (L, D_MODEL), 0.02),
        "ln1_b": nrm(ks[17], (L, D_MODEL), 0.01),
        "w_ffn_in": nrm(ks[18], (L, D_MODEL, 2 * D_FF), D_MODEL ** -0.5),
        "w_ffn_out": nrm(ks[19], (L, D_FF, D_MODEL), BETA * D_FF ** -0.5),
        "ln2_g": 1.0 + nrm(ks[20], (L, D_MODEL), 0.02),
        "ln2_b": nrm(ks[21], (L, D_MODEL), 0.01),
    }

def reference(x, c, w_ada, b_ada, w_in, cmp_pe_k, cmp_w1_k, cmp_w2_k, cmp_pe_v, cmp_w1_v, cmp_w2_v,
              diff_lambda, diff_norm_g, w_branch_nsa, w_branch_diff, w_out, ln1_g, ln1_b,
              w_ffn_in, w_ffn_out, ln2_g, ln2_b):
    for l in range(DEPTH):
        lambda_init = 0.8 - 0.6 * math.exp(-0.3 * l)
        ada = jax.nn.silu(c) @ w_ada[l] + b_ada[l]
        sh1, sc1, g1, sh2, sc2, g2 = jnp.split(ada[:, None, :], 6, axis=-1)
        u = x * (1.0 + sc1) + sh1
        mix = token_mixer(u, w_in[l], cmp_pe_k[l], cmp_w1_k[l], cmp_w2_k[l], cmp_pe_v[l], cmp_w1_v[l],
                          cmp_w2_v[l], diff_lambda[l], diff_norm_g[l], w_branch_nsa[l], w_branch_diff[l],
                          w_out[l], lambda_init)
        x = layer_norm(ALPHA * x + (1.0 + g1) * mix, ln1_g[l], ln1_b[l])
        u = x * (1.0 + sc2) + sh2
        x = layer_norm(ALPHA * x + (1.0 + g2) * swiglu(u, w_ffn_in[l], w_ffn_out[l]), ln2_g[l], ln2_b[l])
    return x


_drawn_inputs = setup_inputs


def setup_inputs(seed=0):
    import zlib

    import numpy as np

    out = dict(_drawn_inputs(seed))
    spreads = {}
    factors = {'b_ada': 5.884,
     'cmp_pe_k': 8.0,
     'cmp_w1_k': 8.0,
     'cmp_w2_k': 7.938,
     'cmp_pe_v': 8.0,
     'cmp_w1_v': 3.2,
     'diff_lambda': 4.672,
     'diff_norm_g': 28.269,
     'ln1_b': 3.658,
     'ln2_b': 3.727}
    for name, (base, spread) in spreads.items():
        noise = np.random.default_rng([zlib.crc32(name.encode()), seed]).standard_normal(out[name].shape)
        drawn = base * np.exp(spread * noise) if base else spread * noise
        out[name] = __import__('jax').numpy.asarray(drawn.astype(out[name].dtype))
    for name, factor in factors.items():
        out[name] = (out[name] * factor).astype(out[name].dtype)
    return out
```

```python
import math
from contextlib import ExitStack

import numpy as np

import concourse.bass as bass
from concourse import mybir

D_MODEL, SEQ, DEPTH = 1024, 512, 2
HEAD_DIM, NSA_HEADS, DIFF_HEADS = 64, 8, 4
NSA_WIDTH, NSA_KV_WIDTH = 512, 128
CMP_BLOCK, CMP_STRIDE, CMP_HIDDEN = 32, 16, 256
D_FF = -(-8 * D_MODEL // (3 * 256)) * 256
ROPE_THETA, ROPE_FRACTION = 500000.0, 4
ALPHA = (2 * DEPTH) ** 0.25
EPS = 1e-5
NEG_INF = -1e30
IN_SIZES = dict(q_n=512, kc=128, vc=128, ksl=128, vsl=128, kwn=128, vwn=128, g_n=24,
                q_d=512, k_d=512, v_d=512, g_m=2048)
IN_AT = dict(zip(IN_SIZES, np.cumsum([0] + list(IN_SIZES.values()))[:-1].tolist()))
LAMBDA_INIT = [0.8 - 0.6 * math.exp(-0.3 * l) for l in range(DEPTH)]

P = 128
TT = SEQ // P
KD = D_MODEL // P
KF = D_FF // P
NC = (SEQ - CMP_BLOCK) // CMP_STRIDE + 1
NCP = 32
KJ = CMP_BLOCK * HEAD_DIM // P

V_ADA, V_LN1G, V_LN1B, V_LN2G, V_LN2B, V_NORM, V_PEK, V_PEV, V_C = 0, 48, 56, 64, 72, 80, 81, 97, 113
V_ROWS = 121

C_COS, C_SIN, C_ID, C_CAUSAL, C_CMP, C_ANY, C_LAM = 0, 512, 1024, 1152, 1280, 1792, 1796
C_COLS = C_LAM + 2 * DEPTH

CHUNKS = (["kc", "vc", "ksl", "kwn"] + [f"vg{i}" for i in range(TT)] + [f"qn{i}" for i in range(4)]
          + ["hk", "hv", "kv2"] + [f"kd{i}" for i in range(4)] + [f"qd{i}" for i in range(4)]
          + [f"vd{i}" for i in range(TT)] + [f"gm{i}" for i in range(16)]
          + [f"y{a}{i}" for i in range(KD) for a in "nd"] + [f"wo{i}" for i in range(KD)]
          + [f"f{a}{i}" for i in range(KF) for a in "ab"] + [f"fo{i}" for i in range(KD)])
CHUNK_AT = {name: i for i, name in enumerate(CHUNKS)}


def chunk(l, name):
    return l * len(CHUNKS) + CHUNK_AT[name]


JOBS = ([("kv", "vc", 1), ("kk", "kwn", 2), ("vg", "vg3", 2), ("qn0", "qn1", 1), ("qn1", "qn3", 1),
         ("w1k0", "hk", 1), ("w1k1", "hk", 1), ("w1v0", "hv", 1), ("w1v1", "hv", 1)]
        + [(f"{a}{i}", f"{a}{2 * i + 1}", 1) for a in ("kd", "qd") for i in range(2)]
        + [("vd0", "vd3", 1), ("vd1", "vd3", 1)]
        + [(f"gm{i}", f"gm{2 * i + 1}", 1) for i in range(8)]
        + [(f"br{i}", f"yd{2 * i + 1}", 2) for i in range(4)]
        + [(f"wo{i}", f"wo{2 * i + 1}", 1) for i in range(4)]
        + [(f"ff{i}", f"fb{i}", 2) for i in range(KF)]
        + [(f"fo{i}", f"fo{i // 2}", 1) for i in range(2 * KD)])
JOB_AT = {j[0]: i for i, j in enumerate(JOBS)}
NS = 4
SLOT = 8 * 280


def ready_counts():
    total, out = [0] * NS, []
    for l in range(DEPTH):
        for i, (_, _, dmas) in enumerate(JOBS):
            s = (l * len(JOBS) + i) % NS
            total[s] += 16 * dmas
            out.append(total[s])
    return out


READY = ready_counts()

ADA1, ADA2 = 16, 32


def ada_job(l, m):
    return 48 * l + m


STEPS = 13
SEQUENCE = [(i, j) for i in range(TT) for j in range(STEPS + 1)]


def score_step(l, i, j):
    return (l * TT + i) * STEPS + j


def turn_step(l, i, j):
    return l * (TT * (STEPS + 1) + TT) + i * (STEPS + 1) + j


def turned_by_act(l, i, j):
    return (l * TT + i) * STEPS + j


def turned_by_dve(l, i, j):
    return l * (9 * TT + TT) + 9 * i + min(j + 1, 9)


def out_bank(l, i, j):
    return (l * TT + i) * 4 + (0 if j == 0 else (j - 1) // 4 + 1)


def build(nc, x, w_ada, b_ada, c, w_in, pe_k, w1_k, w2_k, pe_v, w1_v, w2_v, lam, norm_g,
          w_bn, w_bd, w_o, ln1_g, ln1_b, w_f1, w_f2, ln2_g, ln2_b, consts, out):
    fp32, bf16 = mybir.dt.float32, mybir.dt.bfloat16
    ALU, ACT, AX = mybir.AluOpType, mybir.ActivationFunctionType, mybir.AxisListType

    ctx = ExitStack()
    with ctx:
        def sb(name, shape, dt=fp32):
            return ctx.enter_context(nc.sbuf_tensor(name, shape, dt))

        def sem(name):
            return ctx.enter_context(nc.semaphore(name))

        ring = sb("ring", [P, NS, SLOT])
        ada_ring = sb("ada_ring", [P, 2, KD, P])
        res = sb("res", [P, KD, SEQ])
        uT = sb("uT", [P, KD, SEQ])
        region_a = sb("region_a", [P, 24 * SEQ])
        gm = region_a[:, 0:16 * SEQ].rearrange("p (m t) -> p m t", t=SEQ)
        q_raw = region_a[:, 16 * SEQ:20 * SEQ].rearrange("p (m t) -> p m t", t=SEQ)
        q_rot = region_a[:, 20 * SEQ:24 * SEQ].rearrange("p (m t) -> p m t", t=SEQ)
        hT = region_a[:, 0:KF * SEQ].rearrange("p (m t) -> p m t", t=SEQ)
        kc2 = region_a[:, 0:4 * SEQ].rearrange("p (w g t) -> p w g t", w=2, g=2)
        flat = region_a[:, 4 * SEQ:8 * SEQ].rearrange("p (w j n) -> p w j n", w=2, j=KJ)
        region_b = sb("region_b", [P, 8 * SEQ])
        probs = region_b[:, 0:4 * SEQ].rearrange("p (r h k) -> p r h k", r=2, h=2)
        probsT = region_b[:, 4 * SEQ:8 * SEQ].rearrange("p (r h k) -> p r h k", r=2, h=2)
        mergedT = region_b[:, :].rearrange("p (m t) -> p m t", t=SEQ)
        region_c = sb("region_c", [P, 8 * SEQ])
        x_tok = region_c[:, :].rearrange("p (i n) -> p i n", i=TT)
        qdT = region_c[:, 0:4 * SEQ].rearrange("p (m t) -> p m t", t=SEQ)
        kdT = region_c[:, 4 * SEQ:8 * SEQ].rearrange("p (m t) -> p m t", t=SEQ)
        yT = region_c[:, :].rearrange("p (m t) -> p m t", t=SEQ)
        k_dup = sb("k_dup", [P, 2, 2, SEQ])
        v_tok = sb("v_tok", [P, TT, 256])
        gates = sb("gates", [P, TT, NSA_HEADS, 3])
        vd_tok = sb("vd_tok", [P, TT, 512])
        raw = sb("raw", [P, 2, SEQ])
        t1 = sb("t1", [P, SEQ])
        t2 = sb("t2", [P, SEQ])
        o_nsa = sb("o_nsa", [P, SEQ])
        hid = sb("hid", [P, 2, 2, 2 * NCP])
        hid_rep = sb("hid_rep", [P, 2, 2, 4, NCP])
        k_cmpT = sb("k_cmpT", [P, 2 * NCP])
        v_cmp = sb("v_cmp", [P, 2, 256])
        neg_max = sb("neg_max", [P, 2, 8])
        sums = sb("sums", [P, 2, 32])
        coef = sb("coef", [P, 2, 8])
        d_rs = sb("d_rs", [P, 2, 4])
        d_mix = sb("d_mix", [P, 2])
        d_sq = sb("d_sq", [P, TT * 4])
        sil = raw[:, :, :]
        cst = sb("cst", [P, C_COLS])
        cos, sin, ident = cst[:, C_COS:C_COS + SEQ], cst[:, C_SIN:C_SIN + SEQ], cst[:, C_ID:C_ID + P]
        ident_b = sb("ident_b", [P, P], bf16)
        mask_b = sb("mask_b", [P, P + TT * P], bf16)
        ones = sb("ones", [P, P])
        eps = sb("eps", [P, 1])
        vec_rows = region_b[0:V_ROWS, 0:DEPTH * P].rearrange("p (l n) -> p l n", l=DEPTH)
        vec = sb("vec", [P, DEPTH, V_ROWS])
        lam_in = region_b[:, SEQ:SEQ + DEPTH * 4 * HEAD_DIM].rearrange("p (l a d) -> p l a d", l=DEPTH, a=4)
        lam_s = sb("lam_s", [P, DEPTH, 2])
        neg_lam = sb("neg_lam", [P, DEPTH])
        norm_s = sb("norm_s", [P, DEPTH])
        w2k = sb("w2k", [P, DEPTH, 2, 2, HEAD_DIM])
        w2v = sb("w2v", [P, DEPTH, 2, HEAD_DIM])
        c_silu = sb("c_silu", [P, KD])
        ada_acc = sb("ada_acc", [P, 4, P])
        ada = sb("ada", [P, DEPTH, 48])
        gate1 = sb("gate1", [P, 2, KD])
        mul_u = sb("mul_u", [P, 2, KD])
        add_u = sb("add_u", [P, 2, KD])
        mul_r = sb("mul_r", [P, 2, KD])
        add_r = sb("add_r", [P, 2, KD])

        banks = ctx.enter_context(nc.psum_tensor("banks", [P, 8, SEQ], fp32))
        proj = banks[:, 0:2, :]
        scores = banks[:, 2:4, :]
        turned = banks[:, 4:6, :]
        outs = banks[:, 6:8, :]
        ada_ps = outs[:, 0, 0:48]
        mean_ps, var_ps = scores[:, 0, :], scores[:, 1, :]

        const_in = sem("const_in")
        x_in = sem("x_in")
        vec_in = sem("vec_in")
        slot_ready = [sem(f"slot_ready{s}") for s in range(NS)]
        ada_ready = [sem(f"ada_ready{s}") for s in range(2)]
        ada_summed = sem("ada_summed")
        ada_reduced = sem("ada_reduced")
        setup_done = sem("setup_done")
        vec_turned = sem("vec_turned")
        vec_saved = sem("vec_saved")
        c_ready = sem("c_ready")
        lam_summed = sem("lam_summed")
        lam_exp = sem("lam_exp")
        x_turned = sem("x_turned")
        x_saved = sem("x_saved")
        part1 = sem("part1")
        part2 = sem("part2")
        chunk_done = [sem(f"chunk_done{b}") for b in range(2)]
        chunk_saved = [sem(f"chunk_saved{b}") for b in range(2)]
        flat_ready = sem("flat_ready")
        rep_ready = sem("rep_ready")
        rope_done = sem("rope_done")
        scored = sem("scored")
        max_done = sem("max_done")
        exp_done = sem("exp_done")
        mix_done = sem("mix_done")
        turn_done = sem("turn_done")
        turn_act = sem("turn_act")
        turn_dve = sem("turn_dve")
        pv_done = sem("pv_done")
        out_done = sem("out_done")
        out_saved = sem("out_saved")
        nsa_ready = sem("nsa_ready")
        dsq_ready = sem("dsq_ready")
        dstd_ready = sem("dstd_ready")
        dnorm_ready = sem("dnorm_ready")
        sig_ready = sem("sig_ready")
        merged = sem("merged")
        mean_done = sem("mean_done")
        centred = sem("centred")
        squared = sem("squared")
        var_done = sem("var_done")
        std_ready = sem("std_ready")
        normed = sem("normed")
        u_ready = sem("u_ready")
        res_ready = sem("res_ready")
        out_turned = sem("out_turned")
        out_dve = sem("out_dve")
        out_act = sem("out_act")
        stored = sem("stored")
        dve_chain = sem("dve_chain")
        act_chain = sem("act_chain")

        block = ctx.enter_context(nc.Block())

        def wait_done(eng, l, name):
            n = chunk(l, name)
            eng.wait_ge(chunk_done[n % 2], n // 2 + 1)

        def wait_saved(eng, l, name):
            n = chunk(l, name)
            eng.wait_ge(chunk_saved[n % 2], n // 2 + 1)

        def bank_of(l, name):
            return proj[:, chunk(l, name) % 2, :]

        def saved(l, name):
            return chunk_saved[chunk(l, name) % 2]

        def cols(w, lo, hi):
            return w[:, lo:hi].rearrange("(k p) n -> p k n", p=P)

        @block.sync
        def _(sp):
            sp.dma_start(cst[:, :], consts).then_inc(const_in, 16)
            sp.dma_start(x_tok, x[0].rearrange("(i p) n -> p i n", p=P)).then_inc(x_in, 16)
            sp.wait_ge(ada_ready[1], 16 * 4)
            for l in range(DEPTH):
                for i, (name, _, _) in enumerate(JOBS):
                    g = l * len(JOBS) + i
                    s = g % NS
                    if g >= NS:
                        wait_done(sp, (g - NS) // len(JOBS), JOBS[(g - NS) % len(JOBS)][1])
                    slot = ring[:, s, :]

                    def put(at, width, src):
                        k = src.shape[1]
                        dst = slot[:, 0:k * width].rearrange("p (k n) -> p k n", n=width)
                        sp.dma_start(dst[:, :, at:at + src.shape[2]], src).then_inc(slot_ready[s], 16)

                    def w(at, n):
                        return cols(w_in[l], at, at + n)

                    kind, n = name.rstrip("0123456789"), int(name[-1]) if name[-1].isdigit() else 0
                    if kind == "kv":
                        put(0, 256, w(IN_AT["kc"], 256))
                    elif kind == "kk":
                        put(0, 256, w(IN_AT["ksl"], 128))
                        put(128, 256, w(IN_AT["kwn"], 128))
                    elif kind == "vg":
                        put(0, 280, w(IN_AT["vsl"], 128))
                        put(128, 280, w(IN_AT["vwn"], 152))
                    elif kind in ("qn", "kd", "qd", "vd", "gm"):
                        put(0, 256, w(IN_AT[kind[0] + "_" + kind[1]] + 256 * n, 256))
                    elif name[:2] == "w1":
                        w1 = w1_k if name[2] == "k" else w1_v
                        put(0, 256, w1[l, 1024 * n:1024 * (n + 1), :].rearrange("(k p) n -> p k n", p=P))
                    elif kind == "br":
                        for h, wb in enumerate((w_bn, w_bd)):
                            dst = slot[:, 1024 * h:1024 * (h + 1)].rearrange("p (k n) -> p k n", k=4)
                            sp.dma_start(dst, cols(wb[l], 256 * n, 256 * (n + 1))).then_inc(slot_ready[s], 16)
                    elif kind == "wo":
                        put(0, 256, cols(w_o[l], 256 * n, 256 * (n + 1)))
                    elif kind == "ff":
                        f = int(name[2:])
                        put(0, 256, cols(w_f1[l], P * f, P * (f + 1)))
                        put(128, 256, cols(w_f1[l], D_FF + P * f, D_FF + P * (f + 1)))
                    elif kind == "fo":
                        f, half = int(name[2:]) // 2, int(name[2:]) % 2
                        rows = w_f2[l, half * 11 * P:(half + 1) * 11 * P, :]
                        put(0, P, cols(rows, P * f, P * (f + 1)))
            for i in range(TT):
                sp.wait_ge(out_dve, i + 1)
                sp.wait_ge(out_act, i + 1)
                sp.dma_start(out[0, i * P:(i + 1) * P, :], x_tok[:, i, :]).then_inc(stored, 16)
            sp.wait_ge(stored, 16 * TT)

        @block.gpsimd
        def _(pool):
            def load_ada(l, m):
                n = ada_job(l, m)
                if n >= 2:
                    pool.wait_ge(ada_summed, n - 1)
                pool.dma_start(ada_ring[:, n % 2], cols(w_ada[l], P * m, P * (m + 1)))\
                    .then_inc(ada_ready[n % 2], 16)

            def residual(l, which):
                for m in range(KD):
                    pool.wait_ge(normed, (2 * l + which) * KD + m + 1)
                    if m == 0:
                        pool.wait_ge(part2 if which == 0 else part1, l + 1 + which)
                    nc.gpsimd.tensor_scalar(res[:, m, :], yT[:, m, :], mul_r[:, which, m:m + 1],
                                            add_r[:, which, m:m + 1], ALU.mult, ALU.add)\
                        .then_inc(res_ready, 1)

            for m in range(ADA1):
                load_ada(0, m)
            for l in range(DEPTH):
                for m in range(ADA1, 48):
                    load_ada(l, m)
                residual(l, 0)
                if l + 1 < DEPTH:
                    for m in range(ADA1):
                        load_ada(l + 1, m)
                    residual(l, 1)

        @block.scalar
        def _(act):
            count = [0]

            def link(ins):
                count[0] += 1
                ins.then_inc(act_chain, 1)
                act.wait_ge(act_chain, count[0])

            for l in range(DEPTH):
                for at, src in ((V_ADA, b_ada[l].rearrange("(m p) -> m p", p=P)),
                                (V_LN1G, ln1_g[l].rearrange("(m p) -> m p", p=P)),
                                (V_LN1B, ln1_b[l].rearrange("(m p) -> m p", p=P)),
                                (V_LN2G, ln2_g[l].rearrange("(m p) -> m p", p=P)),
                                (V_LN2B, ln2_b[l].rearrange("(m p) -> m p", p=P)),
                                (V_NORM, norm_g[l:l + 1, :]),
                                (V_PEK, pe_k[l].rearrange("(j c) d -> j (c d)", c=2)),
                                (V_PEV, pe_v[l].rearrange("(j c) d -> j (c d)", c=2)),
                                (V_C, c[0].rearrange("(m p) -> m p", p=P))):
                    act.dma_start(vec_rows[at:at + src.shape[0], l, :], src).then_inc(vec_in, 16)
                act.dma_start(lam_in[:, l], lam[l].partition_broadcast(P)).then_inc(vec_in, 16)
                for d in range(2):
                    act.dma_start(w2k[:, l, :, d, :], w2_k[l].rearrange("(m p) d -> p m d", p=P))\
                        .then_inc(vec_in, 16)
                act.dma_start(w2v[:, l], w2_v[l].rearrange("(m p) d -> p m d", p=P)).then_inc(vec_in, 16)
            act.wait_ge(vec_saved, DEPTH)
            nc.scalar.activation(c_silu[:, :], vec[:, 0, V_C:V_C + KD], ACT.Silu).then_inc(c_ready, 1)
            act.wait_ge(lam_summed, 1)
            nc.scalar.activation(lam_s[:, :, :], lam_s[:, :, :], ACT.Exp).then_inc(lam_exp, 1)
            act.wait_ge(part1, 1)
            for k in range(KD):
                act.wait_ge(x_saved, k + 1)
                nc.scalar.activation(uT[:, k, :], scores[:, k % 2, :], ACT.Identity,
                                     bias=ada[:, 0, k:k + 1], scale=mul_u[:, 0, k:k + 1]).then_inc(u_ready, 1)

            def save(l, name, dst, scale=1.0):
                wait_done(act, l, name)
                nc.scalar.activation(dst, bank_of(l, name), ACT.Copy, scale=scale)\
                    .then_inc(saved(l, name), 1)

            def save_raw(l, name, r, scale=1.0):
                if l * 14 + r >= 2:
                    act.wait_ge(rope_done, l * 14 + r - 1)
                save(l, name, raw[:, r % 2, :], scale)

            def layernorm(l, which):
                n = 2 * l + which
                for m in range(KD):
                    act.wait_ge(centred, n * KD + m + 1)
                    nc.scalar.activation(uT[:, m, :], yT[:, m, :], ACT.Square).then_inc(squared, 1)
                act.wait_ge(var_done, n + 1)
                nc.scalar.activation(t1[:, :], var_ps, ACT.Sqrt, bias=eps[:, :]).then_inc(std_ready, 1)
                last = l == DEPTH - 1 and which == 1
                for m in range(KD):
                    act.wait_ge(normed, n * KD + m + 1)
                    if m == 0:
                        act.wait_ge(part2 if which == 0 else part1, l + 1 + which)
                    w = 1 - which
                    nc.scalar.activation(uT[:, m, :], yT[:, m, :], ACT.Identity,
                                         bias=add_u[:, w, m:m + 1], scale=mul_u[:, w, m:m + 1])\
                        .then_inc(u_ready, 1)

            for l in range(DEPTH):
                wait_done(act, l, "kc")
                for g in range(2):
                    src = bank_of(l, "kc")[64 * g:64 * g + 64, :]
                    nc.scalar.activation(kc2[0:64, 0, g, :], src, ACT.Copy)
                    last = nc.scalar.activation(kc2[64:128, 0, g, 0:SEQ - 1], src[:, 1:SEQ], ACT.Copy)
                last.then_inc(saved(l, "kc"), 1)
                save_raw(l, "ksl", 0)
                save_raw(l, "kwn", 1)
                for i in range(TT):
                    wait_done(act, l, f"vg{i}")
                    bank = bank_of(l, f"vg{i}")
                    nc.scalar.activation(v_tok[:, i, :], bank[:, 0:256], ACT.Copy)
                    nc.scalar.activation(gates[:, i].rearrange("p h b -> p (h b)"), bank[:, 256:280],
                                         ACT.Sigmoid).then_inc(saved(l, f"vg{i}"), 1)
                for i in range(4):
                    save(l, f"qn{i}", q_raw[:, i, :], HEAD_DIM ** -0.5)
                for w, name in enumerate(("hk", "hv")):
                    wait_done(act, l, name)
                    dst = hid[:, w].rearrange("p m (g n) -> p m g n", g=2)[:, :, :, 0:NC]
                    src = bank_of(l, name)[:, 0:128].rearrange("p (m g n) -> p m g n", m=2, g=2)[:, :, :, 0:NC]
                    nc.scalar.activation(dst, src, ACT.Gelu_apprx_tanh).then_inc(saved(l, name), 1)
                for i in range(4):
                    save_raw(l, f"kd{i}", 6 + i)
                for i in range(4):
                    save_raw(l, f"qd{i}", 10 + i, HEAD_DIM ** -0.5)
                for i in range(TT):
                    save(l, f"vd{i}", vd_tok[:, i, :])

                for t in range(len(SEQUENCE) + 1):
                    if t >= 1:
                        i, j = SEQUENCE[t - 1]
                        N = (i + 1) * P
                        if j >= 1:
                            act.wait_ge(turn_done, turn_step(l, i, j) + 1)
                            s = score_step(l, i, j)
                            if j == STEPS:
                                nc.scalar.activation(
                                    q_rot[:, :, i * P:(i + 1) * P],
                                    turned[:, 0, :].rearrange("p (c t) -> p c t", c=4), ACT.Copy)\
                                    .then_inc(turn_act, 1)
                            else:
                                act.wait_ge(pv_done, s - 1)
                                nc.scalar.activation(probsT[:, s % 2, 0, 0:N], turned[:, 0, 0:N], ACT.Copy)\
                                    .then_inc(turn_act, 1)
                    if t == len(SEQUENCE):
                        break
                    i, j = SEQUENCE[t]
                    if j < STEPS:
                        s = score_step(l, i, j)
                        N = (i + 1) * P
                        act.wait_ge(max_done, s + 1)
                        if j == 0:
                            nc.scalar.activation(probs[:, s % 2, 0, 0:256], probs[:, s % 2, 0, 0:256],
                                                 ACT.Exp).then_inc(exp_done, 1)
                        else:
                            if s >= 2:
                                i2, j2 = (i, j - 2) if j >= 2 else (i - 1, j + STEPS - 2)
                                if i2 >= 0:
                                    act.wait_ge(turn_done, turn_step(l, i2, j2) + 1)
                            for h in range(2):
                                at = 8 + 2 * (j - 1) + h
                                last = nc.scalar.activation(
                                    probs[:, s % 2, h, 0:N], scores[:, h, 0:N], ACT.Exp,
                                    bias=neg_max[:, s % 2, h:h + 1],
                                    accum_out=sums[:, i % 2, at:at + 1])
                            last.then_inc(exp_done, 1)
                    if t % 4 == 3:
                        save(l, f"gm{t // 4}", gm[:, t // 4, :])
                save(l, "gm14", gm[:, 14, :])
                act.wait_ge(dsq_ready, l + 1)
                nc.scalar.activation(d_sq[:, :], d_sq[:, :], ACT.Sqrt, bias=eps[:, :],
                                     scale=1.0 / (2 * HEAD_DIM)).then_inc(dstd_ready, 1)
                save(l, "gm15", gm[:, 15, :])
                for m in range(KD):
                    for h in range(2):
                        g = gm[:, 8 * h + m, :]
                        if m == 0 and h == 0:
                            wait_saved(act, l, "gm15")
                            wait_saved(act, l, "gm14")
                        last = nc.scalar.activation(g, g, ACT.Sigmoid)
                    last.then_inc(sig_ready, 1)
                layernorm(l, 0)
                for f in range(KF):
                    if f >= 2:
                        wait_saved(act, l, f"fb{f - 2}")
                    wait_done(act, l, f"fa{f}")
                    nc.scalar.activation(sil[:, f % 2, :], bank_of(l, f"fa{f}"), ACT.Silu)\
                        .then_inc(saved(l, f"fa{f}"), 1)
                layernorm(l, 1)
            for i in range(TT):
                act.wait_ge(out_turned, i + 1)
                nc.scalar.activation(x_tok[:, i, 512:1024], scores[:, 1, :], ACT.Copy).then_inc(out_act, 1)

        @block.vector
        def _(dve):
            V = nc.vector
            count = [0]

            def link(ins):
                count[0] += 1
                ins.then_inc(dve_chain, 1)
                dve.wait_ge(dve_chain, count[0])

            V.memset(ones[:, :], 1.0 / D_MODEL)
            V.memset(eps[:, :], EPS)
            V.memset(hid[:, :, :, :], 0.0)
            V.memset(v_cmp[:, :, :], 0.0)
            dve.wait_ge(const_in, 16)
            V.tensor_copy(ident_b[:, :], ident)
            V.tensor_copy(mask_b[:, :], cst[:, C_CAUSAL:C_CAUSAL + P + TT * P]).then_inc(setup_done, 1)
            for l in range(DEPTH):
                dve.wait_ge(vec_turned, l + 1)
                link(V.tensor_copy(vec[:, l, :], turned[:, l, 0:V_ROWS]))
                V.tensor_scalar(norm_s[:, l:l + 1], vec[:, l, V_NORM:V_NORM + 1],
                                1.0 - LAMBDA_INIT[l], None, ALU.mult).then_inc(vec_saved, 1)
            lam_v = lam_in.rearrange("p l (a b) d -> p l a b d", b=2)
            for l in range(DEPTH):
                link(V.tensor_tensor(lam_v[:, l, :, 0, :], lam_v[:, l, :, 0, :], lam_v[:, l, :, 1, :], ALU.mult))
                link(V.tensor_reduce(lam_s[:, l, :], lam_v[:, l, :, 0, :], AX.X, ALU.add))
            V.memset(t1[:, 0:1], 0.0).then_inc(lam_summed, 1)
            dve.wait_ge(lam_exp, 1)
            link(V.tensor_tensor(neg_lam[:, :], lam_s[:, :, 1], lam_s[:, :, 0], ALU.subtract))
            link(V.tensor_tensor(neg_lam[:, :], neg_lam[:, :], cst[:, C_LAM:C_LAM + DEPTH], ALU.subtract))
            dve.wait_ge(c_ready, 1)

            def ada_step(l, m):
                n = ada_job(l, m)
                dve.wait_ge(ada_ready[n % 2], 16 * (n // 2 + 1))
                if n >= 4:
                    dve.wait_ge(ada_reduced, n - 3)
                acc, w = ada_acc[:, n % 4, :], ada_ring[:, n % 2]
                link(V.tensor_scalar(acc, w[:, 0, :], c_silu[:, 0:1], None, ALU.mult))
                for k in range(1, KD):
                    ins = V.scalar_tensor_tensor(acc, w[:, k, :], c_silu[:, k:k + 1], acc, ALU.mult, ALU.add)
                    if k < KD - 1:
                        link(ins)
                ins.then_inc(ada_summed, 1)

            def ada_part1(l):
                dve.wait_ge(ada_reduced, ada_job(l, ADA1))
                link(V.tensor_tensor(ada[:, l, 0:16], ada_ps[:, 0:16], vec[:, l, 0:16], ALU.add))
                if l == 0:
                    V.tensor_scalar(mul_u[:, 0, :], ada[:, l, 8:16], 1.0, None, ALU.add).then_inc(part1, 1)
                else:
                    link(V.tensor_scalar(ada[:, l, 8:16], ada[:, l, 8:16], 1.0, None, ALU.add))
                    fold(l - 1, V_LN2G, V_LN2B, ada[:, l, 8:16], ada[:, l, 0:8], 0, 1, part1)

            def ada_part2(l):
                dve.wait_ge(ada_reduced, ada_job(l, 48))
                link(V.tensor_tensor(ada[:, l, 16:48], ada_ps[:, 16:48], vec[:, l, 16:48], ALU.add))
                V.tensor_scalar(gate1[:, 0, :], ada[:, l, 16:24], 1.0, None, ALU.add)
                V.tensor_scalar(gate1[:, 1, :], ada[:, l, 40:48], 1.0, None, ALU.add)
                link(V.tensor_scalar(ada[:, l, 32:40], ada[:, l, 32:40], 1.0, None, ALU.add))
                fold(l, V_LN1G, V_LN1B, ada[:, l, 32:40], ada[:, l, 24:32], 1, 0, part2)

            def fold(l, at_g, at_b, scale1, shift, to_u, to_r, signal):
                g, b = vec[:, l, at_g:at_g + KD], vec[:, l, at_b:at_b + KD]
                V.tensor_tensor(mul_u[:, to_u, :], g, scale1, ALU.mult)
                link(V.tensor_tensor(add_u[:, to_u, :], b, scale1, ALU.mult))
                V.tensor_tensor(add_u[:, to_u, :], add_u[:, to_u, :], shift, ALU.add)
                V.tensor_scalar(mul_r[:, to_r, :], g, ALPHA, None, ALU.mult)
                link(V.tensor_scalar(add_r[:, to_r, :], b, ALPHA, None, ALU.mult))
                V.memset(d_mix[:, 0:1], 0.0).then_inc(signal, 1)

            def rope(l, r, src, outs_of):
                shuffle = [i + 8 if i < 8 else i - 8 if i < 16 else i for i in range(32)]
                V.tensor_tensor(t1[:, :], src, cos, ALU.mult)
                link(V.stream_shuffle(t2[:, :], src, shuffle))
                link(V.tensor_tensor(t2[:, :], t2[:, :], sin, ALU.mult))
                for dst, rows in outs_of:
                    last = V.tensor_tensor(dst, t1[rows, :], t2[rows, :], ALU.add)
                link(last)
                V.memset(d_mix[:, 1:2], 0.0).then_inc(rope_done, 1)

            def layernorm(l, which):
                n = 2 * l + which
                names = [f"wo{m}" if which == 0 else f"fo{m}" for m in range(KD)]
                for m in range(KD):
                    wait_done(dve, l, names[m])
                    if n >= 1 and m == 0:
                        dve.wait_ge(res_ready, n * KD)
                    V.scalar_tensor_tensor(yT[:, m, :], bank_of(l, names[m]), gate1[:, which, m:m + 1],
                                           res[:, m, :], ALU.mult, ALU.add).then_inc(saved(l, names[m]), 1)
                dve.wait_ge(mean_done, n + 1)
                wait_saved(dve, l, names[6])
                wait_saved(dve, l, names[7])
                for m in range(KD):
                    V.tensor_tensor(yT[:, m, :], yT[:, m, :], mean_ps, ALU.subtract).then_inc(centred, 1)
                dve.wait_ge(std_ready, n + 1)
                link(V.reciprocal(t2[:, :], t1[:, :]))
                for m in range(KD):
                    V.tensor_tensor(yT[:, m, :], yT[:, m, :], t2[:, :], ALU.mult).then_inc(normed, 1)

            for m in range(ADA1):
                ada_step(0, m)
            ada_part1(0)
            for k in range(KD):
                dve.wait_ge(x_turned, k + 1)
                V.tensor_scalar(res[:, k, :], scores[:, k % 2, :], ALPHA, None, ALU.mult).then_inc(x_saved, 1)

            for l in range(DEPTH):
                ada_at = [ADA1]

                def ada_two():
                    for _ in range(2):
                        ada_step(l, ada_at[0])
                        ada_at[0] += 1

                def build_flat(w):
                    at = (V_PEK, V_PEV)[w]
                    for g in range(2):
                        for hi in range(2):
                            src = kc2[:, w, g, 16 * hi:16 * hi + 16 * NC]\
                                .rearrange("p (n j) -> p j n", j=16)[:, 0:16:2, :]
                            pe = vec[:, l, at + 8 * hi:at + 8 * hi + 8].unsqueeze(2).to_broadcast([P, 8, NC])
                            last = V.tensor_tensor(flat[:, w, 8 * hi:8 * hi + 8, NCP * g:NCP * g + NC],
                                                   src, pe, ALU.add)
                    last.then_inc(flat_ready, 1)

                ada_two()
                wait_saved(dve, l, "kc")
                build_flat(0)
                ada_two()
                wait_done(dve, l, "vc")
                for g in range(2):
                    src = bank_of(l, "vc")[64 * g:64 * g + 64, :]
                    V.tensor_copy(kc2[0:64, 1, g, :], src)
                    last = V.tensor_copy(kc2[64:128, 1, g, 0:SEQ - 1], src[:, 1:SEQ])
                last.then_inc(saved(l, "vc"), 1)
                wait_saved(dve, l, "vc")
                build_flat(1)
                for r, name in enumerate(("ksl", "kwn")):
                    ada_two()
                    wait_saved(dve, l, name)
                    rope(l, r, raw[:, r % 2, :],
                         [(k_dup[64 * h:64 * h + 64, r, g, :], slice(64 * g, 64 * g + 64))
                          for g in range(2) for h in range(2)])
                for i in range(TT):
                    ada_two()
                for i in range(4):
                    ada_two()
                    wait_saved(dve, l, f"qn{i}")
                    rope(l, 2 + i, q_raw[:, i, :], [(q_rot[:, i, :], slice(0, P))])
                wait_saved(dve, l, "hv")
                V.tensor_copy(
                    hid_rep[:, :, :, :, :].rearrange("p m g r n -> p (m g) r n"),
                    hid[:, 1].rearrange("p m (g n) -> p (m g) n", g=2).unsqueeze(2)
                    .to_broadcast([P, 4, 4, NCP])).then_inc(rep_ready, 1)
                wait_done(dve, l, "kv2")
                V.tensor_copy(k_cmpT[:, :], bank_of(l, "kv2")[:, 0:2 * NCP])
                for g in range(2):
                    for r in range(4):
                        last = V.tensor_copy(
                            v_cmp[32 * r:32 * r + 32, g, 64 * r:64 * r + 64],
                            bank_of(l, "kv2")[32 * r:32 * r + 32, 64 + 64 * g:128 + 64 * g])
                last.then_inc(saved(l, "kv2"), 1)
                for i in range(4):
                    ada_two()
                if l:
                    dve.wait_ge(res_ready, 2 * l * KD)
                for i in range(4):
                    wait_saved(dve, l, f"kd{i}")
                    rope(l, 6 + i, raw[:, i % 2, :], [(kdT[:, i, :], slice(0, P))])
                for i in range(4):
                    wait_saved(dve, l, f"qd{i}")
                    rope(l, 10 + i, raw[:, i % 2, :], [(qdT[:, i, :], slice(0, P))])
                ada_part2(l)

                for t in range(len(SEQUENCE) + 2):
                    if 1 <= t <= len(SEQUENCE):
                        i, j = SEQUENCE[t - 1]
                        s = score_step(l, i, j)
                        N = (i + 1) * P
                        if j == 0:
                            dve.wait_ge(exp_done, s + 1)
                            V.tensor_reduce(sums[:, i % 2, 0:8],
                                            probs[:, s % 2, 0, 0:256].rearrange("p (h n) -> p h n", n=NCP),
                                            AX.X, ALU.add)
                        elif 9 <= j < STEPS:
                            dve.wait_ge(exp_done, s + 1)
                            hd = j - 9
                            d_sum = sums[:, i % 2, 24 + 2 * hd:26 + 2 * hd]
                            link(V.reciprocal(d_mix[:, 0:1], d_sum[:, 1:2]))
                            link(V.scalar_tensor_tensor(d_mix[:, 0:1], d_mix[:, 0:1], d_sum[:, 0:1],
                                                        neg_lam[:, l:l + 1], ALU.mult, ALU.mult))
                            V.scalar_tensor_tensor(probs[:, s % 2, 0, 0:N], probs[:, s % 2, 1, 0:N],
                                                   d_mix[:, 0:1], probs[:, s % 2, 0, 0:N],
                                                   ALU.mult, ALU.add).then_inc(mix_done, 1)
                    if t < len(SEQUENCE):
                        i, j = SEQUENCE[t]
                        s = score_step(l, i, j)
                        N = (i + 1) * P
                        if j < STEPS:
                            dve.wait_ge(scored, s + 1)
                        if j == 0:
                            if i >= 1:
                                dve.wait_ge(turn_done, turn_step(l, i - 1, STEPS - 2) + 1)
                            src = scores[:, 0:2, 0:4 * NCP].rearrange("p h (c n) -> p h c n", c=4)
                            link(V.tensor_reduce(neg_max[:, s % 2, 0:8].rearrange("p (h c) -> p h c", h=2),
                                                 src, AX.X, ALU.max))
                            for h in range(2):
                                dst = probs[:, s % 2, 0, 0:256]\
                                    .rearrange("p (c h n) -> p h c n", c=4, h=2)[:, h]
                                last = V.tensor_tensor(
                                    dst, src[:, h],
                                    neg_max[:, s % 2, 4 * h:4 * h + 4].unsqueeze(2).to_broadcast([P, 4, NCP]),
                                    ALU.subtract)
                            last.then_inc(max_done, 1)
                        elif j < STEPS:
                            V.tensor_reduce(neg_max[:, s % 2, 0:2], scores[:, 0:2, 0:N], AX.X, ALU.max,
                                            negate=True).then_inc(max_done, 1)
                    if 1 <= t <= len(SEQUENCE):
                        i, j = SEQUENCE[t - 1]
                        s = score_step(l, i, j)
                        N = (i + 1) * P
                        if j <= 8:
                            dve.wait_ge(turn_done, turn_step(l, i, j) + 1)
                            if s >= 2:
                                dve.wait_ge(pv_done, s - 1)
                            h, n = (0, 256) if j == 0 else (1, N)
                            V.tensor_copy(probsT[:, s % 2, h, 0:n], turned[:, h, 0:n]).then_inc(turn_dve, 1)
                    if t >= 2:
                        i, j = SEQUENCE[t - 2]
                        if j in (0, 4, 8, 12):
                            b = j // 4
                            q = out_bank(l, i, j)
                            bank = outs[:, q % 2, :]
                            dve.wait_ge(out_done, q + 1)
                            if b < 3:
                                link(V.reciprocal(coef[:, 0, :], sums[:, i % 2, 8 * b:8 * b + 8]))
                                if b == 0:
                                    wait_saved(dve, l, f"vg{i}")
                                if b == 0 and i == 0:
                                    link(V.tensor_scalar(coef[:, 0, :], coef[:, 0, :], cst[:, C_ANY:C_ANY + 1],
                                                         None, ALU.mult))
                                link(V.tensor_tensor(coef[:, 0, :], coef[:, 0, :], gates[:, i, :, b], ALU.mult))
                                dst = o_nsa if b == 0 else t1
                                if b == 0 and i >= 1:
                                    dve.wait_ge(turn_done, turn_step(l, i - 1, STEPS) + 1)
                                link(V.tensor_tensor(
                                    dst[:, :].rearrange("p (h d) -> p h d", d=HEAD_DIM),
                                    bank.rearrange("p (h d) -> p h d", d=HEAD_DIM),
                                    coef[:, 0, :].unsqueeze(2).to_broadcast([P, 8, HEAD_DIM]), ALU.mult))
                                V.memset(d_mix[:, 1:2], 0.0).then_inc(out_saved, 1)
                                if b:
                                    ins = V.tensor_tensor(o_nsa[:, :], o_nsa[:, :], t1[:, :], ALU.add)
                                    if b == 2:
                                        ins.then_inc(nsa_ready, 1)
                                    else:
                                        link(ins)
                            else:
                                d_sum = sums[:, i % 2, 24:32].rearrange("p (h m) -> p h m", m=2)
                                link(V.reciprocal(d_rs[:, 0, :], d_sum[:, :, 0]))
                                od = q_raw[:, :, i * P:(i + 1) * P]
                                link(V.tensor_tensor(od, bank.rearrange("p (h e) -> p h e", h=4),
                                                     d_rs[:, 0, :].unsqueeze(2).to_broadcast([P, 4, P]),
                                                     ALU.mult))
                                V.memset(d_mix[:, 1:2], 0.0).then_inc(out_saved, 1)
                                sq = t2[:, :].rearrange("p (h e) -> p h e", h=4)
                                link(V.tensor_tensor(sq, od, od, ALU.mult))
                                ins = V.tensor_reduce(d_sq[:, 4 * i:4 * i + 4], sq, AX.X, ALU.add)
                                if i == TT - 1:
                                    ins.then_inc(dsq_ready, 1)
                                else:
                                    link(ins)

                dve.wait_ge(dstd_ready, l + 1)
                link(V.reciprocal(d_sq[:, :], d_sq[:, :]))
                for i in range(TT):
                    od = q_raw[:, :, i * P:(i + 1) * P]
                    V.tensor_tensor(od, od, d_sq[:, 4 * i:4 * i + 4].unsqueeze(2).to_broadcast([P, 4, P]),
                                    ALU.mult).then_inc(dnorm_ready, 1)
                for i in range(TT):
                    dve.wait_ge(turn_done, turn_step(l, TT, i) + 1)
                    V.tensor_scalar(q_raw[:, :, i * P:(i + 1) * P],
                                    turned[:, i % 2, :].rearrange("p (h t) -> p h t", h=4),
                                    norm_s[:, l:l + 1], None, ALU.mult).then_inc(turn_dve, 1)
                for m in range(KD):
                    dve.wait_ge(sig_ready, l * KD + m + 1)
                    wait_done(dve, l, f"yn{m}")
                    V.tensor_tensor(t1[:, :], bank_of(l, f"yn{m}"), gm[:, m, :], ALU.mult)\
                        .then_inc(saved(l, f"yn{m}"), 1)
                    wait_done(dve, l, f"yd{m}")
                    V.tensor_tensor(t2[:, :], bank_of(l, f"yd{m}"), gm[:, 8 + m, :], ALU.mult)\
                        .then_inc(saved(l, f"yd{m}"), 1)
                    wait_saved(dve, l, f"yn{m}")
                    wait_saved(dve, l, f"yd{m}")
                    ins = V.tensor_tensor(mergedT[:, m, :], t1[:, :], t2[:, :], ALU.add)
                    ins.then_inc(merged, 1)
                    dve.wait_ge(merged, l * KD + m + 1)
                layernorm(l, 0)
                for f in range(KF):
                    wait_done(dve, l, f"fb{f}")
                    wait_saved(dve, l, f"fa{f}")
                    V.tensor_tensor(hT[:, f, :], bank_of(l, f"fb{f}"), sil[:, f % 2, :], ALU.mult)\
                        .then_inc(saved(l, f"fb{f}"), 1)
                    if l + 1 < DEPTH and f < ADA1:
                        ada_step(l + 1, f)
                if l + 1 < DEPTH:
                    ada_part1(l + 1)
                else:
                    V.tensor_copy(mul_u[:, 0, :], vec[:, l, V_LN2G:V_LN2G + KD])
                    link(V.tensor_copy(add_u[:, 0, :], vec[:, l, V_LN2B:V_LN2B + KD]))
                    V.memset(d_mix[:, 0:1], 0.0).then_inc(part1, 1)
                layernorm(l, 1)
            for i in range(TT):
                dve.wait_ge(out_turned, i + 1)
                V.tensor_copy(x_tok[:, i, 0:512], scores[:, 0, :]).then_inc(out_dve, 1)

        @block.tensor
        def _(pe):
            M = nc.tensor.matmul

            pe.wait_ge(const_in, 16)
            pe.wait_ge(vec_in, 16 * 13 * DEPTH)
            for l in range(DEPTH):
                nc.tensor.transpose(turned[:, l, 0:V_ROWS], vec_rows[:, l, :], ident[0:V_ROWS, 0:V_ROWS])\
                    .then_inc(vec_turned, 1)
            pe.wait_ge(setup_done, 1)

            def reduce_ada(l, m):
                n = ada_job(l, m)
                pe.wait_ge(ada_summed, n + 1)
                M(ada_ps[:, m:m + 1], ada_acc[:, n % 4, :], one_col, start=True, stop=True)\
                    .then_inc(ada_reduced, 1)

            one_col = cst[:, C_ANY + 1:C_ANY + 2]
            for m in range(ADA1):
                reduce_ada(0, m)
            pe.wait_ge(x_in, 16)
            for k in range(KD):
                if k >= 2:
                    pe.wait_ge(u_ready, k - 1)
                for i in range(TT):
                    last = nc.tensor.transpose(scores[:, k % 2, i * P:(i + 1) * P],
                                               x_tok[:, i, k * P:(k + 1) * P], ident)
                last.then_inc(x_turned, 1)

            def take_bank(l, name):
                n = chunk(l, name)
                if n >= 2:
                    pe.wait_ge(chunk_saved[n % 2], n // 2)
                return proj[:, n % 2, :]

            def take_slot(l, name):
                g = l * len(JOBS) + JOB_AT[name]
                pe.wait_ge(slot_ready[g % NS], READY[g])
                return ring[:, g % NS, :]

            def done(l, name, ins):
                ins.then_inc(chunk_done[chunk(l, name) % 2], 1)

            def project(l, name, job, at, src=None, width=256, fresh=None):
                src = uT if src is None else src
                w = take_slot(l, job)
                bank = take_bank(l, name)
                for k in range(KD):
                    if fresh is not None:
                        pe.wait_ge(u_ready, fresh * KD + k + 1)
                    last = M(bank, w[:, k * width + at:k * width + at + P], src[:, k, :],
                             start=k == 0, stop=k == KD - 1)
                done(l, name, last)

            def score(l, i, j):
                s = score_step(l, i, j)
                if s >= 1:
                    pe.wait_ge(exp_done, s)
                tile = slice(i * P, (i + 1) * P)
                if j == 0:
                    for h in range(2):
                        M(scores[:, h, 0:P], ident_b[:, :], mask_b[:, P + i * P:2 * P + i * P],
                          start=True, stop=True)
                    for c in range(4):
                        for h in range(2):
                            rows = slice(64 * h, 64 * h + 64)
                            last = M(scores[:, h, NCP * c:NCP * (c + 1)], q_raw[rows, c, tile],
                                     k_cmpT[rows, NCP * (c // 2):NCP * (c // 2 + 1)],
                                     start=False, stop=True, skip_group_check=True)
                    last.then_inc(scored, 1)
                    return
                N = (i + 1) * P
                for h in range(2):
                    rows = slice(64 * h, 64 * h + 64)
                    if j <= 8:
                        c = (j - 1) % 4
                        q, k = q_rot[rows, c, tile], k_dup[rows, (j - 1) // 4, c // 2, 0:N]
                    else:
                        q, k = qdT[rows, j - 9, tile], kdT[rows, j - 9, 0:N]
                    M(scores[:, h, 0:N], q, k, start=True, stop=True)
                for h in range(2):
                    last = M(scores[:, h, i * P:N], ident_b[:, :], mask_b[:, 0:P], start=False, stop=True,
                             skip_group_check=True)
                last.then_inc(scored, 1)

            def free_turned(l, i, j):
                if (i, j) == (0, 0):
                    if l:
                        pe.wait_ge(turn_dve, turned_by_dve(l, 0, -1))
                    return
                if j == 0:
                    i, j = i - 1, STEPS + 1
                pe.wait_ge(turn_act, turned_by_act(l, i, j - 1))
                pe.wait_ge(turn_dve, turned_by_dve(l, i, j - 1))

            def turn(l, i, j):
                s = score_step(l, i, j)
                free_turned(l, i, j)
                if j < STEPS:
                    pe.wait_ge(exp_done, s + 1)
                if 9 <= j < STEPS:
                    pe.wait_ge(mix_done, (l * TT + i) * 4 + j - 8)
                if j == STEPS:
                    pe.wait_ge(nsa_ready, l * TT + i + 1)
                    blocks = [(0, c, o_nsa[:, c * P:(c + 1) * P]) for c in range(4)]
                elif j == 0:
                    blocks = [(0, g, probs[:, s % 2, 0, g * P:(g + 1) * P]) for g in range(2)]
                else:
                    blocks = [(h, b, probs[:, s % 2, h, b * P:(b + 1) * P])
                              for h in range(2 if j <= 8 else 1) for b in range(i + 1)]
                for h, b, src in blocks:
                    last = nc.tensor.transpose(turned[:, h, b * P:(b + 1) * P], src, ident)
                last.then_inc(turn_done, 1)

            def values(l, i, j):
                s = score_step(l, i, j)
                q = out_bank(l, i, j)
                bank = outs[:, q % 2, :]
                if j in (0, 1, 5, 9) and q >= 2:
                    pe.wait_ge(out_saved, q - 1)
                if j <= 8:
                    pe.wait_ge(turn_dve, turned_by_dve(l, i, j))
                if j >= 1:
                    pe.wait_ge(turn_act, turned_by_act(l, i, j))
                if j == 0:
                    for g in range(2):
                        last = M(bank[:, 256 * g:256 * (g + 1)], probsT[:, s % 2, 0, g * P:(g + 1) * P],
                                 v_cmp[:, g, :], start=True, stop=True)
                elif j <= 8:
                    br, c = (j - 1) // 4, (j - 1) % 4
                    for h in range(2):
                        head = 2 * c + h
                        v = slice(128 * br + 64 * (c // 2), 128 * br + 64 * (c // 2) + 64)
                        for b in range(i + 1):
                            last = M(bank[:, 64 * head:64 * head + 64], probsT[:, s % 2, h, b * P:(b + 1) * P],
                                     v_tok[:, b, v], start=b == 0, stop=b == i)
                else:
                    hd = j - 9
                    for b in range(i + 1):
                        last = M(bank[:, P * hd:P * (hd + 1)], probsT[:, s % 2, 0, b * P:(b + 1) * P],
                                 vd_tok[:, b, P * hd:P * (hd + 1)], start=b == 0, stop=b == i)
                if j in (0, 4, 8, 12):
                    last.then_inc(out_done, 1)
                    pe.wait_ge(out_done, q + 1)
                    pe.sem_inc(pv_done, 1)
                else:
                    last.then_inc(pv_done, 1)

            def merge_gate(l, n):
                m, k = divmod(n, KD)
                name = f"gm{m}"
                if k == 0:
                    take_slot(l, f"gm{m // 2}")
                    take_bank(l, name)
                w = ring[:, (l * len(JOBS) + JOB_AT[f"gm{m // 2}"]) % NS, :]
                at = k * 256 + (m % 2) * P
                ins = M(bank_of(l, name), w[:, at:at + P], uT[:, k, :], start=k == 0, stop=k == KD - 1)
                if k == KD - 1:
                    done(l, name, ins)

            def mean_step(l, which, m):
                wait_saved(pe, l, f"wo{m}" if which == 0 else f"fo{m}")
                ins = M(mean_ps, ones[:, :], yT[:, m, :], start=m == 0, stop=m == KD - 1)
                if m == KD - 1:
                    ins.then_inc(mean_done, 1)

            def variance(l, which):
                n = 2 * l + which
                for m in range(KD):
                    pe.wait_ge(squared, n * KD + m + 1)
                    ins = M(var_ps, ones[:, :], uT[:, m, :], start=m == 0, stop=m == KD - 1)
                ins.then_inc(var_done, 1)

            for l in range(DEPTH):
                ada_at = [ADA1]

                def reduce_two():
                    for _ in range(2):
                        if ada_at[0] < 48:
                            reduce_ada(l, ada_at[0])
                            ada_at[0] += 1

                fresh = 2 * l
                project(l, "kc", "kv", 0, fresh=fresh)
                project(l, "vc", "kv", P)
                project(l, "ksl", "kk", 0)
                reduce_two()
                project(l, "kwn", "kk", P)
                reduce_two()
                for i in range(TT):
                    w = take_slot(l, "vg")
                    bank = take_bank(l, f"vg{i}")
                    for k in range(KD):
                        last = M(bank[:, 0:280], uT[:, k, i * P:(i + 1) * P], w[:, 280 * k:280 * (k + 1)],
                                 start=k == 0, stop=k == KD - 1)
                    done(l, f"vg{i}", last)
                    reduce_two()
                for i in range(4):
                    project(l, f"qn{i}", f"qn{i // 2}", (i % 2) * P)
                    reduce_two()
                for w, name in enumerate(("hk", "hv")):
                    bank = take_bank(l, name)
                    pe.wait_ge(flat_ready, 2 * l + w + 1)
                    slots = [take_slot(l, f"w1{name[1]}{half}") for half in range(2)]
                    for m in range(2):
                        dst = bank[:, 2 * NCP * m:2 * NCP * (m + 1)].rearrange("p (g n) -> p g n", g=2)[:, :, 0:NC]
                        for j in range(KJ):
                            at = (j % 8) * 256 + m * P
                            last = M(dst, slots[j // 8][:, at:at + P],
                                     flat[:, w, j, :].rearrange("p (g n) -> p g n", g=2)[:, :, 0:NC],
                                     start=j == 0, stop=j == KJ - 1)
                    done(l, name, last)
                    reduce_two()
                bank = take_bank(l, "kv2")
                wait_saved(pe, l, "hk")
                for m in range(2):
                    M(bank[:, 0:2 * NCP], w2k[:, l, m].rearrange("p a d -> p (a d)"), hid[:, 0, m, :],
                      start=m == 0, stop=m == 1)
                pe.wait_ge(rep_ready, l + 1)
                for g in range(2):
                    for m in range(2):
                        last = M(bank[:, 64 + 64 * g:128 + 64 * g],
                                 hid_rep[:, m, g].rearrange("p r n -> p (r n)"), w2v[:, l, m, :],
                                 start=m == 0, stop=m == 1)
                done(l, "kv2", last)
                for i in range(4):
                    project(l, f"kd{i}", f"kd{i // 2}", (i % 2) * P)
                    reduce_two()
                for i in range(4):
                    project(l, f"qd{i}", f"qd{i // 2}", (i % 2) * P)
                    reduce_two()
                while ada_at[0] < 48:
                    reduce_two()
                for i in range(TT):
                    halves = [take_slot(l, "vd0"), take_slot(l, "vd1")]
                    bank = take_bank(l, f"vd{i}")
                    for h in range(2):
                        for k in range(KD):
                            last = M(bank[:, 256 * h:256 * (h + 1)], uT[:, k, i * P:(i + 1) * P],
                                     halves[h][:, 256 * k:256 * (k + 1)], start=k == 0, stop=k == KD - 1)
                    done(l, f"vd{i}", last)

                pe.wait_ge(rope_done, 14 * (l + 1))
                wait_saved(pe, l, "kv2")
                wait_saved(pe, l, "vd2")
                wait_saved(pe, l, "vd3")
                pe.wait_ge(part2, l + 1)
                for t in range(len(SEQUENCE) + 2):
                    if t < len(SEQUENCE) and SEQUENCE[t][1] < STEPS:
                        score(l, *SEQUENCE[t])
                    if t < len(SEQUENCE):
                        merge_gate(l, 2 * t)
                    if 1 <= t <= len(SEQUENCE):
                        turn(l, *SEQUENCE[t - 1])
                    if t < len(SEQUENCE):
                        merge_gate(l, 2 * t + 1)
                    if t >= 2 and SEQUENCE[t - 2][1] < STEPS:
                        values(l, *SEQUENCE[t - 2])
                for n in range(14 * KD, 16 * KD):
                    merge_gate(l, n)
                pe.wait_ge(turn_act, turned_by_act(l, TT - 1, STEPS))
                for i in range(TT):
                    pe.wait_ge(dnorm_ready, l * TT + i + 1)
                    if i >= 2:
                        pe.wait_ge(turn_dve, turned_by_dve(l, TT, -1) + i - 1)
                    for c in range(4):
                        last = nc.tensor.transpose(turned[:, i % 2, c * P:(c + 1) * P],
                                                   q_raw[:, c, i * P:(i + 1) * P], ident)
                    last.then_inc(turn_done, 1)
                pe.wait_ge(turn_dve, turned_by_dve(l, TT, -1) + TT)
                for m in range(KD):
                    w = take_slot(l, f"br{m // 2}")
                    for h, (a, src) in enumerate((("n", q_rot), ("d", q_raw))):
                        bank = take_bank(l, f"y{a}{m}")
                        for k in range(4):
                            at = 1024 * h + 256 * k + (m % 2) * P
                            last = M(bank, w[:, at:at + P], src[:, k, :], start=k == 0, stop=k == 3)
                        done(l, f"y{a}{m}", last)
                pe.wait_ge(merged, KD * (l + 1))
                for m in range(KD):
                    project(l, f"wo{m}", f"wo{m // 2}", (m % 2) * P, src=mergedT)
                    if m:
                        mean_step(l, 0, m - 1)
                mean_step(l, 0, KD - 1)
                variance(l, 0)
                for f in range(KF):
                    project(l, f"fa{f}", f"ff{f}", 0, fresh=2 * l + 1 if f == 0 else None)
                    project(l, f"fb{f}", f"ff{f}", P)
                    if l + 1 < DEPTH and 1 <= f <= ADA1:
                        reduce_ada(l + 1, f - 1)
                for m in range(KD):
                    halves = [take_slot(l, f"fo{2 * m + h}") for h in range(2)]
                    bank = take_bank(l, f"fo{m}")
                    if m == 0:
                        wait_saved(pe, l, f"fb{KF - 1}")
                        wait_saved(pe, l, f"fb{KF - 2}")
                    for k in range(KF):
                        at = (k % 11) * P
                        last = M(bank, halves[k // 11][:, at:at + P], hT[:, k, :],
                                 start=k == 0, stop=k == KF - 1)
                    done(l, f"fo{m}", last)
                    if m:
                        mean_step(l, 1, m - 1)
                mean_step(l, 1, KD - 1)
                variance(l, 1)
            pe.wait_ge(u_ready, (2 * DEPTH + 1) * KD)
            for i in range(TT):
                if i >= 1:
                    pe.wait_ge(out_dve, i)
                    pe.wait_ge(out_act, i)
                for k in range(KD):
                    last = nc.tensor.transpose(scores[:, k // 4, (k % 4) * P:(k % 4 + 1) * P],
                                               uT[:, k, i * P:(i + 1) * P], ident)
                last.then_inc(out_turned, 1)


def constants():
    c = np.zeros((P, C_COLS), np.float32)
    rot = HEAD_DIM // ROPE_FRACTION
    half = rot // 2
    inv = np.float32(ROPE_THETA) ** (-np.arange(half, dtype=np.float32) * np.float32(2.0) / np.float32(rot))
    ang = (np.arange(SEQ, dtype=np.float32)[:, None] * inv.astype(np.float32)[None, :]).T
    c[:, C_COS:C_COS + SEQ] = 1.0
    for base in (0, 64):
        c[base:base + half, C_COS:C_COS + SEQ] = np.cos(ang)
        c[base + half:base + rot, C_COS:C_COS + SEQ] = np.cos(ang)
        c[base:base + half, C_SIN:C_SIN + SEQ] = -np.sin(ang)
        c[base + half:base + rot, C_SIN:C_SIN + SEQ] = np.sin(ang)
    c[:, C_ID:C_ID + P] = np.eye(P)
    q = np.arange(P)
    c[:, C_CAUSAL:C_CAUSAL + P] = np.where(q[None, :] <= q[:, None], 0.0, NEG_INF)
    ends = np.arange(NCP) * CMP_STRIDE + CMP_BLOCK - 1
    for i in range(TT):
        m = np.where(ends[None, :] <= (i * P + q)[:, None], 0.0, NEG_INF)
        c[:, C_CMP + i * P:C_CMP + (i + 1) * P] = np.tile(m, (1, 4))
    c[:, C_ANY] = (q >= CMP_BLOCK - 1)
    c[:, C_ANY + 1] = 1.0
    c[:, C_LAM:C_LAM + DEPTH] = np.array(LAMBDA_INIT)[None, :]
    return c


_INS = ["x", "w_ada", "b_ada", "c", "w_in", "cmp_pe_k", "cmp_w1_k", "cmp_w2_k", "cmp_pe_v", "cmp_w1_v",
        "cmp_w2_v", "diff_lambda", "diff_norm_g", "w_branch_nsa", "w_branch_diff", "w_out", "ln1_g",
        "ln1_b", "w_ffn_in", "w_ffn_out", "ln2_g", "ln2_b"]


def kernel(**inputs):
    import numpy as _np
    import concourse.bacc as _bacc
    from concourse import mybir as _mybir
    from concourse.bass_utils import run_bass_kernel_spmd as _run

    nc = _bacc.Bacc("TRN2", target_bir_lowering=False, num_devices=1)
    arrays, args = {}, []
    for name in _INS + ["consts"]:
        a = _np.ascontiguousarray(inputs[name]) if name != "consts" else constants()
        arrays[f"in_{name}_dram"] = a
        args.append(nc.dram_tensor(f"in_{name}_dram", a.shape, _mybir.dt.from_np(a.dtype),
                                   kind="ExternalInput").ap())
    args.append(nc.dram_tensor("out_0_dram", (1, SEQ, D_MODEL), _mybir.dt.float32,
                               kind="ExternalOutput").ap())
    build(nc, *args)
    r = _run(nc, [arrays], core_ids=[0])
    return r.results[0]["out_0_dram"]
```

```python
import math
from contextlib import ExitStack

import numpy as np

import concourse.bass as bass
from concourse import mybir

D_MODEL, SEQ, DEPTH = 1024, 512, 2
HEAD_DIM, NSA_HEADS, DIFF_HEADS = 64, 8, 4
NSA_WIDTH, NSA_KV_WIDTH = 512, 128
CMP_BLOCK, CMP_STRIDE, CMP_HIDDEN = 32, 16, 256
D_FF = -(-8 * D_MODEL // (3 * 256)) * 256
ROPE_THETA, ROPE_FRACTION = 500000.0, 4
ALPHA = (2 * DEPTH) ** 0.25
EPS = 1e-5
NEG_INF = -1e30
IN_SIZES = dict(q_n=512, kc=128, vc=128, ksl=128, vsl=128, kwn=128, vwn=128, g_n=24,
                q_d=512, k_d=512, v_d=512, g_m=2048)
IN_AT = dict(zip(IN_SIZES, np.cumsum([0] + list(IN_SIZES.values()))[:-1].tolist()))
LAMBDA_INIT = [0.8 - 0.6 * math.exp(-0.3 * l) for l in range(DEPTH)]

P = 128
TT = SEQ // P
KD = D_MODEL // P
KF = D_FF // P
NC = (SEQ - CMP_BLOCK) // CMP_STRIDE + 1
NCP = 32
KJ = CMP_BLOCK * HEAD_DIM // P

V_ADA, V_LN1G, V_LN1B, V_LN2G, V_LN2B, V_NORM, V_PEK, V_PEV, V_C = 0, 48, 56, 64, 72, 80, 81, 97, 113
V_ROWS = 121

C_COS, C_SIN, C_ID, C_ANY, C_LAM = 0, 512, 1024, 1152, 1154
C_MASKS = C_LAM + DEPTH
C_COLS = C_MASKS + P + TT * P

GM_IN = 12
TOKEN = ["vs", "vw", "g"] + [f"vd{i}" for i in range(4)]
CHUNKS = (["kc", "vc", "ksl", "kwn", "vs", "vw", "g"] + [f"qn{i}" for i in range(4)]
          + ["hk", "hv", "kv2"] + [f"kd{i}" for i in range(4)] + [f"qd{i}" for i in range(4)]
          + [f"vd{i}" for i in range(4)] + [f"gm{i}" for i in range(16)]
          + [f"y{a}{i}" for i in range(KD) for a in "nd"] + [f"wo{i}" for i in range(KD)]
          + [f"f{a}{i}" for i in range(KF) for a in "ab"] + [f"fo{i}" for i in range(KD)])
CHUNK_AT = {name: i for i, name in enumerate(CHUNKS)}
W_IN_AT = {"kc": IN_AT["kc"], "vc": IN_AT["vc"], "ksl": IN_AT["ksl"], "kwn": IN_AT["kwn"],
           "vs": IN_AT["vsl"], "vw": IN_AT["vwn"], "g": IN_AT["g_n"]}
for _a, _n, _k in (("qn", "q_n", 4), ("kd", "k_d", 4), ("qd", "q_d", 4), ("vd", "v_d", 4), ("gm", "g_m", 16)):
    W_IN_AT.update({f"{_a}{i}": IN_AT[_n] + P * i for i in range(_k)})


def chunk(l, name):
    return l * len(CHUNKS) + CHUNK_AT[name]


JOBS = (["kc", "vc", "ksl", "kwn", "vs", "vw", "g"] + [f"qn{i}" for i in range(4)]
        + ["kd0"] + [f"w1{a}{i}" for a in "kv" for i in range(4)]
        + [f"{a}{i}" for a in ("kd", "qd", "vd") for i in range(4)][1:]
        + [f"gm{i}" for i in range(16)] + ["wo0"] + [f"br{i}" for i in range(KD)]
        + [f"wo{i}" for i in range(1, KD)]
        + [f"f{a}{i}" for i in range(KF) for a in "ab"] + [f"fo{i}" for i in range(2 * KD)])
JOB_AT = {name: i for i, name in enumerate(JOBS)}
SPLIT = [name for name in JOBS if name[:2] not in ("w1", "br")]
SPLIT_AT = {name: i for i, name in enumerate(SPLIT)}
NS = 2
NQ = 2
KH = KF // 2
SLOT = KH * P


def ready_counts():
    total, out = [0] * NS, []
    for g in range(DEPTH * len(JOBS)):
        total[g % NS] += 32 if JOBS[g % len(JOBS)][:2] == "br" else 16
        out.append(total[g % NS])
    return out


READY = ready_counts()


def split_job(l, name):
    return l * len(SPLIT) + SPLIT_AT[name]


def reader(name):
    return f"fo{int(name[2:]) // 2}" if name[:2] == "fo" else name


def prepared_at(l, name):
    out = []
    for i, job in enumerate(SPLIT):
        if reader(job) == name:
            nl, ni = (l, i + 1) if i + 1 < len(SPLIT) else (l + 1, 0)
            if nl < DEPTH and SPLIT[ni] not in ("vc", "fb0"):
                out.append((nl, SPLIT[ni]))
    return out


RAW = ["ksl", "kwn", "vs", "vw", "g"] + [f"{a}{i}" for a in ("kd", "qd", "vd") for i in range(4)]
ROPE = ["ksl", "kwn"] + [f"{a}{i}" for a in ("qn", "kd", "qd") for i in range(4)]


def gate_units(t):
    n, steps = GM_IN * KD, TT * (STEPS + 1)
    return [divmod(u, KD) for u in range(n * t // steps, n * (t + 1) // steps)]


ADA1, ADA2 = 16, 32


def ada_job(l, m):
    return 48 * l + m


STEPS = 13
SEQUENCE = [(i, j) for i in range(TT) for j in range(STEPS + 1)]


def score_step(l, i, j):
    return (l * TT + i) * STEPS + j


def turn_step(l, i, j):
    return l * (TT * (STEPS + 1) + TT) + i * (STEPS + 1) + j


def turned_by_act(l, i, j):
    return (l * TT + i) * STEPS + j


def turned_by_dve(l, i, j):
    return l * (9 * TT + TT) + 9 * i + min(j + 1, 9)


def out_bank(l, i, j):
    return (l * TT + i) * 4 + (0 if j == 0 else (j - 1) // 4 + 1)


def build(nc, x, w_ada, b_ada, c, w_in, pe_k, w1_k, w2_k, pe_v, w1_v, w2_v, lam, norm_g,
          w_bn, w_bd, w_o, ln1_g, ln1_b, w_f1, w_f2, ln2_g, ln2_b, consts, out):
    fp32, fp32r, bf16 = mybir.dt.float32, mybir.dt.float32r, mybir.dt.bfloat16
    ALU, ACT, AX = mybir.AluOpType, mybir.ActivationFunctionType, mybir.AxisListType

    ctx = ExitStack()
    with ctx:
        def sb(name, shape, dt=fp32):
            return ctx.enter_context(nc.sbuf_tensor(name, shape, dt))

        def sem(name):
            return ctx.enter_context(nc.semaphore(name))

        ring = sb("ring", [P, NS, SLOT])
        w_hi = sb("w_hi", [P, NQ, SLOT], fp32r)
        w_lo = sb("w_lo", [P, NQ, SLOT], fp32r)
        ada_ring = sb("ada_ring", [P, 2, KD, P])
        res = sb("res", [P, KD, SEQ])
        arena_at = -(-nc.sbuf_base // 32) * 32
        sb("arena", [P, 62 * SEQ])

        def at(name, first, n, dt=fp32):
            return nc.alloc_sbuf_tensor_at(name, [P, n, SEQ], dt, offset=arena_at + 4 * SEQ * first)

        gm_all = at("gm", 0, GM_IN)
        q_raw = at("q_raw", 12, 4)
        q_rot = at("q_rot", 16, 4)
        probs_all = at("probs", 20, 4)
        probsT_all = at("probsT", 24, 4)
        qdT = at("qdT", 28, 4)
        kdT = at("kdT", 32, 4)
        k_dup_all = at("k_dup", 36, 4)
        gm_late = at("gm_late", 36, 4)
        vd_all = at("vd_tok", 40, 4)
        v_all = at("v_tok", 44, 2)
        kc2_all = at("kc2", 0, 4)
        flat_all = at("flat", 4, 4)
        hid_rep_all = at("hid_rep", 8, 1)
        merged_hi = at("merged_hi", 20, KD, fp32r)
        merged_lo = at("merged_lo", 28, KD, fp32r)
        merged_raw = at("merged_raw", 28, KD)
        h_hi = at("h_hi", 0, KF, fp32r)
        h_lo = at("h_lo", KF, KF, fp32r)
        h_raw = at("h_raw", KF, KF)
        u_hi = at("u_hi", 46, KD, fp32r)
        u_lo = at("u_lo", 46 + KD, KD, fp32r)
        squares = at("squares", 46, KD)
        yT = at("yT", 46 + KD, KD)
        x_all = at("x_tok", 28, KD)
        mask_in = at("mask_in", 20, 2)
        vec_in_all = at("vec_rows", 22, 1)
        lam_in_all = at("lam_in", 23, 1)
        probs = probs_all[:, :, :].rearrange("p (r h) k -> p r h k", r=2)
        probsT = probsT_all[:, :, :].rearrange("p (r h) k -> p r h k", r=2)
        k_dup = k_dup_all[:, :, :].rearrange("p (b g) t -> p b g t", b=2)
        vd_tok = vd_all[:, :, :]
        v_tok = v_all[:, :, :].rearrange("p a (i n) -> p (a i) n", n=256)
        kc2 = kc2_all[:, :, :].rearrange("p (w g) t -> p w g t", w=2)
        flat = flat_all[:, :, :].rearrange("p (w a) (b n) -> p w (a b) n", w=2, n=2 * NCP)
        hid_rep = hid_rep_all[:, 0, :].rearrange("p (m g r n) -> p m g r n", m=2, g=2, r=4)
        x_tok = x_all[:, :, :].rearrange("p (i a) n -> p i (a n)", a=2)
        vec_rows = vec_in_all[0:V_ROWS, 0, 0:DEPTH * P].rearrange("p (l n) -> p l n", l=DEPTH)
        lam_in = lam_in_all[:, 0, :].rearrange("p (l a d) -> p l a d", l=DEPTH, a=4)

        def gm(m):
            return gm_all[:, m, :] if m < GM_IN else gm_late[:, m - GM_IN, :]

        gates = sb("gates", [P, TT, NSA_HEADS, 3])
        raw = sb("raw", [P, 2, SEQ])
        t1 = sb("t1", [P, SEQ])[:, :]
        t2 = sb("t2", [P, SEQ])[:, :]
        o_nsa = raw[:, 0, :]
        hid = sb("hid", [P, 2, 2, 2 * NCP])
        k_cmpT = sb("k_cmpT", [P, 2 * NCP])
        v_cmp = sb("v_cmp", [P, 2, 256])
        neg_max = sb("neg_max", [P, 2, 8])
        sums = sb("sums", [P, 2, 32])
        coef = sb("coef", [P, 2, 8])
        d_rs = sb("d_rs", [P, 2, 4])
        d_mix = sb("d_mix", [P, 2])
        d_sq = sb("d_sq", [P, TT * 4])
        sil = raw[:, :, :]
        cst = sb("cst", [P, C_MASKS])
        cos, sin, ident = cst[:, C_COS:C_COS + SEQ], cst[:, C_SIN:C_SIN + SEQ], cst[:, C_ID:C_ID + P]
        ident_b = sb("ident_b", [P, P], bf16)
        mask_b = sb("mask_b", [P, P + TT * P], bf16)
        ones = sb("ones", [P, P])
        eps = sb("eps", [P, 1])
        vec = sb("vec", [P, DEPTH, V_ROWS])
        lam_s = sb("lam_s", [P, DEPTH, 2])
        neg_lam = sb("neg_lam", [P, DEPTH])
        norm_s = sb("norm_s", [P, DEPTH])
        w2k = sb("w2k", [P, DEPTH, 2, 2, HEAD_DIM])
        w2v = sb("w2v", [P, DEPTH, 2, HEAD_DIM])
        c_silu = sb("c_silu", [P, KD])
        ada_acc = sb("ada_acc", [P, 4, P])
        ada = sb("ada", [P, DEPTH, 48])
        gate1 = sb("gate1", [P, 2, KD])
        mul_u = sb("mul_u", [P, 2, KD])
        add_u = sb("add_u", [P, 2, KD])
        mul_r = sb("mul_r", [P, 2, KD])
        add_r = sb("add_r", [P, 2, KD])

        banks = ctx.enter_context(nc.psum_tensor("banks", [P, 8, SEQ], fp32))
        proj = banks[:, 0:2, :]
        scores = banks[:, 2:4, :]
        turned = banks[:, 4:6, :]
        outs = banks[:, 6:8, :]
        ada_ps = outs[:, 0, 0:48]
        mean_ps, var_ps = scores[:, 0, :], scores[:, 1, :]

        const_in = sem("const_in")
        x_in = sem("x_in")
        vec_in = sem("vec_in")
        slot_ready = [sem(f"slot_ready{s}") for s in range(NS)]
        ada_ready = [sem(f"ada_ready{s}") for s in range(2)]
        ada_summed = sem("ada_summed")
        ada_reduced = sem("ada_reduced")
        setup_done = sem("setup_done")
        vec_turned = sem("vec_turned")
        vec_saved = sem("vec_saved")
        c_ready = sem("c_ready")
        lam_summed = sem("lam_summed")
        lam_exp = sem("lam_exp")
        x_turned = sem("x_turned")
        x_saved = sem("x_saved")
        part1 = sem("part1")
        part2 = sem("part2")
        chunk_done = [sem(f"chunk_done{b}") for b in range(2)]
        chunk_saved = [sem(f"chunk_saved{b}") for b in range(2)]
        split_hi = sem("split_hi")
        split_lo = sem("split_lo")
        half_read = sem("half_read")
        w1_read = sem("w1_read")
        token_saved = sem("token_saved")
        token_turned = sem("token_turned")
        gates_ready = sem("gates_ready")
        u_high = sem("u_high")
        merged_sum = sem("merged_sum")
        merged_high = sem("merged_high")
        h_high = sem("h_high")
        h_ready = sem("h_ready")
        ada_scaled = sem("ada_scaled")
        flat_ready = sem("flat_ready")
        rep_ready = sem("rep_ready")
        rope_done = sem("rope_done")
        scored = sem("scored")
        max_done = sem("max_done")
        exp_done = sem("exp_done")
        mix_done = sem("mix_done")
        turn_done = sem("turn_done")
        turn_act = sem("turn_act")
        turn_dve = sem("turn_dve")
        pv_done = sem("pv_done")
        out_done = sem("out_done")
        out_saved = sem("out_saved")
        nsa_ready = sem("nsa_ready")
        dsq_ready = sem("dsq_ready")
        dstd_ready = sem("dstd_ready")
        dnorm_ready = sem("dnorm_ready")
        sig_ready = sem("sig_ready")
        merged = sem("merged")
        mean_done = sem("mean_done")
        centred = sem("centred")
        squared = sem("squared")
        var_done = sem("var_done")
        std_ready = sem("std_ready")
        normed = sem("normed")
        u_ready = sem("u_ready")
        res_ready = sem("res_ready")
        out_turned = sem("out_turned")
        out_dve = sem("out_dve")
        out_act = sem("out_act")
        stored = sem("stored")
        dve_chain = sem("dve_chain")
        act_chain = sem("act_chain")

        block = ctx.enter_context(nc.Block())

        def wait_done(eng, l, name):
            n = chunk(l, name)
            eng.wait_ge(chunk_done[n % 2], n // 2 + 1)

        def wait_saved(eng, l, name):
            n = chunk(l, name)
            eng.wait_ge(chunk_saved[n % 2], n // 2 + 1)

        def bank_of(l, name):
            return proj[:, chunk(l, name) % 2, :]

        def saved(l, name):
            return chunk_saved[chunk(l, name) % 2]

        def cols(w, lo, hi):
            return w[:, lo:hi].rearrange("(k p) n -> p k n", p=P)

        def weights_in(eng, l, name):
            g = l * len(JOBS) + JOB_AT[name]
            eng.wait_ge(slot_ready[g % NS], READY[g])
            return ring[:, g % NS, 0:(KH if name[:2] == "fo" else KD) * P]

        def split_slot(l, name):
            n, size = split_job(l, name), (KH if name[:2] == "fo" else KD) * P
            return w_hi[:, n % NQ, 0:size], w_lo[:, n % NQ, 0:size]

        @block.sync
        def _(sp):
            sp.dma_start(cst[:, :], consts[:, 0:C_MASKS]).then_inc(const_in, 16)
            sp.dma_start(mask_in[:, :, :].rearrange("p a n -> p (a n)")[:, 0:P + TT * P],
                         consts[:, C_MASKS:C_COLS]).then_inc(const_in, 16)
            sp.dma_start(x_tok, x[0].rearrange("(i p) n -> p i n", p=P)).then_inc(x_in, 16)

            def wait_read(l, name):
                if name in SPLIT_AT:
                    sp.wait_ge(split_lo, split_job(l, name) + 1)
                elif name[:2] == "br":
                    wait_done(sp, l, f"yd{name[2:]}")
                elif name[-1] == "3":
                    wait_done(sp, l, f"h{name[2]}")
                else:
                    sp.wait_ge(w1_read, 6 * l + 3 * "kv".index(name[2]) + int(name[-1]) + 1)

            for l in range(DEPTH):
                for i, name in enumerate(JOBS):
                    g = l * len(JOBS) + i
                    s = g % NS
                    if g >= NS:
                        wait_read((g - NS) // len(JOBS), JOBS[(g - NS) % len(JOBS)])
                    slot = ring[:, s, :]
                    if name in W_IN_AT:
                        srcs = [cols(w_in[l], W_IN_AT[name], W_IN_AT[name] + P)]
                    elif name[:2] == "w1":
                        m, half = divmod(int(name[-1]), 2)
                        w1 = w1_k if name[2] == "k" else w1_v
                        srcs = [cols(w1[l, KD * P * half:KD * P * (half + 1), :], P * m, P * (m + 1))]
                    elif name[:2] == "br":
                        m = int(name[2:])
                        srcs = [cols(w[l], P * m, P * (m + 1)) for w in (w_bn, w_bd)]
                    elif name[:2] == "wo":
                        m = int(name[2:])
                        srcs = [cols(w_o[l], P * m, P * (m + 1))]
                    elif name[:2] == "fo":
                        m, half = divmod(int(name[2:]), 2)
                        srcs = [cols(w_f2[l, KH * P * half:KH * P * (half + 1), :], P * m, P * (m + 1))]
                    else:
                        first = P * int(name[2:]) + (D_FF if name[1] == "b" else 0)
                        srcs = [cols(w_f1[l], first, first + P)]
                    k = 0
                    for src in srcs:
                        n = src.shape[1]
                        dst = slot[:, k * P:(k + n) * P].rearrange("p (k n) -> p k n", n=P)
                        sp.dma_start(dst, src).then_inc(slot_ready[s], 16)
                        k += n
            for i in range(TT):
                sp.wait_ge(out_dve, i + 1)
                sp.wait_ge(out_act, i + 1)
                sp.dma_start(out[0, i * P:(i + 1) * P, :], x_tok[:, i, :]).then_inc(stored, 16)
            sp.wait_ge(stored, 16 * TT)

        @block.gpsimd
        def _(pool):
            def load_ada(l, m):
                n = ada_job(l, m)
                if n >= 2:
                    pool.wait_ge(ada_summed, n - 1)
                pool.dma_start(ada_ring[:, n % 2], cols(w_ada[l], P * m, P * (m + 1)))\
                    .then_inc(ada_ready[n % 2], 16)

            def residual(l, which):
                for m in range(KD):
                    pool.wait_ge(normed, (2 * l + which) * KD + m + 1)
                    if m == 0:
                        pool.wait_ge(part2 if which == 0 else part1, l + 1 + which)
                    nc.gpsimd.tensor_scalar(res[:, m, :], yT[:, m, :], mul_r[:, which, m:m + 1],
                                            add_r[:, which, m:m + 1], ALU.mult, ALU.add)\
                        .then_inc(res_ready, 1)

            def scale_ada(n):
                pool.wait_ge(ada_ready[n % 2], 16 * (n // 2 + 1))
                w = ada_ring[:, n % 2]
                nc.gpsimd.tensor_tensor(w, w, c_silu[:, :].unsqueeze(2).to_broadcast([P, KD, P]), ALU.mult)\
                    .then_inc(ada_scaled, 1)

            def ada_jobs(l, first, last):
                load_ada(l, first)
                for m in range(first, last):
                    if m + 1 < last:
                        load_ada(l, m + 1)
                    if (l, m) == (0, 0):
                        pool.wait_ge(c_ready, 1)
                    scale_ada(ada_job(l, m))

            ada_jobs(0, 0, ADA1)
            for l in range(DEPTH):
                ada_jobs(l, ADA1, 48)
                residual(l, 0)
                if l + 1 < DEPTH:
                    ada_jobs(l + 1, 0, ADA1)
                    residual(l, 1)

        @block.scalar
        def _(act):
            count = [0]

            def link(ins):
                count[0] += 1
                ins.then_inc(act_chain, 1)
                act.wait_ge(act_chain, count[0])

            for l in range(DEPTH):
                for at, src in ((V_ADA, b_ada[l].rearrange("(m p) -> m p", p=P)),
                                (V_LN1G, ln1_g[l].rearrange("(m p) -> m p", p=P)),
                                (V_LN1B, ln1_b[l].rearrange("(m p) -> m p", p=P)),
                                (V_LN2G, ln2_g[l].rearrange("(m p) -> m p", p=P)),
                                (V_LN2B, ln2_b[l].rearrange("(m p) -> m p", p=P)),
                                (V_NORM, norm_g[l:l + 1, :]),
                                (V_PEK, pe_k[l].rearrange("(j c) d -> j (c d)", c=2)),
                                (V_PEV, pe_v[l].rearrange("(j c) d -> j (c d)", c=2)),
                                (V_C, c[0].rearrange("(m p) -> m p", p=P))):
                    act.dma_start(vec_rows[at:at + src.shape[0], l, :], src).then_inc(vec_in, 16)
                act.dma_start(lam_in[:, l], lam[l].partition_broadcast(P)).then_inc(vec_in, 16)
                for d in range(2):
                    act.dma_start(w2k[:, l, :, d, :], w2_k[l].rearrange("(m p) d -> p m d", p=P))\
                        .then_inc(vec_in, 16)
                act.dma_start(w2v[:, l], w2_v[l].rearrange("(m p) d -> p m d", p=P)).then_inc(vec_in, 16)
            act.wait_ge(vec_saved, DEPTH)
            nc.scalar.activation(c_silu[:, :], vec[:, 0, V_C:V_C + KD], ACT.Silu).then_inc(c_ready, 1)
            act.wait_ge(lam_summed, 1)
            nc.scalar.activation(lam_s[:, :, :], lam_s[:, :, :], ACT.Exp).then_inc(lam_exp, 1)

            def prepare(l, name):
                n = split_job(l, name)
                src = weights_in(act, l, name)
                if n >= NQ:
                    ll, before = divmod(n - NQ, len(SPLIT))
                    if SPLIT[before][:2] == "fo" and int(SPLIT[before][2:]) % 2 == 0:
                        act.wait_ge(half_read, ll * KD + int(SPLIT[before][2:]) // 2 + 1)
                    else:
                        wait_done(act, ll, reader(SPLIT[before]))
                nc.scalar.activation(split_slot(l, name)[0], src, ACT.Copy).then_inc(split_hi, 1)

            def prepare_behind(l, name):
                for job in prepared_at(l, name):
                    prepare(*job)

            def sub_layer_input(n, m, src, scale, bias):
                if n * KD + m >= 2:
                    act.wait_ge(u_ready, n * KD + m - 1)
                link(nc.scalar.activation(raw[:, m % 2, :], src, ACT.Identity, bias=bias, scale=scale))
                nc.scalar.activation(u_hi[:, m, :], raw[:, m % 2, :], ACT.Copy).then_inc(u_high, 1)

            prepare(0, "kc")
            prepare(0, "vc")
            act.wait_ge(part1, 1)
            for k in range(KD):
                act.wait_ge(x_saved, k + 1)
                sub_layer_input(0, k, scores[:, k % 2, :], mul_u[:, 0, k:k + 1], ada[:, 0, k:k + 1])

            def save(l, name, dst, scale=1.0):
                prepare_behind(l, name)
                wait_done(act, l, name)
                nc.scalar.activation(dst, bank_of(l, name), ACT.Copy, scale=scale)\
                    .then_inc(saved(l, name), 1)

            def save_raw(l, name, r, scale=1.0):
                prepare_behind(l, name)
                if r == 0:
                    act.wait_ge(u_ready, (2 * l + 1) * KD)
                elif r >= 2:
                    before = RAW[r - 2]
                    if before in TOKEN:
                        act.wait_ge(token_turned, l * len(TOKEN) + TOKEN.index(before) + 1)
                    else:
                        act.wait_ge(rope_done, l * 14 + ROPE.index(before) + 1)
                wait_done(act, l, name)
                nc.scalar.activation(raw[:, r % 2, :], bank_of(l, name), ACT.Copy, scale=scale)\
                    .then_inc(saved(l, name), 1)

            def save_gate(l, m):
                wait_done(act, l, f"gm{m}")
                nc.scalar.activation(gm(m), bank_of(l, f"gm{m}"), ACT.Copy)\
                    .then_inc(saved(l, f"gm{m}"), 1)

            def layernorm(l, which):
                n = 2 * l + which
                last = l == DEPTH - 1 and which == 1
                for m in range(KD):
                    prepare_behind(l, ("wo", "fo")[which] + str(m))
                for m in range(KD):
                    act.wait_ge(centred, n * KD + m + 1)
                    nc.scalar.activation(squares[:, m, :], yT[:, m, :], ACT.Square).then_inc(squared, 1)
                if not last:
                    prepare(l + which, "vc" if which else "fb0")
                act.wait_ge(var_done, n + 1)
                nc.scalar.activation(t1, var_ps, ACT.Sqrt, bias=eps[:, :]).then_inc(std_ready, 1)
                w = 1 - which
                for m in range(KD):
                    act.wait_ge(normed, n * KD + m + 1)
                    if m == 0:
                        act.wait_ge(part2 if which == 0 else part1, l + 1 + which)
                    if last:
                        nc.scalar.activation(res[:, m, :], yT[:, m, :], ACT.Identity,
                                             bias=add_u[:, w, m:m + 1], scale=mul_u[:, w, m:m + 1])\
                            .then_inc(u_high, 1)
                    else:
                        sub_layer_input(n + 1, m, yT[:, m, :], mul_u[:, w, m:m + 1], add_u[:, w, m:m + 1])

            for l in range(DEPTH):
                wait_done(act, l, "kc")
                for g in range(2):
                    src = bank_of(l, "kc")[64 * g:64 * g + 64, :]
                    nc.scalar.activation(kc2[0:64, 0, g, :], src, ACT.Copy)
                    last = nc.scalar.activation(kc2[64:128, 0, g, 0:SEQ - 1], src[:, 1:SEQ], ACT.Copy)
                last.then_inc(saved(l, "kc"), 1)
                prepare_behind(l, "vc")
                for r, name in enumerate(RAW[:5]):
                    save_raw(l, name, r)
                for i in range(4):
                    save(l, f"qn{i}", q_raw[:, i, :], HEAD_DIM ** -0.5)
                    if i == 1:
                        act.wait_ge(token_saved, l * len(TOKEN) + 3)
                        nc.scalar.activation(gates[:, :, :, :], gates[:, :, :, :], ACT.Sigmoid)\
                            .then_inc(gates_ready, 1)
                for w, name in enumerate(("hk", "hv")):
                    wait_done(act, l, name)
                    dst = hid[:, w].rearrange("p m (g n) -> p m g n", g=2)[:, :, :, 0:NC]
                    src = bank_of(l, name)[:, 0:128].rearrange("p (m g n) -> p m g n", m=2, g=2)[:, :, :, 0:NC]
                    nc.scalar.activation(dst, src, ACT.Gelu_apprx_tanh).then_inc(saved(l, name), 1)
                for r, name in enumerate(RAW[5:], 5):
                    save_raw(l, name, r, HEAD_DIM ** -0.5 if name[:2] == "qd" else 1.0)

                for t in range(len(SEQUENCE) + 1):
                    if t >= 1:
                        for m, k in gate_units(t - 1):
                            if k == 0:
                                prepare_behind(l, f"gm{m}")
                        i, j = SEQUENCE[t - 1]
                        N = (i + 1) * P
                        if j >= 1:
                            act.wait_ge(turn_done, turn_step(l, i, j) + 1)
                            s = score_step(l, i, j)
                            if j == STEPS:
                                nc.scalar.activation(
                                    q_rot[:, :, i * P:(i + 1) * P],
                                    turned[:, 0, :].rearrange("p (c t) -> p c t", c=4), ACT.Copy)\
                                    .then_inc(turn_act, 1)
                            else:
                                act.wait_ge(pv_done, s - 1)
                                nc.scalar.activation(probsT[:, s % 2, 0, 0:N], turned[:, 0, 0:N], ACT.Copy)\
                                    .then_inc(turn_act, 1)
                    if t == len(SEQUENCE):
                        break
                    i, j = SEQUENCE[t]
                    if j < STEPS:
                        s = score_step(l, i, j)
                        N = (i + 1) * P
                        act.wait_ge(max_done, s + 1)
                        if j == 0:
                            nc.scalar.activation(probs[:, s % 2, 0, 0:256], probs[:, s % 2, 0, 0:256],
                                                 ACT.Exp).then_inc(exp_done, 1)
                        else:
                            if s >= 2:
                                i2, j2 = (i, j - 2) if j >= 2 else (i - 1, j + STEPS - 2)
                                if i2 >= 0:
                                    act.wait_ge(turn_done, turn_step(l, i2, j2) + 1)
                            for h in range(2):
                                at = 8 + 2 * (j - 1) + h
                                last = nc.scalar.activation(
                                    probs[:, s % 2, h, 0:N], scores[:, h, 0:N], ACT.Exp,
                                    bias=neg_max[:, s % 2, h:h + 1],
                                    accum_out=sums[:, i % 2, at:at + 1])
                            last.then_inc(exp_done, 1)
                    for m, k in gate_units(t):
                        if k == KD - 1:
                            save_gate(l, m)
                prepare_behind(l, f"gm{GM_IN}")
                act.wait_ge(dsq_ready, l + 1)
                nc.scalar.activation(d_sq[:, :], d_sq[:, :], ACT.Sqrt, bias=eps[:, :],
                                     scale=1.0 / (2 * HEAD_DIM)).then_inc(dstd_ready, 1)
                for m in range(GM_IN, 16):
                    if m > GM_IN:
                        prepare_behind(l, f"gm{m}")
                    save_gate(l, m)
                wait_saved(act, l, "gm15")
                wait_saved(act, l, "gm14")
                for m in range(KD):
                    for g in (gm(m), gm(8 + m)):
                        last = nc.scalar.activation(g, g, ACT.Sigmoid)
                    last.then_inc(sig_ready, 1)
                for m in range(KD):
                    act.wait_ge(merged_sum, l * KD + m + 1)
                    nc.scalar.activation(merged_hi[:, m, :], merged_raw[:, m, :], ACT.Copy)\
                        .then_inc(merged_high, 1)
                layernorm(l, 0)
                for f in range(KF):
                    if f == 0:
                        act.wait_ge(u_ready, (2 * l + 2) * KD)
                    else:
                        prepare_behind(l, f"fa{f}")
                    if f >= 2:
                        wait_saved(act, l, f"fb{f - 2}")
                    wait_done(act, l, f"fa{f}")
                    nc.scalar.activation(sil[:, f % 2, :], bank_of(l, f"fa{f}"), ACT.Silu)\
                        .then_inc(saved(l, f"fa{f}"), 1)
                    prepare_behind(l, f"fb{f}")
                    wait_saved(act, l, f"fb{f}")
                    nc.scalar.activation(h_hi[:, f, :], h_raw[:, f, :], ACT.Copy).then_inc(h_high, 1)
                layernorm(l, 1)
            for i in range(TT):
                act.wait_ge(out_turned, i + 1)
                nc.scalar.activation(x_tok[:, i, 512:1024], scores[:, 1, :], ACT.Copy).then_inc(out_act, 1)

        @block.vector
        def _(dve):
            V = nc.vector
            count = [0]

            def link(ins):
                count[0] += 1
                ins.then_inc(dve_chain, 1)
                dve.wait_ge(dve_chain, count[0])

            V.memset(ones[:, :], 1.0 / D_MODEL)
            V.memset(eps[:, :], EPS)
            V.memset(hid[:, :, :, :], 0.0)
            V.memset(v_cmp[:, :, :], 0.0)
            dve.wait_ge(const_in, 32)
            V.tensor_copy(ident_b[:, :], ident)
            V.tensor_copy(mask_b[:, :], mask_in[:, :, :].rearrange("p a n -> p (a n)")[:, 0:P + TT * P]).then_inc(setup_done, 1)
            for l in range(DEPTH):
                dve.wait_ge(vec_turned, l + 1)
                link(V.tensor_copy(vec[:, l, :], turned[:, l, 0:V_ROWS]))
                V.tensor_scalar(norm_s[:, l:l + 1], vec[:, l, V_NORM:V_NORM + 1],
                                1.0 - LAMBDA_INIT[l], None, ALU.mult).then_inc(vec_saved, 1)
            lam_v = lam_in.rearrange("p l (a b) d -> p l a b d", b=2)
            for l in range(DEPTH):
                link(V.tensor_tensor(lam_v[:, l, :, 0, :], lam_v[:, l, :, 0, :], lam_v[:, l, :, 1, :], ALU.mult))
                link(V.tensor_reduce(lam_s[:, l, :], lam_v[:, l, :, 0, :], AX.X, ALU.add))
            V.memset(t1[:, 0:1], 0.0).then_inc(lam_summed, 1)
            dve.wait_ge(lam_exp, 1)
            link(V.tensor_tensor(neg_lam[:, :], lam_s[:, :, 1], lam_s[:, :, 0], ALU.subtract))
            link(V.tensor_tensor(neg_lam[:, :], neg_lam[:, :], cst[:, C_LAM:C_LAM + DEPTH], ALU.subtract))
            dve.wait_ge(c_ready, 1)

            def ada_step(l, m):
                n = ada_job(l, m)
                dve.wait_ge(ada_scaled, n + 1)
                if n >= 4:
                    dve.wait_ge(ada_reduced, n - 3)
                V.tensor_reduce(ada_acc[:, n % 4, :], ada_ring[:, n % 2].rearrange("p k n -> p n k"),
                                AX.X, ALU.add).then_inc(ada_summed, 1)

            def ada_part1(l):
                dve.wait_ge(ada_reduced, ada_job(l, ADA1))
                link(V.tensor_tensor(ada[:, l, 0:16], ada_ps[:, 0:16], vec[:, l, 0:16], ALU.add))
                if l == 0:
                    V.tensor_scalar(mul_u[:, 0, :], ada[:, l, 8:16], 1.0, None, ALU.add).then_inc(part1, 1)
                else:
                    link(V.tensor_scalar(ada[:, l, 8:16], ada[:, l, 8:16], 1.0, None, ALU.add))
                    fold(l - 1, V_LN2G, V_LN2B, ada[:, l, 8:16], ada[:, l, 0:8], 0, 1, part1)

            def ada_part2(l):
                dve.wait_ge(ada_reduced, ada_job(l, 48))
                link(V.tensor_tensor(ada[:, l, 16:48], ada_ps[:, 16:48], vec[:, l, 16:48], ALU.add))
                V.tensor_scalar(gate1[:, 0, :], ada[:, l, 16:24], 1.0, None, ALU.add)
                V.tensor_scalar(gate1[:, 1, :], ada[:, l, 40:48], 1.0, None, ALU.add)
                link(V.tensor_scalar(ada[:, l, 32:40], ada[:, l, 32:40], 1.0, None, ALU.add))
                fold(l, V_LN1G, V_LN1B, ada[:, l, 32:40], ada[:, l, 24:32], 1, 0, part2)

            def fold(l, at_g, at_b, scale1, shift, to_u, to_r, signal):
                g, b = vec[:, l, at_g:at_g + KD], vec[:, l, at_b:at_b + KD]
                V.tensor_tensor(mul_u[:, to_u, :], g, scale1, ALU.mult)
                link(V.tensor_tensor(add_u[:, to_u, :], b, scale1, ALU.mult))
                V.tensor_tensor(add_u[:, to_u, :], add_u[:, to_u, :], shift, ALU.add)
                V.tensor_scalar(mul_r[:, to_r, :], g, ALPHA, None, ALU.mult)
                link(V.tensor_scalar(add_r[:, to_r, :], b, ALPHA, None, ALU.mult))
                V.memset(d_mix[:, 0:1], 0.0).then_inc(signal, 1)

            def rope(l, r, src, outs_of):
                shuffle = [i + 8 if i < 8 else i - 8 if i < 16 else i for i in range(32)]
                V.tensor_tensor(t1, src, cos, ALU.mult)
                link(V.stream_shuffle(t2, src, shuffle))
                link(V.tensor_tensor(t2, t2, sin, ALU.mult))
                for dst, rows in outs_of:
                    last = V.tensor_tensor(dst, t1[rows, :], t2[rows, :], ALU.add)
                link(last)
                V.memset(d_mix[:, 1:2], 0.0).then_inc(rope_done, 1)

            def layernorm(l, which):
                n = 2 * l + which
                names = [f"wo{m}" if which == 0 else f"fo{m}" for m in range(KD)]
                last_norm = l == DEPTH - 1 and which == 1
                for m in range(KD):
                    prepare_behind(l, names[m])
                    wait_done(dve, l, names[m])
                    if n >= 1 and m == 0:
                        dve.wait_ge(res_ready, n * KD)
                    V.scalar_tensor_tensor(yT[:, m, :], bank_of(l, names[m]), gate1[:, which, m:m + 1],
                                           res[:, m, :], ALU.mult, ALU.add).then_inc(saved(l, names[m]), 1)
                dve.wait_ge(mean_done, n + 1)
                wait_saved(dve, l, names[6])
                wait_saved(dve, l, names[7])
                for m in range(KD):
                    V.tensor_tensor(yT[:, m, :], yT[:, m, :], mean_ps, ALU.subtract).then_inc(centred, 1)
                if not last_norm:
                    prepare(l + which, "vc" if which else "fb0")
                dve.wait_ge(std_ready, n + 1)
                link(V.reciprocal(t2, t1))
                for m in range(KD + 1):
                    if m < KD:
                        V.tensor_tensor(yT[:, m, :], yT[:, m, :], t2, ALU.mult).then_inc(normed, 1)
                    if m and not last_norm:
                        sub_layer_low(n + 1, m - 1)

            def prepare(l, name):
                n = split_job(l, name)
                src = weights_in(dve, l, name)
                hi, lo = split_slot(l, name)
                dve.wait_ge(split_hi, n + 1)
                V.tensor_tensor(lo, src, hi.bitcast(fp32), ALU.subtract).then_inc(split_lo, 1)

            def prepare_behind(l, name):
                for job in prepared_at(l, name):
                    prepare(*job)

            def sub_layer_low(n, m):
                dve.wait_ge(u_high, n * KD + m + 1)
                if n:
                    dve.wait_ge(res_ready, (n - 1) * KD + m + 1)
                V.tensor_tensor(u_lo[:, m, :], raw[:, m % 2, :], u_hi[:, m, :].bitcast(fp32), ALU.subtract)\
                    .then_inc(u_ready, 1)

            for m in range(ADA1):
                ada_step(0, m)
            ada_part1(0)
            prepare(0, "kc")
            prepare(0, "vc")
            for k in range(KD + 1):
                if k < KD:
                    dve.wait_ge(x_turned, k + 1)
                    V.tensor_scalar(res[:, k, :], scores[:, k % 2, :], ALPHA, None, ALU.mult)\
                        .then_inc(x_saved, 1)
                if k:
                    sub_layer_low(0, k - 1)

            def merged_low(l, m):
                dve.wait_ge(merged_high, l * KD + m + 1)
                V.tensor_tensor(merged_lo[:, m, :], merged_raw[:, m, :], merged_hi[:, m, :].bitcast(fp32),
                                ALU.subtract).then_inc(merged, 1)

            for l in range(DEPTH):
                ada_at = [ADA1]

                def ada_two():
                    for _ in range(2):
                        ada_step(l, ada_at[0])
                        ada_at[0] += 1

                def build_flat(w):
                    at = (V_PEK, V_PEV)[w]
                    for g in range(2):
                        for hi in range(2):
                            src = kc2[:, w, g, 16 * hi:16 * hi + 16 * NC]\
                                .rearrange("p (n j) -> p j n", j=16)[:, 0:16:2, :]
                            pe = vec[:, l, at + 8 * hi:at + 8 * hi + 8].unsqueeze(2).to_broadcast([P, 8, NC])
                            last = V.tensor_tensor(flat[:, w, 8 * hi:8 * hi + 8, NCP * g:NCP * g + NC],
                                                   src, pe, ALU.add)
                    last.then_inc(flat_ready, 1)

                def save_tokens(name):
                    n = TOKEN.index(name)
                    dve.wait_ge(token_turned, l * len(TOKEN) + n + 1)
                    src = turned[:, n % 2, :].rearrange("p (i n) -> p i n", i=TT)
                    if name == "g":
                        src, dst = src[:, :, 0:24], gates[:, :, :, :].rearrange("p i h b -> p i (h b)")
                    elif name[:2] == "vd":
                        dst = vd_tok[:, :, P * int(name[2:]):P * (int(name[2:]) + 1)]
                    else:
                        dst = v_tok[:, :, P * n:P * (n + 1)]
                    V.tensor_copy(dst, src).then_inc(token_saved, 1)

                ada_two()
                wait_saved(dve, l, "kc")
                build_flat(0)
                prepare_behind(l, "vc")
                ada_two()
                wait_done(dve, l, "vc")
                for g in range(2):
                    src = bank_of(l, "vc")[64 * g:64 * g + 64, :]
                    V.tensor_copy(kc2[0:64, 1, g, :], src)
                    last = V.tensor_copy(kc2[64:128, 1, g, 0:SEQ - 1], src[:, 1:SEQ])
                last.then_inc(saved(l, "vc"), 1)
                wait_saved(dve, l, "vc")
                build_flat(1)
                for r, name in enumerate(("ksl", "kwn")):
                    prepare_behind(l, name)
                    ada_two()
                    wait_saved(dve, l, name)
                    rope(l, r, raw[:, r % 2, :],
                         [(k_dup[64 * h:64 * h + 64, r, g, :], slice(64 * g, 64 * g + 64))
                          for g in range(2) for h in range(2)])
                for name in ("vs", "vw", "g"):
                    prepare_behind(l, name)
                    ada_two()
                    if name != "vs":
                        save_tokens(TOKEN[TOKEN.index(name) - 1])
                for i in range(4):
                    prepare_behind(l, f"qn{i}")
                    ada_two()
                    if i == 0:
                        save_tokens("g")
                    wait_saved(dve, l, f"qn{i}")
                    rope(l, 2 + i, q_raw[:, i, :], [(q_rot[:, i, :], slice(0, P))])
                wait_saved(dve, l, "hv")
                V.tensor_copy(
                    hid_rep.rearrange("p m g r n -> p (m g) r n"),
                    hid[:, 1].rearrange("p m (g n) -> p (m g) n", g=2).unsqueeze(2)
                    .to_broadcast([P, 4, 4, NCP])).then_inc(rep_ready, 1)
                wait_done(dve, l, "kv2")
                V.tensor_copy(k_cmpT[:, :], bank_of(l, "kv2")[:, 0:2 * NCP])
                for g in range(2):
                    for r in range(4):
                        last = V.tensor_copy(
                            v_cmp[32 * r:32 * r + 32, g, 64 * r:64 * r + 64],
                            bank_of(l, "kv2")[32 * r:32 * r + 32, 64 + 64 * g:128 + 64 * g])
                last.then_inc(saved(l, "kv2"), 1)
                for a, first, dst in (("kd", 6, kdT), ("qd", 10, qdT)):
                    for i in range(4):
                        prepare_behind(l, f"{a}{i}")
                        if a == "kd" or i == 0:
                            ada_two()
                        wait_saved(dve, l, f"{a}{i}")
                        rope(l, first + i, raw[:, RAW.index(f"{a}{i}") % 2, :], [(dst[:, i, :], slice(0, P))])
                for i in range(4):
                    prepare_behind(l, f"vd{i}")
                    if i:
                        save_tokens(f"vd{i - 1}")
                ada_part2(l)
                save_tokens("vd3")
                dve.wait_ge(gates_ready, l + 1)

                for t in range(len(SEQUENCE) + 2):
                    if 1 <= t <= len(SEQUENCE):
                        for m, k in gate_units(t - 1):
                            if k == 0:
                                prepare_behind(l, f"gm{m}")
                        i, j = SEQUENCE[t - 1]
                        s = score_step(l, i, j)
                        N = (i + 1) * P
                        if j == 0:
                            dve.wait_ge(exp_done, s + 1)
                            V.tensor_reduce(sums[:, i % 2, 0:8],
                                            probs[:, s % 2, 0, 0:256].rearrange("p (h n) -> p h n", n=NCP),
                                            AX.X, ALU.add)
                        elif 9 <= j < STEPS:
                            dve.wait_ge(exp_done, s + 1)
                            hd = j - 9
                            d_sum = sums[:, i % 2, 24 + 2 * hd:26 + 2 * hd]
                            link(V.reciprocal(d_mix[:, 0:1], d_sum[:, 1:2]))
                            link(V.scalar_tensor_tensor(d_mix[:, 0:1], d_mix[:, 0:1], d_sum[:, 0:1],
                                                        neg_lam[:, l:l + 1], ALU.mult, ALU.mult))
                            V.scalar_tensor_tensor(probs[:, s % 2, 0, 0:N], probs[:, s % 2, 1, 0:N],
                                                   d_mix[:, 0:1], probs[:, s % 2, 0, 0:N],
                                                   ALU.mult, ALU.add).then_inc(mix_done, 1)
                    if t < len(SEQUENCE):
                        i, j = SEQUENCE[t]
                        s = score_step(l, i, j)
                        N = (i + 1) * P
                        if j < STEPS:
                            dve.wait_ge(scored, s + 1)
                        if j == 0:
                            if i >= 1:
                                dve.wait_ge(turn_done, turn_step(l, i - 1, STEPS - 2) + 1)
                            src = scores[:, 0:2, 0:4 * NCP].rearrange("p h (c n) -> p h c n", c=4)
                            link(V.tensor_reduce(neg_max[:, s % 2, 0:8].rearrange("p (h c) -> p h c", h=2),
                                                 src, AX.X, ALU.max))
                            for h in range(2):
                                dst = probs[:, s % 2, 0, 0:256]\
                                    .rearrange("p (c h n) -> p h c n", c=4, h=2)[:, h]
                                last = V.tensor_tensor(
                                    dst, src[:, h],
                                    neg_max[:, s % 2, 4 * h:4 * h + 4].unsqueeze(2).to_broadcast([P, 4, NCP]),
                                    ALU.subtract)
                            last.then_inc(max_done, 1)
                        elif j < STEPS:
                            V.tensor_reduce(neg_max[:, s % 2, 0:2], scores[:, 0:2, 0:N], AX.X, ALU.max,
                                            negate=True).then_inc(max_done, 1)
                    if 1 <= t <= len(SEQUENCE):
                        i, j = SEQUENCE[t - 1]
                        s = score_step(l, i, j)
                        N = (i + 1) * P
                        if j <= 8:
                            dve.wait_ge(turn_done, turn_step(l, i, j) + 1)
                            if s >= 2:
                                dve.wait_ge(pv_done, s - 1)
                            h, n = (0, 256) if j == 0 else (1, N)
                            V.tensor_copy(probsT[:, s % 2, h, 0:n], turned[:, h, 0:n]).then_inc(turn_dve, 1)
                    if t >= 2:
                        i, j = SEQUENCE[t - 2]
                        if j in (0, 4, 8, 12):
                            b = j // 4
                            q = out_bank(l, i, j)
                            bank = outs[:, q % 2, :]
                            dve.wait_ge(out_done, q + 1)
                            if b < 3:
                                link(V.reciprocal(coef[:, 0, :], sums[:, i % 2, 8 * b:8 * b + 8]))
                                if b == 0 and i == 0:
                                    link(V.tensor_scalar(coef[:, 0, :], coef[:, 0, :], cst[:, C_ANY:C_ANY + 1],
                                                         None, ALU.mult))
                                link(V.tensor_tensor(coef[:, 0, :], coef[:, 0, :], gates[:, i, :, b], ALU.mult))
                                dst = o_nsa if b == 0 else t1
                                if b == 0 and i >= 1:
                                    dve.wait_ge(turn_done, turn_step(l, i - 1, STEPS) + 1)
                                link(V.tensor_tensor(
                                    dst[:, :].rearrange("p (h d) -> p h d", d=HEAD_DIM),
                                    bank.rearrange("p (h d) -> p h d", d=HEAD_DIM),
                                    coef[:, 0, :].unsqueeze(2).to_broadcast([P, 8, HEAD_DIM]), ALU.mult))
                                V.memset(d_mix[:, 1:2], 0.0).then_inc(out_saved, 1)
                                if b:
                                    ins = V.tensor_tensor(o_nsa[:, :], o_nsa[:, :], t1, ALU.add)
                                    if b == 2:
                                        ins.then_inc(nsa_ready, 1)
                                    else:
                                        link(ins)
                            else:
                                d_sum = sums[:, i % 2, 24:32].rearrange("p (h m) -> p h m", m=2)
                                link(V.reciprocal(d_rs[:, 0, :], d_sum[:, :, 0]))
                                od = q_raw[:, :, i * P:(i + 1) * P]
                                link(V.tensor_tensor(od, bank.rearrange("p (h e) -> p h e", h=4),
                                                     d_rs[:, 0, :].unsqueeze(2).to_broadcast([P, 4, P]),
                                                     ALU.mult))
                                V.memset(d_mix[:, 1:2], 0.0).then_inc(out_saved, 1)
                                sq = t2.rearrange("p (h e) -> p h e", h=4)
                                link(V.tensor_tensor(sq, od, od, ALU.mult))
                                ins = V.tensor_reduce(d_sq[:, 4 * i:4 * i + 4], sq, AX.X, ALU.add)
                                if i == TT - 1:
                                    ins.then_inc(dsq_ready, 1)
                                else:
                                    link(ins)

                prepare_behind(l, f"gm{GM_IN}")
                dve.wait_ge(dstd_ready, l + 1)
                link(V.reciprocal(d_sq[:, :], d_sq[:, :]))
                for i in range(TT):
                    od = q_raw[:, :, i * P:(i + 1) * P]
                    V.tensor_tensor(od, od, d_sq[:, 4 * i:4 * i + 4].unsqueeze(2).to_broadcast([P, 4, P]),
                                    ALU.mult).then_inc(dnorm_ready, 1)
                for m in range(GM_IN + 1, 16):
                    prepare_behind(l, f"gm{m}")
                for i in range(TT):
                    dve.wait_ge(turn_done, turn_step(l, TT, i) + 1)
                    V.tensor_scalar(q_raw[:, :, i * P:(i + 1) * P],
                                    turned[:, i % 2, :].rearrange("p (h t) -> p h t", h=4),
                                    norm_s[:, l:l + 1], None, ALU.mult).then_inc(turn_dve, 1)
                for m in range(KD):
                    dve.wait_ge(sig_ready, l * KD + m + 1)
                    wait_done(dve, l, f"yn{m}")
                    if m:
                        dve.wait_ge(merged_sum, l * KD + m)
                    V.tensor_tensor(t1, bank_of(l, f"yn{m}"), gm(m), ALU.mult).then_inc(saved(l, f"yn{m}"), 1)
                    wait_done(dve, l, f"yd{m}")
                    V.tensor_tensor(t2, bank_of(l, f"yd{m}"), gm(8 + m), ALU.mult)\
                        .then_inc(saved(l, f"yd{m}"), 1)
                    wait_saved(dve, l, f"yn{m}")
                    wait_saved(dve, l, f"yd{m}")
                    V.tensor_tensor(merged_raw[:, m, :], t1, t2, ALU.add).then_inc(merged_sum, 1)
                    if m:
                        merged_low(l, m - 1)
                merged_low(l, KD - 1)
                layernorm(l, 0)
                for f in range(KF + 1):
                    if f < KF:
                        if f:
                            prepare_behind(l, f"fa{f}")
                        prepare_behind(l, f"fb{f}")
                        wait_done(dve, l, f"fb{f}")
                        wait_saved(dve, l, f"fa{f}")
                        V.tensor_tensor(h_raw[:, f, :], bank_of(l, f"fb{f}"), sil[:, f % 2, :], ALU.mult)\
                            .then_inc(saved(l, f"fb{f}"), 1)
                        if l + 1 < DEPTH and f < ADA1:
                            ada_step(l + 1, f)
                    if f:
                        dve.wait_ge(h_high, l * KF + f)
                        V.tensor_tensor(h_lo[:, f - 1, :], h_raw[:, f - 1, :],
                                        h_hi[:, f - 1, :].bitcast(fp32), ALU.subtract).then_inc(h_ready, 1)
                if l + 1 < DEPTH:
                    ada_part1(l + 1)
                else:
                    V.tensor_copy(mul_u[:, 0, :], vec[:, l, V_LN2G:V_LN2G + KD])
                    link(V.tensor_copy(add_u[:, 0, :], vec[:, l, V_LN2B:V_LN2B + KD]))
                    V.memset(d_mix[:, 0:1], 0.0).then_inc(part1, 1)
                layernorm(l, 1)
            for i in range(TT):
                dve.wait_ge(out_turned, i + 1)
                V.tensor_copy(x_tok[:, i, 0:512], scores[:, 0, :]).then_inc(out_dve, 1)

        @block.tensor
        def _(pe):
            M = nc.tensor.matmul

            pe.wait_ge(const_in, 32)
            pe.wait_ge(vec_in, 16 * 13 * DEPTH)
            for l in range(DEPTH):
                nc.tensor.transpose(turned[:, l, 0:V_ROWS], vec_rows[:, l, :], ident[0:V_ROWS, 0:V_ROWS])\
                    .then_inc(vec_turned, 1)
            pe.wait_ge(setup_done, 1)

            def reduce_ada(l, m):
                n = ada_job(l, m)
                pe.wait_ge(ada_summed, n + 1)
                M(ada_ps[:, m:m + 1], ada_acc[:, n % 4, :], one_col, start=True, stop=True)\
                    .then_inc(ada_reduced, 1)

            one_col = cst[:, C_ANY + 1:C_ANY + 2]
            for m in range(ADA1):
                reduce_ada(0, m)
            pe.wait_ge(x_in, 16)
            for k in range(KD):
                if k >= 2:
                    pe.wait_ge(u_ready, k - 1)
                for i in range(TT):
                    last = nc.tensor.transpose(scores[:, k % 2, i * P:(i + 1) * P],
                                               x_tok[:, i, k * P:(k + 1) * P], ident)
                last.then_inc(x_turned, 1)

            def take_bank(l, name):
                n = chunk(l, name)
                if n >= 2:
                    pe.wait_ge(chunk_saved[n % 2], n // 2)
                return proj[:, n % 2, :]

            def take_split(l, name):
                pe.wait_ge(split_lo, split_job(l, name) + 1)
                return split_slot(l, name)

            def product(bank, w, src, k, at, start, stop):
                (wh, wl), (sh, sl) = w, src
                block = slice(at * P, (at + 1) * P)
                M(bank, wh[:, block], sh[:, k, :], start=start, stop=False)
                M(bank, wh[:, block], sl[:, k, :], start=False, stop=False)
                return M(bank, wl[:, block], sh[:, k, :], start=False, stop=stop)

            def done(l, name, ins):
                ins.then_inc(chunk_done[chunk(l, name) % 2], 1)

            def project(l, name, src=(u_hi, u_lo)):
                w = take_split(l, name)
                bank = take_bank(l, name)
                for k in range(KD):
                    last = product(bank, w, src, k, k, k == 0, k == KD - 1)
                done(l, name, last)

            def project_first(l, names, n):
                w = [take_split(l, name) for name in names]
                out = [take_bank(l, name) for name in names]
                for k in range(KD):
                    pe.wait_ge(u_ready, n * KD + k + 1)
                    for i, name in enumerate(names):
                        last = product(out[i], w[i], (u_hi, u_lo), k, k, k == 0, k == KD - 1)
                        if k == KD - 1:
                            done(l, name, last)

            def turn_tokens(l, name):
                n, r = TOKEN.index(name), RAW.index(name)
                wait_saved(pe, l, name)
                if n >= 2:
                    pe.wait_ge(token_saved, l * len(TOKEN) + n - 1)
                for i in range(TT):
                    last = nc.tensor.transpose(turned[:, n % 2, i * P:(i + 1) * P],
                                               raw[:, r % 2, i * P:(i + 1) * P], ident)
                last.then_inc(token_turned, 1)

            def score(l, i, j):
                s = score_step(l, i, j)
                if s >= 1:
                    pe.wait_ge(exp_done, s)
                tile = slice(i * P, (i + 1) * P)
                if j == 0:
                    for h in range(2):
                        M(scores[:, h, 0:P], ident_b[:, :], mask_b[:, P + i * P:2 * P + i * P],
                          start=True, stop=True)
                    for c in range(4):
                        for h in range(2):
                            rows = slice(64 * h, 64 * h + 64)
                            last = M(scores[:, h, NCP * c:NCP * (c + 1)], q_raw[rows, c, tile],
                                     k_cmpT[rows, NCP * (c // 2):NCP * (c // 2 + 1)],
                                     start=False, stop=True, skip_group_check=True)
                    last.then_inc(scored, 1)
                    return
                N = (i + 1) * P
                for h in range(2):
                    rows = slice(64 * h, 64 * h + 64)
                    if j <= 8:
                        c = (j - 1) % 4
                        q, k = q_rot[rows, c, tile], k_dup[rows, (j - 1) // 4, c // 2, 0:N]
                    else:
                        q, k = qdT[rows, j - 9, tile], kdT[rows, j - 9, 0:N]
                    M(scores[:, h, 0:N], q, k, start=True, stop=True)
                for h in range(2):
                    last = M(scores[:, h, i * P:N], ident_b[:, :], mask_b[:, 0:P], start=False, stop=True,
                             skip_group_check=True)
                last.then_inc(scored, 1)

            def free_turned(l, i, j):
                if (i, j) == (0, 0):
                    if l:
                        pe.wait_ge(turn_dve, turned_by_dve(l, 0, -1))
                    return
                if j == 0:
                    i, j = i - 1, STEPS + 1
                pe.wait_ge(turn_act, turned_by_act(l, i, j - 1))
                pe.wait_ge(turn_dve, turned_by_dve(l, i, j - 1))

            def turn(l, i, j):
                s = score_step(l, i, j)
                free_turned(l, i, j)
                if j < STEPS:
                    pe.wait_ge(exp_done, s + 1)
                if 9 <= j < STEPS:
                    pe.wait_ge(mix_done, (l * TT + i) * 4 + j - 8)
                if j == STEPS:
                    pe.wait_ge(nsa_ready, l * TT + i + 1)
                    blocks = [(0, c, o_nsa[:, c * P:(c + 1) * P]) for c in range(4)]
                elif j == 0:
                    blocks = [(0, g, probs[:, s % 2, 0, g * P:(g + 1) * P]) for g in range(2)]
                else:
                    blocks = [(h, b, probs[:, s % 2, h, b * P:(b + 1) * P])
                              for h in range(2 if j <= 8 else 1) for b in range(i + 1)]
                for h, b, src in blocks:
                    last = nc.tensor.transpose(turned[:, h, b * P:(b + 1) * P], src, ident)
                last.then_inc(turn_done, 1)

            def values(l, i, j):
                s = score_step(l, i, j)
                q = out_bank(l, i, j)
                bank = outs[:, q % 2, :]
                if j in (0, 1, 5, 9) and q >= 2:
                    pe.wait_ge(out_saved, q - 1)
                if j <= 8:
                    pe.wait_ge(turn_dve, turned_by_dve(l, i, j))
                if j >= 1:
                    pe.wait_ge(turn_act, turned_by_act(l, i, j))
                if j == 0:
                    for g in range(2):
                        last = M(bank[:, 256 * g:256 * (g + 1)], probsT[:, s % 2, 0, g * P:(g + 1) * P],
                                 v_cmp[:, g, :], start=True, stop=True)
                elif j <= 8:
                    br, c = (j - 1) // 4, (j - 1) % 4
                    for h in range(2):
                        head = 2 * c + h
                        v = slice(128 * br + 64 * (c // 2), 128 * br + 64 * (c // 2) + 64)
                        for b in range(i + 1):
                            last = M(bank[:, 64 * head:64 * head + 64], probsT[:, s % 2, h, b * P:(b + 1) * P],
                                     v_tok[:, b, v], start=b == 0, stop=b == i)
                else:
                    hd = j - 9
                    for b in range(i + 1):
                        last = M(bank[:, P * hd:P * (hd + 1)], probsT[:, s % 2, 0, b * P:(b + 1) * P],
                                 vd_tok[:, b, P * hd:P * (hd + 1)], start=b == 0, stop=b == i)
                if j in (0, 4, 8, 12):
                    last.then_inc(out_done, 1)
                    pe.wait_ge(out_done, q + 1)
                    pe.sem_inc(pv_done, 1)
                else:
                    last.then_inc(pv_done, 1)

            def merge_gate(l, m, k):
                name = f"gm{m}"
                if k == 0:
                    take_split(l, name)
                    take_bank(l, name)
                ins = product(bank_of(l, name), split_slot(l, name), (u_hi, u_lo), k, k, k == 0, k == KD - 1)
                if k == KD - 1:
                    done(l, name, ins)

            def mean_step(l, which, m):
                wait_saved(pe, l, f"wo{m}" if which == 0 else f"fo{m}")
                ins = M(mean_ps, ones[:, :], yT[:, m, :], start=m == 0, stop=m == KD - 1)
                if m == KD - 1:
                    ins.then_inc(mean_done, 1)

            def variance(l, which):
                n = 2 * l + which
                for m in range(KD):
                    pe.wait_ge(squared, n * KD + m + 1)
                    ins = M(var_ps, ones[:, :], squares[:, m, :], start=m == 0, stop=m == KD - 1)
                ins.then_inc(var_done, 1)

            for l in range(DEPTH):
                ada_at = [ADA1]

                def reduce_two():
                    for _ in range(2):
                        if ada_at[0] < 48:
                            reduce_ada(l, ada_at[0])
                            ada_at[0] += 1

                project_first(l, ("kc", "vc"), 2 * l)
                project(l, "ksl")
                reduce_two()
                project(l, "kwn")
                reduce_two()
                for name in ("vs", "vw", "g"):
                    project(l, name)
                    reduce_two()
                    if name != "vs":
                        turn_tokens(l, TOKEN[TOKEN.index(name) - 1])
                for i in range(4):
                    project(l, f"qn{i}")
                    reduce_two()
                    if i == 0:
                        turn_tokens(l, "g")
                for w, name in enumerate(("hk", "hv")):
                    bank = take_bank(l, name)
                    pe.wait_ge(flat_ready, 2 * l + w + 1)
                    for m in range(2):
                        dst = bank[:, 2 * NCP * m:2 * NCP * (m + 1)].rearrange("p (g n) -> p g n", g=2)[:, :, 0:NC]
                        for j in range(KJ):
                            if j % KD == 0:
                                slot = weights_in(pe, l, f"w1{name[1]}{2 * m + j // KD}")
                            last = M(dst, slot[:, (j % KD) * P:(j % KD + 1) * P],
                                     flat[:, w, j, :].rearrange("p (g n) -> p g n", g=2)[:, :, 0:NC],
                                     start=j == 0, stop=j == KJ - 1)
                            if j % KD == KD - 1 and (m, j) != (1, KJ - 1):
                                last.then_inc(w1_read, 1)
                    done(l, name, last)
                    reduce_two()
                bank = take_bank(l, "kv2")
                wait_saved(pe, l, "hk")
                for m in range(2):
                    M(bank[:, 0:2 * NCP], w2k[:, l, m].rearrange("p a d -> p (a d)"), hid[:, 0, m, :],
                      start=m == 0, stop=m == 1)
                pe.wait_ge(rep_ready, l + 1)
                for g in range(2):
                    for m in range(2):
                        last = M(bank[:, 64 + 64 * g:128 + 64 * g],
                                 hid_rep[:, m, g].rearrange("p r n -> p (r n)"), w2v[:, l, m, :],
                                 start=m == 0, stop=m == 1)
                done(l, "kv2", last)
                for name in [f"{a}{i}" for a in ("kd", "qd") for i in range(4)]:
                    project(l, name)
                    reduce_two()
                for i in range(4):
                    project(l, f"vd{i}")
                    if i:
                        turn_tokens(l, f"vd{i - 1}")
                first_gates = gate_units(0)
                for m, k in first_gates:
                    merge_gate(l, m, k)
                turn_tokens(l, "vd3")

                pe.wait_ge(rope_done, 14 * (l + 1))
                wait_saved(pe, l, "kv2")
                pe.wait_ge(token_saved, len(TOKEN) * (l + 1))
                pe.wait_ge(part2, l + 1)
                for t in range(len(SEQUENCE) + 2):
                    if t < len(SEQUENCE) and SEQUENCE[t][1] < STEPS:
                        score(l, *SEQUENCE[t])
                    units = gate_units(t) if 0 < t < len(SEQUENCE) else []
                    for m, k in units[:1]:
                        merge_gate(l, m, k)
                    if 1 <= t <= len(SEQUENCE):
                        turn(l, *SEQUENCE[t - 1])
                    for m, k in units[1:]:
                        merge_gate(l, m, k)
                    if t >= 2 and SEQUENCE[t - 2][1] < STEPS:
                        values(l, *SEQUENCE[t - 2])
                for n in range(GM_IN * KD, 16 * KD):
                    merge_gate(l, *divmod(n, KD))
                pe.wait_ge(turn_act, turned_by_act(l, TT - 1, STEPS))
                for i in range(TT):
                    pe.wait_ge(dnorm_ready, l * TT + i + 1)
                    if i >= 2:
                        pe.wait_ge(turn_dve, turned_by_dve(l, TT, -1) + i - 1)
                    for c in range(4):
                        last = nc.tensor.transpose(turned[:, i % 2, c * P:(c + 1) * P],
                                                   q_raw[:, c, i * P:(i + 1) * P], ident)
                    last.then_inc(turn_done, 1)
                pe.wait_ge(turn_dve, turned_by_dve(l, TT, -1) + TT)
                for m in range(KD):
                    w = weights_in(pe, l, f"br{m}")
                    for h, (a, src) in enumerate((("n", q_rot), ("d", q_raw))):
                        bank = take_bank(l, f"y{a}{m}")
                        for k in range(4):
                            last = M(bank, w[:, (4 * h + k) * P:(4 * h + k + 1) * P], src[:, k, :],
                                     start=k == 0, stop=k == 3)
                        done(l, f"y{a}{m}", last)
                pe.wait_ge(merged, KD * (l + 1))
                for m in range(KD):
                    project(l, f"wo{m}", (merged_hi, merged_lo))
                    if m:
                        mean_step(l, 0, m - 1)
                mean_step(l, 0, KD - 1)
                variance(l, 0)
                for f in range(KF):
                    if f == 0:
                        project_first(l, ("fa0", "fb0"), 2 * l + 1)
                    else:
                        project(l, f"fa{f}")
                        project(l, f"fb{f}")
                    if l + 1 < DEPTH and 1 <= f <= ADA1:
                        reduce_ada(l + 1, f - 1)
                for m in range(KD):
                    bank = take_bank(l, f"fo{m}")
                    for half in range(2):
                        w = take_split(l, f"fo{2 * m + half}")
                        for k in range(KH):
                            if m == 0:
                                pe.wait_ge(h_ready, l * KF + half * KH + k + 1)
                            last = product(bank, w, (h_hi, h_lo), half * KH + k, k,
                                           half + k == 0, half == 1 and k == KH - 1)
                        if half == 0:
                            last.then_inc(half_read, 1)
                    done(l, f"fo{m}", last)
                    if m:
                        mean_step(l, 1, m - 1)
                mean_step(l, 1, KD - 1)
                variance(l, 1)
            pe.wait_ge(u_high, (2 * DEPTH + 1) * KD)
            for i in range(TT):
                if i >= 1:
                    pe.wait_ge(out_dve, i)
                    pe.wait_ge(out_act, i)
                for k in range(KD):
                    last = nc.tensor.transpose(scores[:, k // 4, (k % 4) * P:(k % 4 + 1) * P],
                                               res[:, k, i * P:(i + 1) * P], ident)
                last.then_inc(out_turned, 1)


def constants():
    c = np.zeros((P, C_COLS), np.float32)
    rot = HEAD_DIM // ROPE_FRACTION
    half = rot // 2
    inv = np.float32(ROPE_THETA) ** (-np.arange(half, dtype=np.float32) * np.float32(2.0) / np.float32(rot))
    ang = (np.arange(SEQ, dtype=np.float32)[:, None] * inv.astype(np.float32)[None, :]).T
    c[:, C_COS:C_COS + SEQ] = 1.0
    for base in (0, 64):
        c[base:base + half, C_COS:C_COS + SEQ] = np.cos(ang)
        c[base + half:base + rot, C_COS:C_COS + SEQ] = np.cos(ang)
        c[base:base + half, C_SIN:C_SIN + SEQ] = -np.sin(ang)
        c[base + half:base + rot, C_SIN:C_SIN + SEQ] = np.sin(ang)
    c[:, C_ID:C_ID + P] = np.eye(P)
    q = np.arange(P)
    c[:, C_MASKS:C_MASKS + P] = np.where(q[None, :] <= q[:, None], 0.0, NEG_INF)
    ends = np.arange(NCP) * CMP_STRIDE + CMP_BLOCK - 1
    for i in range(TT):
        m = np.where(ends[None, :] <= (i * P + q)[:, None], 0.0, NEG_INF)
        c[:, C_MASKS + (i + 1) * P:C_MASKS + (i + 2) * P] = np.tile(m, (1, 4))
    c[:, C_ANY] = (q >= CMP_BLOCK - 1)
    c[:, C_ANY + 1] = 1.0
    c[:, C_LAM:C_LAM + DEPTH] = np.array(LAMBDA_INIT)[None, :]
    return c


_INS = ["x", "w_ada", "b_ada", "c", "w_in", "cmp_pe_k", "cmp_w1_k", "cmp_w2_k", "cmp_pe_v", "cmp_w1_v",
        "cmp_w2_v", "diff_lambda", "diff_norm_g", "w_branch_nsa", "w_branch_diff", "w_out", "ln1_g",
        "ln1_b", "w_ffn_in", "w_ffn_out", "ln2_g", "ln2_b"]


def kernel(**inputs):
    import numpy as _np
    import concourse.bacc as _bacc
    from concourse import mybir as _mybir
    from concourse.bass_utils import run_bass_kernel_spmd as _run

    nc = _bacc.Bacc("TRN2", target_bir_lowering=False, num_devices=1)
    arrays, args = {}, []
    for name in _INS + ["consts"]:
        a = _np.ascontiguousarray(inputs[name]) if name != "consts" else constants()
        arrays[f"in_{name}_dram"] = a
        args.append(nc.dram_tensor(f"in_{name}_dram", a.shape, _mybir.dt.from_np(a.dtype),
                                   kind="ExternalInput").ap())
    args.append(nc.dram_tensor("out_0_dram", (1, SEQ, D_MODEL), _mybir.dt.float32,
                               kind="ExternalOutput").ap())
    build(nc, *args)
    r = _run(nc, [arrays], core_ids=[0])
    return r.results[0]["out_0_dram"]
```

```python
import math
from contextlib import ExitStack

import numpy as np

import concourse.bass as bass
from concourse import mybir

D_MODEL, SEQ, DEPTH = 1024, 512, 2
HEAD_DIM, NSA_HEADS, DIFF_HEADS = 64, 8, 4
NSA_WIDTH, NSA_KV_WIDTH = 512, 128
CMP_BLOCK, CMP_STRIDE, CMP_HIDDEN = 32, 16, 256
D_FF = -(-8 * D_MODEL // (3 * 256)) * 256
ROPE_THETA, ROPE_FRACTION = 500000.0, 4
ALPHA = (2 * DEPTH) ** 0.25
EPS = 1e-5
NEG_INF = -1e30
IN_SIZES = dict(q_n=512, kc=128, vc=128, ksl=128, vsl=128, kwn=128, vwn=128, g_n=24,
                q_d=512, k_d=512, v_d=512, g_m=2048)
IN_AT = dict(zip(IN_SIZES, np.cumsum([0] + list(IN_SIZES.values()))[:-1].tolist()))
LAMBDA_INIT = [0.8 - 0.6 * math.exp(-0.3 * l) for l in range(DEPTH)]

P = 128
TT = SEQ // P
KD = D_MODEL // P
KF = D_FF // P
NC = (SEQ - CMP_BLOCK) // CMP_STRIDE + 1
NCP = 32
KJ = CMP_BLOCK * HEAD_DIM // P

V_ADA, V_LN1G, V_LN1B, V_LN2G, V_LN2B, V_NORM, V_PEK, V_PEV, V_ROWS = 0, 48, 56, 64, 72, 80, 81, 97, 113

C_COS, C_SIN, C_ID, C_ANY, C_LAM = 0, 512, 1024, 1152, 1154
C_MASKS = C_LAM + DEPTH
C_COLS = C_MASKS + P + TT * P

GM_IN = 12
TOKEN = ["vs", "vw", "g"] + [f"vd{i}" for i in range(4)]
CHUNKS = (["kc", "vc", "ksl", "kwn", "vs", "vw", "g"] + [f"qn{i}" for i in range(4)]
          + ["hk", "hv", "kv2"] + [f"kd{i}" for i in range(4)] + [f"qd{i}" for i in range(4)]
          + [f"vd{i}" for i in range(4)] + [f"gm{i}" for i in range(16)]
          + [f"y{a}{i}" for i in range(KD) for a in "nd"] + [f"wo{i}" for i in range(KD)]
          + [f"f{a}{i}" for i in range(KF) for a in "ab"] + [f"fo{i}" for i in range(KD)])
ADA_BEFORE = {"qn1": 2, "kd1": 3, "vd1": 4, f"gm{GM_IN}": 5, "fa10": 0, "fa20": 1}


def ada_before(l, name):
    j = ADA_BEFORE.get(name)
    if j is None or (j < 2 and l + 1 == DEPTH):
        return None
    return (l + 1 if j < 2 else l, j)


def chunk_order():
    order = [(0, "ada01")]
    for l in range(DEPTH):
        for name in CHUNKS:
            if ada_before(l, name):
                group_l, j = ada_before(l, name)
                order.append((group_l, f"ada{j}"))
            order.append((l, name))
    return {key: i for i, key in enumerate(order)}


CHUNK_AT = chunk_order()
W_IN_AT = {"kc": IN_AT["kc"], "vc": IN_AT["vc"], "ksl": IN_AT["ksl"], "kwn": IN_AT["kwn"],
           "vs": IN_AT["vsl"], "vw": IN_AT["vwn"], "g": IN_AT["g_n"]}
for _a, _n, _k in (("qn", "q_n", 4), ("kd", "k_d", 4), ("qd", "q_d", 4), ("vd", "v_d", 4), ("gm", "g_m", 16)):
    W_IN_AT.update({f"{_a}{i}": IN_AT[_n] + P * i for i in range(_k)})


def chunk(l, name):
    return CHUNK_AT[l, name]


FO_PARTS = -(-KF // KD)
FO_AT = [KF * i // FO_PARTS for i in range(FO_PARTS + 1)]

JOBS = (["kc", "vc", "ksl", "kwn", "vs", "vw", "g"] + [f"qn{i}" for i in range(4)]
        + ["kd0", "kd1"] + [f"w1{a}{i}" for a in "kv" for i in range(4)]
        + [f"{a}{i}" for a in ("kd", "qd", "vd") for i in range(4)][2:]
        + [f"gm{i}" for i in range(16)] + [f"br{i}" for i in range(KD)] + [f"wo{i}" for i in range(KD)]
        + [f"f{a}{i}" for i in range(KF) for a in "ab"] + [f"fo{i}" for i in range(FO_PARTS * KD)])
JOB_AT = {name: i for i, name in enumerate(JOBS)}
SPLIT = [name for name in JOBS if name[:2] != "w1"]
SPLIT_AT = {name: i for i, name in enumerate(SPLIT)}
NS = 2
NQ = 3
SLOT = KD * P


def ready_counts():
    total, out = [0] * NS, []
    for g in range(DEPTH * len(JOBS)):
        total[g % NS] += 32 if JOBS[g % len(JOBS)][:2] == "br" else 16
        out.append(total[g % NS])
    return out


READY = ready_counts()


def split_job(l, name):
    return l * len(SPLIT) + SPLIT_AT[name]


def reader(name):
    return (f"fo{int(name[2:]) // FO_PARTS}" if name[:2] == "fo"
            else f"yd{name[2:]}" if name[:2] == "br" else name)


def blocks_of(name):
    part = int(name[2:]) % FO_PARTS if name[:2] == "fo" else None
    return KD if part is None else FO_AT[part + 1] - FO_AT[part]


FIRST_SPLIT = ("fa1", "ksl")


def prepared_at(l, name):
    out = []
    for i, job in enumerate(SPLIT):
        if reader(job) == name:
            nl, ni = divmod(l * len(SPLIT) + i + NQ - 1, len(SPLIT))
            if nl < DEPTH and SPLIT[ni] not in FIRST_SPLIT:
                out.append((nl, SPLIT[ni]))
    return out


RAW = ["ksl", "kwn", "vs", "vw", "g"] + [f"{a}{i}" for a in ("kd", "qd", "vd") for i in range(4)]
ROPE = ["ksl", "kwn"] + [f"{a}{i}" for a in ("qn", "kd", "qd") for i in range(4)]


def gate_units(t):
    n, steps = GM_IN * KD, TT * (STEPS + 1)
    return [divmod(u, KD) for u in range(n * t // steps, n * (t + 1) // steps)]


ADA_GROUPS = [(0, j) for j in range(2, 6)] + [(l, j) for l in range(1, DEPTH) for j in range(6)]
FIRST_DVE, FIRST_PE = (0, 2, 3, 5, 6, 7), (1, 4)
ROW_LOADS, VEC_LOADS = 8 * DEPTH, 4 * DEPTH
NA = 2


STEPS = 13
SEQUENCE = [(i, j) for i in range(TT) for j in range(STEPS + 1)]


def score_step(l, i, j):
    return (l * TT + i) * STEPS + j


def turn_step(l, i, j):
    return l * (TT * (STEPS + 1) + TT) + i * (STEPS + 1) + j


def turned_by_act(l, i, j):
    return (l * TT + i) * STEPS + j


def turned_by_dve(l, i, j):
    return l * (9 * TT + TT) + 9 * i + min(j + 1, 9)


def out_bank(l, i, j):
    return (l * TT + i) * 4 + (0 if j == 0 else (j - 1) // 4 + 1)


def build(nc, x, w_ada, b_ada, c, w_in, pe_k, w1_k, w2_k, pe_v, w1_v, w2_v, lam, norm_g,
          w_bn, w_bd, w_o, ln1_g, ln1_b, w_f1, w_f2, ln2_g, ln2_b, consts, out):
    fp32, fp32r, bf16 = mybir.dt.float32, mybir.dt.float32r, mybir.dt.bfloat16
    ALU, ACT, AX = mybir.AluOpType, mybir.ActivationFunctionType, mybir.AxisListType

    ctx = ExitStack()
    with ctx:
        def sb(name, shape, dt=fp32):
            return ctx.enter_context(nc.sbuf_tensor(name, shape, dt))

        def sem(name):
            return ctx.enter_context(nc.semaphore(name))

        ring = sb("ring", [P, NS, SLOT])
        w_hi = sb("w_hi", [P, NQ, SLOT], fp32r)
        w_lo = sb("w_lo", [P, NQ, SLOT], fp32r)
        ada_ring = sb("ada_ring", [P, NA, D_MODEL])
        res = sb("res", [P, KD, SEQ])
        arena_at = -(-nc.sbuf_base // 32) * 32
        sb("arena", [P, 62 * SEQ])

        def at(name, first, n, dt=fp32):
            return nc.alloc_sbuf_tensor_at(name, [P, n, SEQ], dt, offset=arena_at + 4 * SEQ * first)

        gm_all = at("gm", 0, GM_IN)
        q_raw = at("q_raw", 12, 4)
        q_rot = at("q_rot", 16, 4)
        probs_all = at("probs", 20, 4)
        probsT_all = at("probsT", 24, 4)
        qdT = at("qdT", 28, 4)
        kdT = at("kdT", 32, 4)
        k_dup_all = at("k_dup", 36, 4)
        gm_late = at("gm_late", 36, 4)
        vd_all = at("vd_tok", 40, 4)
        v_all = at("v_tok", 44, 2)
        kc2_all = at("kc2", 0, 4)
        flat_all = at("flat", 4, 4)
        hid_rep_all = at("hid_rep", 8, 1)
        cmp_raw = at("cmp_raw", 9, 2)
        merged_hi = at("merged_hi", 20, KD, fp32r)
        merged_lo = at("merged_lo", 28, KD, fp32r)
        merged_raw = at("merged_raw", 28, KD)
        h_hi = at("h_hi", 0, KF, fp32r)
        h_lo = at("h_lo", KF, KF, fp32r)
        h_raw = at("h_raw", KF, KF)
        u_hi = at("u_hi", 46, KD, fp32r)
        u_lo = at("u_lo", 46 + KD, KD, fp32r)
        mix_hi = at("mix_hi", 46, KD, fp32r)
        mix_lo = at("mix_lo", 46 + KD, KD, fp32r)
        squares = at("squares", 46, KD)
        yT = at("yT", 46 + KD, KD)
        x_all = at("x_tok", 28, KD)
        mask_in = at("mask_in", 20, 2)
        vec_in_all = at("vec_rows", 22, 1)
        lam_in_all = at("lam_in", 23, 1)
        c_in_all = at("c_in", 48, 1)
        ada_first_a = at("ada_first_a", 0, 20)
        ada_first_b = at("ada_first_b", 36, 12)
        ada_first_sum = at("ada_first_sum", 24, 4)
        probs = probs_all[:, :, :].rearrange("p (r h) k -> p r h k", r=2)
        probsT = probsT_all[:, :, :].rearrange("p (r h) k -> p r h k", r=2)
        k_dup = k_dup_all[:, :, :].rearrange("p (b g) t -> p b g t", b=2)
        vd_tok = vd_all[:, :, :]
        v_tok = v_all[:, :, :].rearrange("p a (i n) -> p (a i) n", n=256)
        kc2 = kc2_all[:, :, :].rearrange("p (w g) t -> p w g t", w=2)
        flat = flat_all[:, :, :].rearrange("p (w a) (b n) -> p w (a b) n", w=2, n=2 * NCP)
        hid_rep = hid_rep_all[:, 0, :].rearrange("p (m g r n) -> p m g r n", m=2, g=2, r=4)
        x_tok = x_all[:, :, :].rearrange("p (i a) n -> p i (a n)", a=2)
        ada_first = [a[:, 4 * k:4 * k + 4, :].rearrange("p a n -> p (a n)")
                     for a, n in ((ada_first_a, 5), (ada_first_b, 3)) for k in range(n)]
        first_sum = ada_first_sum[:, :, :].rearrange("p a n -> p (a n)")
        c_rows = c_in_all[0:KD, 0, 0:P]
        vec_rows = vec_in_all[0:V_ROWS, 0, 0:DEPTH * P].rearrange("p (l n) -> p l n", l=DEPTH)
        lam_in = lam_in_all[:, 0, :].rearrange("p (l a d) -> p l a d", l=DEPTH, a=4)

        def gm(m):
            return gm_all[:, m, :] if m < GM_IN else gm_late[:, m - GM_IN, :]

        gates = sb("gates", [P, TT, NSA_HEADS, 3])
        raw = sb("raw", [P, 2, SEQ])
        t1 = sb("t1", [P, SEQ])[:, :]
        t2 = sb("t2", [P, SEQ])[:, :]
        o_nsa = raw[:, 0, :]
        hid = sb("hid", [P, 2, 2, 2 * NCP])
        k_cmpT = sb("k_cmpT", [P, 2 * NCP])
        v_cmp = sb("v_cmp", [P, 2, 256])
        neg_max = sb("neg_max", [P, 2, 8])
        sums = sb("sums", [P, 2, 32])
        coef = sb("coef", [P, 2, 8])
        d_rs = sb("d_rs", [P, 2, 4])
        d_mix = sb("d_mix", [P, 2])
        d_sq = sb("d_sq", [P, TT * 4])
        sil = raw[:, :, :]
        cst = sb("cst", [P, C_MASKS])
        cos, sin, ident = cst[:, C_COS:C_COS + SEQ], cst[:, C_SIN:C_SIN + SEQ], cst[:, C_ID:C_ID + P]
        ident_b = sb("ident_b", [P, P], bf16)
        mask_b = sb("mask_b", [P, P + TT * P], bf16)
        ones = sb("ones", [P, P])
        eps = sb("eps", [P, 1])
        table_out = sb("table_out", [P, 1])
        zeros = sb("zeros", [P, 2 * KD])
        vec = sb("vec", [P, DEPTH, V_ROWS])
        lam_s = sb("lam_s", [P, DEPTH, 2])
        neg_lam = sb("neg_lam", [P, DEPTH])
        norm_s = sb("norm_s", [P, DEPTH])
        w2k = sb("w2k", [P, DEPTH, 2, 2, HEAD_DIM])
        w2v = sb("w2v", [P, DEPTH, 2, HEAD_DIM])
        c_silu = sb("c_silu", [P, KD])
        ada_acc = sb("ada_acc", [P, D_MODEL])
        ada = sb("ada", [P, DEPTH, 48])
        gate1 = sb("gate1", [P, 2, KD])
        mul_u = sb("mul_u", [P, 2, KD])
        add_u = sb("add_u", [P, 2, KD])
        mul_r = sb("mul_r", [P, 2, KD])
        add_r = sb("add_r", [P, 2, KD])

        banks = ctx.enter_context(nc.psum_tensor("banks", [P, 8, SEQ], fp32))
        proj = banks[:, 0:2, :]
        scores = banks[:, 2:4, :]
        turned = banks[:, 4:6, :]
        outs = banks[:, 6:8, :]
        mean_ps, var_ps = scores[:, 0, :], scores[:, 1, :]

        ident_in = sem("ident_in")
        const_in = sem("const_in")
        x_in = sem("x_in")
        vec_in = sem("vec_in")
        rows_in = sem("rows_in")
        slot_ready = [sem(f"slot_ready{s}") for s in range(NS)]
        c_loaded = sem("c_loaded")
        c_turned = sem("c_turned")
        zeros_ready = sem("zeros_ready")
        first_in = [sem(f"first_in{k}") for k in range(KD)]
        first_summed = sem("first_summed")
        ada_ready = [sem(f"ada_ready{s}") for s in range(NA)]
        ada_summed = sem("ada_summed")
        setup_done = sem("setup_done")
        vec_turned = sem("vec_turned")
        vec_saved = sem("vec_saved")
        c_ready = sem("c_ready")
        lam_summed = sem("lam_summed")
        lam_exp = sem("lam_exp")
        x_turned = sem("x_turned")
        x_saved = sem("x_saved")
        part1 = sem("part1")
        part2 = sem("part2")
        chunk_done = [sem(f"chunk_done{b}") for b in range(2)]
        chunk_saved = [sem(f"chunk_saved{b}") for b in range(2)]
        split_hi = sem("split_hi")
        split_lo = sem("split_lo")
        part_read = sem("part_read")
        w1_read = sem("w1_read")
        token_saved = sem("token_saved")
        token_turned = sem("token_turned")
        gates_ready = sem("gates_ready")
        u_high = sem("u_high")
        mix_high = sem("mix_high")
        mix_ready = sem("mix_ready")
        merged_sum = sem("merged_sum")
        merged_high = sem("merged_high")
        h_high = sem("h_high")
        h_ready = sem("h_ready")
        kc2_ready = sem("kc2_ready")
        flat_ready = sem("flat_ready")
        rep_ready = sem("rep_ready")
        rope_done = sem("rope_done")
        scored = sem("scored")
        max_done = sem("max_done")
        exp_done = sem("exp_done")
        mix_done = sem("mix_done")
        turn_done = sem("turn_done")
        turn_act = sem("turn_act")
        turn_dve = sem("turn_dve")
        pv_done = sem("pv_done")
        out_done = sem("out_done")
        out_saved = sem("out_saved")
        nsa_ready = sem("nsa_ready")
        dsq_ready = sem("dsq_ready")
        dstd_ready = sem("dstd_ready")
        dnorm_ready = sem("dnorm_ready")
        sig_ready = sem("sig_ready")
        merged = sem("merged")
        y_summed = sem("y_summed")
        mean_done = sem("mean_done")
        centred = sem("centred")
        squared = sem("squared")
        paired = sem("paired")
        var_done = sem("var_done")
        std_ready = sem("std_ready")
        normed = sem("normed")
        u_ready = sem("u_ready")
        res_ready = sem("res_ready")
        out_turned = sem("out_turned")
        out_dve = sem("out_dve")
        out_act = sem("out_act")
        stored = sem("stored")
        dve_chain = sem("dve_chain")
        act_chain = sem("act_chain")
        pool_chain = sem("pool_chain")

        block = ctx.enter_context(nc.Block())

        def wait_done(eng, l, name):
            n = chunk(l, name)
            eng.wait_ge(chunk_done[n % 2], n // 2 + 1)

        def wait_saved(eng, l, name):
            n = chunk(l, name)
            eng.wait_ge(chunk_saved[n % 2], n // 2 + 1)

        def bank_of(l, name):
            return proj[:, chunk(l, name) % 2, :]

        def saved(l, name):
            return chunk_saved[chunk(l, name) % 2]

        def cols(w, lo, hi):
            return w[:, lo:hi].rearrange("(k p) n -> p k n", p=P)

        def weights_in(eng, l, name):
            g = l * len(JOBS) + JOB_AT[name]
            eng.wait_ge(slot_ready[g % NS], READY[g])
            return ring[:, g % NS, 0:blocks_of(name) * P]

        def split_slot(l, name):
            n, size = split_job(l, name), blocks_of(name) * P
            return w_hi[:, n % NQ, 0:size], w_lo[:, n % NQ, 0:size]

        @block.sync
        def _(sp):
            def wait_read(l, name):
                if name in SPLIT_AT:
                    sp.wait_ge(split_lo, split_job(l, name) + 1)
                elif name[-1] == "3":
                    wait_done(sp, l, f"h{name[2]}")
                else:
                    sp.wait_ge(w1_read, 6 * l + 3 * "kv".index(name[2]) + int(name[-1]) + 1)

            def load(l, name):
                g = l * len(JOBS) + JOB_AT[name]
                s = g % NS
                if g >= NS:
                    wait_read((g - NS) // len(JOBS), JOBS[(g - NS) % len(JOBS)])
                slot = ring[:, s, :]
                if name in W_IN_AT:
                    srcs = [cols(w_in[l], W_IN_AT[name], W_IN_AT[name] + P)]
                elif name[:2] == "w1":
                    m, half = divmod(int(name[-1]), 2)
                    w1 = w1_k if name[2] == "k" else w1_v
                    srcs = [cols(w1[l, KD * P * half:KD * P * (half + 1), :], P * m, P * (m + 1))]
                elif name[:2] == "br":
                    m = int(name[2:])
                    srcs = [cols(w[l], P * m, P * (m + 1)) for w in (w_bn, w_bd)]
                elif name[:2] == "wo":
                    m = int(name[2:])
                    srcs = [cols(w_o[l], P * m, P * (m + 1))]
                elif name[:2] == "fo":
                    m, part = divmod(int(name[2:]), FO_PARTS)
                    srcs = [cols(w_f2[l, P * FO_AT[part]:P * FO_AT[part + 1], :], P * m, P * (m + 1))]
                else:
                    first = P * int(name[2:]) + (D_FF if name[1] == "b" else 0)
                    srcs = [cols(w_f1[l], first, first + P)]
                k = 0
                for src in srcs:
                    n = src.shape[1]
                    dst = slot[:, k * P:(k + n) * P].rearrange("p (k n) -> p k n", n=P)
                    sp.dma_start(dst, src).then_inc(slot_ready[s], 16)
                    k += n

            sp.dma_start(c_rows, c[0].rearrange("(k p) -> k p", p=P)).then_inc(c_loaded, 16)
            sp.dma_start(cst[:, C_ID:C_MASKS], consts[:, C_ID:C_MASKS]).then_inc(ident_in, 16)
            for k in range(KD):
                if k >= 3:
                    sp.wait_ge(first_in[k - 3], 16)
                if k == 6:
                    sp.dma_start(x_tok, x[0].rearrange("(i p) n -> p i n", p=P)).then_inc(x_in, 16)
                sp.dma_start(ada_first[k], w_ada[0, k * P:(k + 1) * P, 0:2 * D_MODEL]).then_inc(first_in[k], 16)
            for name in JOBS[:NS]:
                load(0, name)
            sp.dma_start(cst[:, 0:C_ID], consts[:, 0:C_ID]).then_inc(const_in, 16)
            sp.dma_start(mask_in[:, :, :].rearrange("p a n -> p (a n)")[:, 0:P + TT * P],
                         consts[:, C_MASKS:C_COLS]).then_inc(const_in, 16)

            for l in range(DEPTH):
                for name in JOBS[NS if l == 0 else 0:]:
                    load(l, name)
            for half in range(2):
                cut = slice(512 * half, 512 * half + 512)
                for i in range(TT):
                    if half and i >= 2:
                        sp.wait_ge(out_act, i - 1)
                    else:
                        sp.wait_ge(out_dve, TT * half + i + 1)
                    sp.dma_start(out[0, i * P:(i + 1) * P, cut], x_tok[:, i, cut]).then_inc(stored, 16)
            sp.wait_ge(stored, 16 * 2 * TT)

        @block.gpsimd
        def _(pool):
            count = [0]

            def link(ins):
                count[0] += 1
                ins.then_inc(pool_chain, 1)
                pool.wait_ge(pool_chain, count[0])

            def load_slice(n):
                l, j = ADA_GROUPS[n // KD]
                k = n % KD
                pool.dma_start(ada_ring[:, n % NA, :], w_ada[l, k * P:(k + 1) * P, j * D_MODEL:(j + 1) * D_MODEL])\
                    .then_inc(ada_ready[n % NA], 16)

            def ada_groups(first, last):
                for n in range(first * KD, last * KD):
                    g, k = divmod(n, KD)
                    for ahead in (range(n, n + NA) if n == first * KD else (n + NA - 1,)):
                        if ahead < last * KD:
                            load_slice(ahead)
                    acc, w, c_k = ada_acc[:, :], ada_ring[:, n % NA, :], c_silu[:, k:k + 1]
                    pool.wait_ge(ada_ready[n % NA], 16 * (n // NA + 1))
                    if k == 0:
                        if g >= 1:
                            wait_done(pool, ADA_GROUPS[g - 1][0], f"ada{ADA_GROUPS[g - 1][1]}")
                        link(nc.gpsimd.tensor_scalar(acc, w, c_k, 0.0, ALU.mult, ALU.add))
                    else:
                        link(nc.gpsimd.tensor_scalar(w, w, c_k, 0.0, ALU.mult, ALU.add))
                        link(nc.gpsimd.tensor_tensor(acc, acc, w, ALU.add))
                    if k == KD - 1:
                        pool.sem_inc(ada_summed, 1)

            def residual(l, which):
                for m in range(KD):
                    pool.wait_ge(normed, (2 * l + which) * KD + m + 1)
                    if m == 0:
                        pool.wait_ge(part2 if which == 0 else part1, l + 1 + which)
                    nc.gpsimd.tensor_scalar(res[:, m, :], yT[:, m, :], mul_r[:, which, m:m + 1],
                                            add_r[:, which, m:m + 1], ALU.mult, ALU.add)\
                        .then_inc(res_ready, 1)

            for l in range(DEPTH):
                for at, src in ((V_ADA, b_ada[l].rearrange("(m p) -> m p", p=P)),
                                (V_LN1G, ln1_g[l].rearrange("(m p) -> m p", p=P)),
                                (V_LN1B, ln1_b[l].rearrange("(m p) -> m p", p=P)),
                                (V_LN2G, ln2_g[l].rearrange("(m p) -> m p", p=P)),
                                (V_LN2B, ln2_b[l].rearrange("(m p) -> m p", p=P)),
                                (V_NORM, norm_g[l:l + 1, :]),
                                (V_PEK, pe_k[l].rearrange("(j c) d -> j (c d)", c=2)),
                                (V_PEV, pe_v[l].rearrange("(j c) d -> j (c d)", c=2))):
                    pool.dma_start(vec_rows[at:at + src.shape[0], l, :], src).then_inc(rows_in, 16)
            pool.wait_ge(part1, 1)
            ada_groups(0, 4)
            for l in range(DEPTH):
                residual(l, 0)
                if l + 1 < DEPTH:
                    ada_groups(4 + 6 * l, 6 + 6 * l)
                    residual(l, 1)
                    ada_groups(6 + 6 * l, 10 + 6 * l)

        @block.scalar
        def _(act):
            count = [0]

            def link(ins):
                count[0] += 1
                ins.then_inc(act_chain, 1)
                act.wait_ge(act_chain, count[0])

            act.wait_ge(c_turned, 1)
            nc.scalar.activation(c_silu[:, :], banks[:, 3, 0:KD], ACT.Silu).then_inc(c_ready, 1)
            for l in range(DEPTH):
                act.dma_start(lam_in[:, l], lam[l].partition_broadcast(P)).then_inc(vec_in, 16)
                for d in range(2):
                    act.dma_start(w2k[:, l, :, d, :], w2_k[l].rearrange("(m p) d -> p m d", p=P))\
                        .then_inc(vec_in, 16)
                act.dma_start(w2v[:, l], w2_v[l].rearrange("(m p) d -> p m d", p=P)).then_inc(vec_in, 16)

            def prepare(l, name):
                n = split_job(l, name)
                src = weights_in(act, l, name)
                if n >= NQ:
                    ll, before = divmod(n - NQ, len(SPLIT))
                    m, part = divmod(int(SPLIT[before][2:]), FO_PARTS) if SPLIT[before][:2] == "fo" else (0, None)
                    if part is None or part == FO_PARTS - 1:
                        wait_done(act, ll, reader(SPLIT[before]))
                    else:
                        act.wait_ge(part_read, (ll * KD + m) * (FO_PARTS - 1) + part + 1)
                nc.scalar.activation(split_slot(l, name)[0], src, ACT.Copy).then_inc(split_hi, 1)

            def prepare_behind(l, name):
                for job in prepared_at(l, name):
                    prepare(*job)

            def sub_layer_input(n, m, src, scale, bias):
                if n * KD + m >= 2:
                    act.wait_ge(u_ready, n * KD + m - 1)
                link(nc.scalar.activation(raw[:, m % 2, :], src, ACT.Identity, bias=bias, scale=scale))
                nc.scalar.activation(u_hi[:, m, :], raw[:, m % 2, :], ACT.Copy).then_inc(u_high, 1)

            prepare(0, "kc")
            prepare(0, "vc")
            act.wait_ge(part1, 1)
            for k in range(KD):
                act.wait_ge(x_saved, k + 1)
                sub_layer_input(0, k, banks[:, 2 + k % 6, :], mul_u[:, 0, k:k + 1], ada[:, 0, k:k + 1])
                if k == 3:
                    prepare(0, "ksl")
            act.wait_ge(lam_summed, 1)
            nc.scalar.activation(lam_s[:, :, :], lam_s[:, :, :], ACT.Exp).then_inc(lam_exp, 1)

            def save(l, name, dst, scale=1.0):
                prepare_behind(l, name)
                wait_done(act, l, name)
                nc.scalar.activation(dst, bank_of(l, name), ACT.Copy, scale=scale)\
                    .then_inc(saved(l, name), 1)

            def save_raw(l, name, r, scale=1.0):
                prepare_behind(l, name)
                if r == 0:
                    act.wait_ge(u_ready, (2 * l + 1) * KD)
                elif r >= 2:
                    before = RAW[r - 2]
                    if before in TOKEN:
                        act.wait_ge(token_turned, l * len(TOKEN) + TOKEN.index(before) + 1)
                    else:
                        act.wait_ge(rope_done, l * 14 + ROPE.index(before) + 1)
                wait_done(act, l, name)
                nc.scalar.activation(raw[:, r % 2, :], bank_of(l, name), ACT.Copy, scale=scale)\
                    .then_inc(saved(l, name), 1)

            def save_gate(l, m):
                wait_done(act, l, f"gm{m}")
                nc.scalar.activation(gm(m), bank_of(l, f"gm{m}"), ACT.Copy)\
                    .then_inc(saved(l, f"gm{m}"), 1)

            def layernorm(l, which):
                n = 2 * l + which
                last = l == DEPTH - 1 and which == 1
                for m in range(KD):
                    prepare_behind(l, ("wo", "fo")[which] + str(m))
                for m in range(KD):
                    act.wait_ge(centred, n * KD + m + 1)
                    nc.scalar.activation(squares[:, m, :], yT[:, m, :], ACT.Square).then_inc(squared, 1)
                nc.scalar.activation(table_out[:, :], eps[:, :], ACT.Sqrt)
                if not last:
                    prepare(l + which, FIRST_SPLIT[which])
                act.wait_ge(var_done, n + 1)
                nc.scalar.activation(t1, var_ps, ACT.Sqrt, bias=eps[:, :]).then_inc(std_ready, 1)
                w = 1 - which
                for m in range(KD):
                    act.wait_ge(normed, n * KD + m + 1)
                    if m == 0:
                        act.wait_ge(part2 if which == 0 else part1, l + 1 + which)
                    if last:
                        nc.scalar.activation(res[:, m, :], yT[:, m, :], ACT.Identity,
                                             bias=add_u[:, w, m:m + 1], scale=mul_u[:, w, m:m + 1])\
                            .then_inc(u_high, 1)
                    else:
                        sub_layer_input(n + 1, m, yT[:, m, :], mul_u[:, w, m:m + 1], add_u[:, w, m:m + 1])
                if which == 0:
                    nc.scalar.activation(table_out[:, :], eps[:, :], ACT.Silu)

            for l in range(DEPTH):
                wait_done(act, l, "kc")
                nc.scalar.activation(cmp_raw[:, 0, :], bank_of(l, "kc"), ACT.Copy).then_inc(saved(l, "kc"), 1)
                wait_saved(act, l, "kc")
                for g in range(2):
                    src = cmp_raw[64 * g:64 * g + 64, 0, :]
                    nc.scalar.activation(kc2[0:64, 0, g, :], src, ACT.Copy)
                    last = nc.scalar.activation(kc2[64:128, 0, g, 0:SEQ - 1], src[:, 1:SEQ], ACT.Copy)
                last.then_inc(kc2_ready, 1)
                prepare_behind(l, "vc")
                for r, name in enumerate(RAW[:5]):
                    save_raw(l, name, r)
                for i in range(4):
                    save(l, f"qn{i}", q_raw[:, i, :], HEAD_DIM ** -0.5)
                    if i == 1:
                        act.wait_ge(token_saved, l * len(TOKEN) + 3)
                        nc.scalar.activation(gates[:, :, :, :], gates[:, :, :, :], ACT.Sigmoid)\
                            .then_inc(gates_ready, 1)
                for w, name in enumerate(("hk", "hv")):
                    wait_done(act, l, name)
                    dst = hid[:, w].rearrange("p m (g n) -> p m g n", g=2)[:, :, :, 0:NC]
                    src = bank_of(l, name)[:, 0:128].rearrange("p (m g n) -> p m g n", m=2, g=2)[:, :, :, 0:NC]
                    nc.scalar.activation(dst, src, ACT.Gelu_apprx_tanh).then_inc(saved(l, name), 1)
                for r, name in enumerate(RAW[5:], 5):
                    save_raw(l, name, r, HEAD_DIM ** -0.5 if name[:2] == "qd" else 1.0)

                for t in range(len(SEQUENCE) + 1):
                    if t >= 1:
                        for m, k in gate_units(t - 1):
                            if k == 0:
                                prepare_behind(l, f"gm{m}")
                        i, j = SEQUENCE[t - 1]
                        N = (i + 1) * P
                        if j >= 1:
                            act.wait_ge(turn_done, turn_step(l, i, j) + 1)
                            s = score_step(l, i, j)
                            if j == STEPS:
                                nc.scalar.activation(
                                    q_rot[:, :, i * P:(i + 1) * P],
                                    turned[:, 0, :].rearrange("p (c t) -> p c t", c=4), ACT.Copy)\
                                    .then_inc(turn_act, 1)
                            else:
                                act.wait_ge(pv_done, s - 1)
                                nc.scalar.activation(probsT[:, s % 2, 0, 0:N], turned[:, 0, 0:N], ACT.Copy)\
                                    .then_inc(turn_act, 1)
                    if t == len(SEQUENCE):
                        break
                    i, j = SEQUENCE[t]
                    if j < STEPS:
                        s = score_step(l, i, j)
                        N = (i + 1) * P
                        act.wait_ge(max_done, s + 1)
                        if j == 0:
                            nc.scalar.activation(probs[:, s % 2, 0, 0:256], probs[:, s % 2, 0, 0:256],
                                                 ACT.Exp).then_inc(exp_done, 1)
                        else:
                            if s >= 2:
                                i2, j2 = (i, j - 2) if j >= 2 else (i - 1, j + STEPS - 2)
                                if i2 >= 0:
                                    act.wait_ge(turn_done, turn_step(l, i2, j2) + 1)
                            for h in range(2):
                                at = 8 + 2 * (j - 1) + h
                                last = nc.scalar.activation(
                                    probs[:, s % 2, h, 0:N], scores[:, h, 0:N], ACT.Exp,
                                    bias=neg_max[:, s % 2, h:h + 1],
                                    accum_out=sums[:, i % 2, at:at + 1])
                            last.then_inc(exp_done, 1)
                    for m, k in gate_units(t):
                        if k == KD - 1:
                            save_gate(l, m)
                prepare_behind(l, f"gm{GM_IN}")
                act.wait_ge(dsq_ready, l + 1)
                nc.scalar.activation(d_sq[:, :], d_sq[:, :], ACT.Sqrt, bias=eps[:, :],
                                     scale=1.0 / (2 * HEAD_DIM)).then_inc(dstd_ready, 1)

                def open_gates(m):
                    for g in (gm(m), gm(8 + m)):
                        last = nc.scalar.activation(g, g, ACT.Sigmoid)
                    last.then_inc(sig_ready, 1)

                def split_mixer(src, first):
                    for c in range(4):
                        nc.scalar.activation(mix_hi[:, first + c, :], src[:, c, :], ACT.Copy).then_inc(mix_high, 1)

                for m in range(GM_IN, 16):
                    if m > GM_IN:
                        prepare_behind(l, f"gm{m}")
                    if m == 15:
                        wait_saved(act, l, "gm13")
                        wait_saved(act, l, "gm14")
                        open_gates(0)
                        wait_done(act, l, "gm15")
                        act.wait_ge(turn_act, turned_by_act(l, TT - 1, STEPS))
                        split_mixer(q_rot, 0)
                    save_gate(l, m)
                act.wait_ge(turn_dve, turned_by_dve(l, TT, -1) + TT)
                split_mixer(q_raw, 4)
                prepare_behind(l, "yd0")
                wait_saved(act, l, "gm15")
                for m in range(KD):
                    if m:
                        prepare_behind(l, f"yd{m}")
                    if m + 1 < KD:
                        open_gates(m + 1)
                    act.wait_ge(merged_sum, l * KD + m + 1)
                    nc.scalar.activation(merged_hi[:, m, :], merged_raw[:, m, :], ACT.Copy)\
                        .then_inc(merged_high, 1)
                layernorm(l, 0)
                for f in range(KF):
                    if f == 0:
                        act.wait_ge(u_ready, (2 * l + 2) * KD)
                    else:
                        prepare_behind(l, f"fa{f}")
                    if f >= 2:
                        wait_saved(act, l, f"fb{f - 2}")
                    wait_done(act, l, f"fa{f}")
                    nc.scalar.activation(sil[:, f % 2, :], bank_of(l, f"fa{f}"), ACT.Silu)\
                        .then_inc(saved(l, f"fa{f}"), 1)
                    prepare_behind(l, f"fb{f}")
                    wait_saved(act, l, f"fb{f}")
                    nc.scalar.activation(h_hi[:, f, :], h_raw[:, f, :], ACT.Copy).then_inc(h_high, 1)
                layernorm(l, 1)
            act.wait_ge(out_turned, 2)
            for i in (2, 3):
                nc.scalar.activation(x_tok[:, i, 512:1024], banks[:, 2 * i + 1, :], ACT.Copy).then_inc(out_act, 1)

        @block.vector
        def _(dve):
            V = nc.vector
            count = [0]

            def link(ins):
                count[0] += 1
                ins.then_inc(dve_chain, 1)
                dve.wait_ge(dve_chain, count[0])

            def prepare(l, name):
                n = split_job(l, name)
                src = weights_in(dve, l, name)
                hi, lo = split_slot(l, name)
                dve.wait_ge(split_hi, n + 1)
                V.tensor_tensor(lo, src, hi.bitcast(fp32), ALU.subtract).then_inc(split_lo, 1)

            def prepare_behind(l, name):
                for job in prepared_at(l, name):
                    prepare(*job)

            V.memset(zeros[:, :], 0.0).then_inc(zeros_ready, 1)
            V.memset(eps[:, :], EPS)
            V.memset(ones[:, :], 1.0 / D_MODEL)
            dve.wait_ge(c_ready, 1)
            for k in FIRST_DVE:
                dve.wait_ge(first_in[k], 16)
                if k == FIRST_DVE[0]:
                    link(V.tensor_scalar(first_sum, ada_first[k], c_silu[:, k:k + 1], None, ALU.mult))
                else:
                    ins = V.scalar_tensor_tensor(first_sum, ada_first[k], c_silu[:, k:k + 1], first_sum,
                                                 ALU.mult, ALU.add)
                    if k == FIRST_DVE[-1]:
                        ins.then_inc(first_summed, 1)
                    else:
                        link(ins)
                if k == FIRST_DVE[3]:
                    for l in range(DEPTH):
                        dve.wait_ge(vec_turned, l + 1)
                        link(V.tensor_copy(vec[:, l, :], turned[:, l, 0:V_ROWS]))
                        V.tensor_scalar(norm_s[:, l:l + 1], vec[:, l, V_NORM:V_NORM + 1],
                                        1.0 - LAMBDA_INIT[l], None, ALU.mult).then_inc(vec_saved, 1)
            prepare(0, "kc")
            prepare(0, "vc")

            def save_x(k):
                dve.wait_ge(x_turned, k + 1)
                V.tensor_scalar(res[:, k, :], banks[:, 2 + k % 6, :], ALPHA, None, ALU.mult)\
                    .then_inc(x_saved, 1)

            for k in range(6):
                save_x(k)
            wait_done(dve, 0, "ada01")
            link(V.tensor_tensor(ada[:, 0, 0:16], bank_of(0, "ada01")[:, 0:16], vec[:, 0, 0:16], ALU.add))
            V.memset(d_mix[:, 0:1], 0.0).then_inc(saved(0, "ada01"), 1)
            V.tensor_scalar(mul_u[:, 0, :], ada[:, 0, 8:16], 1.0, None, ALU.add).then_inc(part1, 1)

            def save_ada(before_l, name):
                if not ada_before(before_l, name):
                    return
                l, j = ada_before(before_l, name)
                wait_done(dve, l, f"ada{j}")
                link(V.tensor_tensor(ada[:, l, 8 * j:8 * j + 8], bank_of(l, f"ada{j}")[:, 0:8],
                                     vec[:, l, 8 * j:8 * j + 8], ALU.add))
                if j in (1, 4):
                    link(V.tensor_scalar(ada[:, l, 8 * j:8 * j + 8], ada[:, l, 8 * j:8 * j + 8],
                                         1.0, None, ALU.add))
                elif j in (2, 5):
                    V.tensor_scalar(gate1[:, j // 3, :], ada[:, l, 8 * j:8 * j + 8], 1.0, None, ALU.add)
                V.memset(d_mix[:, 0:1], 0.0).then_inc(saved(l, f"ada{j}"), 1)

            def ada_part1(l):
                fold(l - 1, V_LN2G, V_LN2B, ada[:, l, 8:16], ada[:, l, 0:8], 0, 1, part1)

            def ada_part2(l):
                fold(l, V_LN1G, V_LN1B, ada[:, l, 32:40], ada[:, l, 24:32], 1, 0, part2)

            def fold(l, at_g, at_b, scale1, shift, to_u, to_r, signal):
                g, b = vec[:, l, at_g:at_g + KD], vec[:, l, at_b:at_b + KD]
                V.tensor_tensor(mul_u[:, to_u, :], g, scale1, ALU.mult)
                link(V.tensor_tensor(add_u[:, to_u, :], b, scale1, ALU.mult))
                V.tensor_tensor(add_u[:, to_u, :], add_u[:, to_u, :], shift, ALU.add)
                V.tensor_scalar(mul_r[:, to_r, :], g, ALPHA, None, ALU.mult)
                link(V.tensor_scalar(add_r[:, to_r, :], b, ALPHA, None, ALU.mult))
                V.memset(d_mix[:, 0:1], 0.0).then_inc(signal, 1)

            def rope(l, r, src, outs_of):
                shuffle = [i + 8 if i < 8 else i - 8 if i < 16 else i for i in range(32)]
                V.tensor_tensor(t1, src, cos, ALU.mult)
                link(V.stream_shuffle(t2, src, shuffle))
                link(V.tensor_tensor(t2, t2, sin, ALU.mult))
                for dst, rows in outs_of:
                    last = V.tensor_tensor(dst, t1[rows, :], t2[rows, :], ALU.add)
                link(last)
                V.memset(d_mix[:, 1:2], 0.0).then_inc(rope_done, 1)

            def layernorm(l, which):
                n = 2 * l + which
                names = [f"wo{m}" if which == 0 else f"fo{m}" for m in range(KD)]
                last_norm = l == DEPTH - 1 and which == 1
                for m in range(KD):
                    prepare_behind(l, names[m])
                    wait_done(dve, l, names[m])
                    if n >= 1 and m == 0:
                        dve.wait_ge(res_ready, n * KD)
                    V.scalar_tensor_tensor(yT[:, m, :], bank_of(l, names[m]), gate1[:, which, m:m + 1],
                                           res[:, m, :], ALU.mult, ALU.add).then_inc(saved(l, names[m]), 1)
                    if m < KD - 1:
                        wait_saved(dve, l, names[m])
                        if m == 1:
                            link(V.tensor_tensor(t2, yT[:, 0, :], yT[:, 1, :], ALU.add))
                        elif m == KD - 2:
                            V.tensor_tensor(t2, t2, yT[:, m, :], ALU.add).then_inc(y_summed, 1)
                        elif m:
                            link(V.tensor_tensor(t2, t2, yT[:, m, :], ALU.add))
                dve.wait_ge(mean_done, n + 1)
                for m in range(KD):
                    V.tensor_tensor(yT[:, m, :], yT[:, m, :], mean_ps, ALU.subtract).then_inc(centred, 1)
                for m in (4, 6):
                    dve.wait_ge(squared, n * KD + m + 2)
                    V.tensor_tensor(squares[:, m, :], squares[:, m, :], squares[:, m + 1, :], ALU.add)\
                        .then_inc(paired, 1)
                if not last_norm:
                    prepare(l + which, FIRST_SPLIT[which])
                dve.wait_ge(std_ready, n + 1)
                link(V.reciprocal(t2, t1))
                for m in range(KD + 1):
                    if m < KD:
                        V.tensor_tensor(yT[:, m, :], yT[:, m, :], t2, ALU.mult).then_inc(normed, 1)
                    if m and not last_norm:
                        sub_layer_low(n + 1, m - 1)

            def sub_layer_low(n, m):
                dve.wait_ge(u_high, n * KD + m + 1)
                if n:
                    dve.wait_ge(res_ready, (n - 1) * KD + m + 1)
                V.tensor_tensor(u_lo[:, m, :], raw[:, m % 2, :], u_hi[:, m, :].bitcast(fp32), ALU.subtract)\
                    .then_inc(u_ready, 1)

            for k in range(KD + 1):
                if 6 <= k < KD:
                    save_x(k)
                if k:
                    sub_layer_low(0, k - 1)
                if k == 3:
                    prepare(0, "ksl")
            V.memset(hid[:, :, :, :], 0.0)
            V.memset(v_cmp[:, :, :], 0.0)
            dve.wait_ge(const_in, 32)
            V.tensor_copy(ident_b[:, :], ident)
            V.tensor_copy(mask_b[:, :], mask_in[:, :, :].rearrange("p a n -> p (a n)")[:, 0:P + TT * P])\
                .then_inc(setup_done, 1)
            dve.wait_ge(vec_in, 16 * VEC_LOADS)
            lam_v = lam_in.rearrange("p l (a b) d -> p l a b d", b=2)
            for l in range(DEPTH):
                link(V.tensor_tensor(lam_v[:, l, :, 0, :], lam_v[:, l, :, 0, :], lam_v[:, l, :, 1, :], ALU.mult))
                link(V.tensor_reduce(lam_s[:, l, :], lam_v[:, l, :, 0, :], AX.X, ALU.add))
            V.memset(t1[:, 0:1], 0.0).then_inc(lam_summed, 1)
            dve.wait_ge(lam_exp, 1)
            link(V.tensor_tensor(neg_lam[:, :], lam_s[:, :, 1], lam_s[:, :, 0], ALU.subtract))
            link(V.tensor_tensor(neg_lam[:, :], neg_lam[:, :], cst[:, C_LAM:C_LAM + DEPTH], ALU.subtract))

            def merged_low(l, m):
                dve.wait_ge(merged_high, l * KD + m + 1)
                V.tensor_tensor(merged_lo[:, m, :], merged_raw[:, m, :], merged_hi[:, m, :].bitcast(fp32),
                                ALU.subtract).then_inc(merged, 1)

            for l in range(DEPTH):
                def build_flat(w):
                    at = (V_PEK, V_PEV)[w]
                    for g in range(2):
                        for hi in range(2):
                            src = kc2[:, w, g, 16 * hi:16 * hi + 16 * NC]\
                                .rearrange("p (n j) -> p j n", j=16)[:, 0:16:2, :]
                            pe = vec[:, l, at + 8 * hi:at + 8 * hi + 8].unsqueeze(2).to_broadcast([P, 8, NC])
                            last = V.tensor_tensor(flat[:, w, 8 * hi:8 * hi + 8, NCP * g:NCP * g + NC],
                                                   src, pe, ALU.add)
                    last.then_inc(flat_ready, 1)

                def save_tokens(name):
                    n = TOKEN.index(name)
                    dve.wait_ge(token_turned, l * len(TOKEN) + n + 1)
                    src = turned[:, n % 2, :].rearrange("p (i n) -> p i n", i=TT)
                    if name == "g":
                        src, dst = src[:, :, 0:24], gates[:, :, :, :].rearrange("p i h b -> p i (h b)")
                    elif name[:2] == "vd":
                        dst = vd_tok[:, :, P * int(name[2:]):P * (int(name[2:]) + 1)]
                    else:
                        dst = v_tok[:, :, P * n:P * (n + 1)]
                    V.tensor_copy(dst, src).then_inc(token_saved, 1)

                wait_done(dve, l, "vc")
                V.tensor_copy(cmp_raw[:, 1, :], bank_of(l, "vc")).then_inc(saved(l, "vc"), 1)
                prepare_behind(l, "vc")
                wait_saved(dve, l, "vc")
                for g in range(2):
                    src = cmp_raw[64 * g:64 * g + 64, 1, :]
                    V.tensor_copy(kc2[0:64, 1, g, :], src)
                    last = V.tensor_copy(kc2[64:128, 1, g, 0:SEQ - 1], src[:, 1:SEQ])
                link(last)
                build_flat(1)
                dve.wait_ge(kc2_ready, l + 1)
                build_flat(0)
                for r, name in enumerate(("ksl", "kwn")):
                    prepare_behind(l, name)
                    wait_saved(dve, l, name)
                    rope(l, r, raw[:, r % 2, :],
                         [(k_dup[64 * h:64 * h + 64, r, g, :], slice(64 * g, 64 * g + 64))
                          for g in range(2) for h in range(2)])
                for name in ("vs", "vw", "g"):
                    prepare_behind(l, name)
                    if name != "vs":
                        save_tokens(TOKEN[TOKEN.index(name) - 1])
                for i in range(4):
                    save_ada(l, f"qn{i}")
                    prepare_behind(l, f"qn{i}")
                    if i == 0:
                        save_tokens("g")
                    wait_saved(dve, l, f"qn{i}")
                    rope(l, 2 + i, q_raw[:, i, :], [(q_rot[:, i, :], slice(0, P))])
                wait_saved(dve, l, "hv")
                V.tensor_copy(
                    hid_rep.rearrange("p m g r n -> p (m g) r n"),
                    hid[:, 1].rearrange("p m (g n) -> p (m g) n", g=2).unsqueeze(2)
                    .to_broadcast([P, 4, 4, NCP])).then_inc(rep_ready, 1)
                wait_done(dve, l, "kv2")
                V.tensor_copy(k_cmpT[:, :], bank_of(l, "kv2")[:, 0:2 * NCP])
                for g in range(2):
                    for r in range(4):
                        last = V.tensor_copy(
                            v_cmp[32 * r:32 * r + 32, g, 64 * r:64 * r + 64],
                            bank_of(l, "kv2")[32 * r:32 * r + 32, 64 + 64 * g:128 + 64 * g])
                last.then_inc(saved(l, "kv2"), 1)
                for a, first, dst in (("kd", 6, kdT), ("qd", 10, qdT)):
                    for i in range(4):
                        save_ada(l, f"{a}{i}")
                        prepare_behind(l, f"{a}{i}")
                        wait_saved(dve, l, f"{a}{i}")
                        rope(l, first + i, raw[:, RAW.index(f"{a}{i}") % 2, :], [(dst[:, i, :], slice(0, P))])
                for i in range(4):
                    save_ada(l, f"vd{i}")
                    prepare_behind(l, f"vd{i}")
                    if i:
                        save_tokens(f"vd{i - 1}")
                save_tokens("vd3")
                dve.wait_ge(gates_ready, l + 1)

                for t in range(len(SEQUENCE) + 2):
                    if 1 <= t <= len(SEQUENCE):
                        i, j = SEQUENCE[t - 1]
                        s = score_step(l, i, j)
                        N = (i + 1) * P
                        if 9 <= j < STEPS:
                            dve.wait_ge(exp_done, s + 1)
                            hd = j - 9
                            d_sum = sums[:, i % 2, 24 + 2 * hd:26 + 2 * hd]
                            link(V.reciprocal(d_mix[:, 0:1], d_sum[:, 1:2]))
                            link(V.scalar_tensor_tensor(d_mix[:, 0:1], d_mix[:, 0:1], d_sum[:, 0:1],
                                                        neg_lam[:, l:l + 1], ALU.mult, ALU.mult))
                            V.scalar_tensor_tensor(probs[:, s % 2, 0, 0:N], probs[:, s % 2, 1, 0:N],
                                                   d_mix[:, 0:1], probs[:, s % 2, 0, 0:N],
                                                   ALU.mult, ALU.add).then_inc(mix_done, 1)
                    if t < len(SEQUENCE):
                        i, j = SEQUENCE[t]
                        s = score_step(l, i, j)
                        N = (i + 1) * P
                        if j < STEPS:
                            dve.wait_ge(scored, s + 1)
                        if j == 0:
                            if i >= 1:
                                dve.wait_ge(turn_done, turn_step(l, i - 1, STEPS - 2) + 1)
                            src = scores[:, 0:2, 0:4 * NCP].rearrange("p h (c n) -> p h c n", c=4)
                            link(V.tensor_reduce(neg_max[:, s % 2, 0:8].rearrange("p (h c) -> p h c", h=2),
                                                 src, AX.X, ALU.max))
                            for h in range(2):
                                dst = probs[:, s % 2, 0, 0:256]\
                                    .rearrange("p (c h n) -> p h c n", c=4, h=2)[:, h]
                                last = V.tensor_tensor(
                                    dst, src[:, h],
                                    neg_max[:, s % 2, 4 * h:4 * h + 4].unsqueeze(2).to_broadcast([P, 4, NCP]),
                                    ALU.subtract)
                            last.then_inc(max_done, 1)
                        elif j < STEPS:
                            V.tensor_reduce(neg_max[:, s % 2, 0:2], scores[:, 0:2, 0:N], AX.X, ALU.max,
                                            negate=True).then_inc(max_done, 1)
                    if 1 <= t <= len(SEQUENCE):
                        i, j = SEQUENCE[t - 1]
                        s = score_step(l, i, j)
                        N = (i + 1) * P
                        if j == 0:
                            dve.wait_ge(exp_done, s + 1)
                            V.tensor_reduce(sums[:, i % 2, 0:8],
                                            probs[:, s % 2, 0, 0:256].rearrange("p (h n) -> p h n", n=NCP),
                                            AX.X, ALU.add)
                        if j <= 8:
                            dve.wait_ge(turn_done, turn_step(l, i, j) + 1)
                            if s >= 2:
                                dve.wait_ge(pv_done, s - 1)
                            h, n = (0, 256) if j == 0 else (1, N)
                            V.tensor_copy(probsT[:, s % 2, h, 0:n], turned[:, h, 0:n]).then_inc(turn_dve, 1)
                    if 1 <= t <= len(SEQUENCE):
                        for m, k in gate_units(t - 1):
                            if k == 0:
                                prepare_behind(l, f"gm{m}")
                    if t >= 2:
                        i, j = SEQUENCE[t - 2]
                        if j in (0, 4, 8, 12):
                            b = j // 4
                            q = out_bank(l, i, j)
                            bank = outs[:, q % 2, :]
                            dve.wait_ge(out_done, q + 1)
                            if b < 3:
                                link(V.reciprocal(coef[:, 0, :], sums[:, i % 2, 8 * b:8 * b + 8]))
                                if b == 0 and i == 0:
                                    link(V.tensor_scalar(coef[:, 0, :], coef[:, 0, :], cst[:, C_ANY:C_ANY + 1],
                                                         None, ALU.mult))
                                link(V.tensor_tensor(coef[:, 0, :], coef[:, 0, :], gates[:, i, :, b], ALU.mult))
                                dst = o_nsa if b == 0 else t1
                                if b == 0 and i >= 1:
                                    dve.wait_ge(turn_done, turn_step(l, i - 1, STEPS) + 1)
                                link(V.tensor_tensor(
                                    dst[:, :].rearrange("p (h d) -> p h d", d=HEAD_DIM),
                                    bank.rearrange("p (h d) -> p h d", d=HEAD_DIM),
                                    coef[:, 0, :].unsqueeze(2).to_broadcast([P, 8, HEAD_DIM]), ALU.mult))
                                V.memset(d_mix[:, 1:2], 0.0).then_inc(out_saved, 1)
                                if b:
                                    ins = V.tensor_tensor(o_nsa[:, :], o_nsa[:, :], t1, ALU.add)
                                    if b == 2:
                                        ins.then_inc(nsa_ready, 1)
                                    else:
                                        link(ins)
                            else:
                                d_sum = sums[:, i % 2, 24:32].rearrange("p (h m) -> p h m", m=2)
                                link(V.reciprocal(d_rs[:, 0, :], d_sum[:, :, 0]))
                                od = q_raw[:, :, i * P:(i + 1) * P]
                                link(V.tensor_tensor(od, bank.rearrange("p (h e) -> p h e", h=4),
                                                     d_rs[:, 0, :].unsqueeze(2).to_broadcast([P, 4, P]),
                                                     ALU.mult))
                                V.memset(d_mix[:, 1:2], 0.0).then_inc(out_saved, 1)
                        elif j == STEPS:
                            sq, od = t2.rearrange("p (h e) -> p h e", h=4), q_raw[:, :, i * P:(i + 1) * P]
                            link(V.tensor_tensor(sq, od, od, ALU.mult))
                            ins = V.tensor_reduce(d_sq[:, 4 * i:4 * i + 4], sq, AX.X, ALU.add)
                            if i == TT - 1:
                                ins.then_inc(dsq_ready, 1)
                            else:
                                link(ins)

                save_ada(l, f"gm{GM_IN}")
                ada_part2(l)
                prepare_behind(l, f"gm{GM_IN}")
                dve.wait_ge(dstd_ready, l + 1)
                link(V.reciprocal(d_sq[:, :], d_sq[:, :]))
                for i in range(TT):
                    od = q_raw[:, :, i * P:(i + 1) * P]
                    V.tensor_tensor(od, od, d_sq[:, 4 * i:4 * i + 4].unsqueeze(2).to_broadcast([P, 4, P]),
                                    ALU.mult).then_inc(dnorm_ready, 1)
                for m in range(GM_IN + 1, 16):
                    prepare_behind(l, f"gm{m}")
                for i in range(TT):
                    dve.wait_ge(turn_done, turn_step(l, TT, i) + 1)
                    V.tensor_scalar(q_raw[:, :, i * P:(i + 1) * P],
                                    turned[:, i % 2, :].rearrange("p (h t) -> p h t", h=4),
                                    norm_s[:, l:l + 1], None, ALU.mult).then_inc(turn_dve, 1)
                for k in range(KD):
                    dve.wait_ge(mix_high, l * KD + k + 1)
                    src = q_rot[:, k, :] if k < 4 else q_raw[:, k - 4, :]
                    V.tensor_tensor(mix_lo[:, k, :], src, mix_hi[:, k, :].bitcast(fp32), ALU.subtract)\
                        .then_inc(mix_ready, 1)
                for m in range(KD):
                    prepare_behind(l, f"yd{m}")
                    dve.wait_ge(sig_ready, l * KD + m + 1)
                    wait_done(dve, l, f"yn{m}")
                    if m:
                        dve.wait_ge(merged_sum, l * KD + m)
                    V.tensor_tensor(t1, bank_of(l, f"yn{m}"), gm(m), ALU.mult).then_inc(saved(l, f"yn{m}"), 1)
                    wait_done(dve, l, f"yd{m}")
                    V.tensor_tensor(t2, bank_of(l, f"yd{m}"), gm(8 + m), ALU.mult)\
                        .then_inc(saved(l, f"yd{m}"), 1)
                    wait_saved(dve, l, f"yn{m}")
                    wait_saved(dve, l, f"yd{m}")
                    V.tensor_tensor(merged_raw[:, m, :], t1, t2, ALU.add).then_inc(merged_sum, 1)
                    if m:
                        merged_low(l, m - 1)
                merged_low(l, KD - 1)
                layernorm(l, 0)
                for f in range(KF + 1):
                    if f < KF:
                        save_ada(l, f"fa{f}")
                        if f:
                            prepare_behind(l, f"fa{f}")
                        prepare_behind(l, f"fb{f}")
                        wait_done(dve, l, f"fb{f}")
                        wait_saved(dve, l, f"fa{f}")
                        V.tensor_tensor(h_raw[:, f, :], bank_of(l, f"fb{f}"), sil[:, f % 2, :], ALU.mult)\
                            .then_inc(saved(l, f"fb{f}"), 1)
                    if f:
                        dve.wait_ge(h_high, l * KF + f)
                        V.tensor_tensor(h_lo[:, f - 1, :], h_raw[:, f - 1, :],
                                        h_hi[:, f - 1, :].bitcast(fp32), ALU.subtract).then_inc(h_ready, 1)
                if l + 1 < DEPTH:
                    ada_part1(l + 1)
                else:
                    V.tensor_copy(mul_u[:, 0, :], vec[:, l, V_LN2G:V_LN2G + KD])
                    link(V.tensor_copy(add_u[:, 0, :], vec[:, l, V_LN2B:V_LN2B + KD]))
                    V.memset(d_mix[:, 0:1], 0.0).then_inc(part1, 1)
                layernorm(l, 1)
            for half, tiles in enumerate((range(TT), (0, 1))):
                dve.wait_ge(out_turned, half + 1)
                for i in tiles:
                    V.tensor_copy(x_tok[:, i, 512 * half:512 * half + 512], banks[:, 2 * i + half, :])\
                        .then_inc(out_dve, 1)

        @block.tensor
        def _(pe):
            M = nc.tensor.matmul

            one_col = cst[:, C_ANY + 1:C_ANY + 2]
            pe.wait_ge(ident_in, 16)

            def first_slice(k):
                pe.wait_ge(first_in[k], 16)
                for m in range(2 * KD):
                    M(bank_of(0, "ada01")[:, m:m + 1], ada_first[k][:, m * P:(m + 1) * P], c_silu[:, k:k + 1],
                      start=False, stop=True, skip_group_check=True)

            def turn_vectors():
                pe.wait_ge(rows_in, 16 * ROW_LOADS)
                for l in range(DEPTH):
                    nc.tensor.transpose(turned[:, l, 0:V_ROWS], vec_rows[:, l, :], ident[0:V_ROWS, 0:V_ROWS])\
                        .then_inc(vec_turned, 1)

            def turn_x(chunks):
                pe.wait_ge(x_in, 16)
                for k in chunks:
                    if k == 2:
                        pe.wait_ge(vec_saved, DEPTH)
                    if k >= 6:
                        pe.wait_ge(u_ready, k - 5)
                    for i in range(TT):
                        last = nc.tensor.transpose(banks[:, 2 + k % 6, i * P:(i + 1) * P],
                                                   x_tok[:, i, k * P:(k + 1) * P], ident)
                    last.then_inc(x_turned, 1)

            pe.wait_ge(c_loaded, 16)
            nc.tensor.transpose(banks[:, 3, 0:KD], c_rows, ident[0:KD, 0:KD]).then_inc(c_turned, 1)
            pe.wait_ge(zeros_ready, 1)
            M(bank_of(0, "ada01")[:, 0:2 * KD], ident, zeros[:, :], start=True, stop=True)
            pe.wait_ge(c_ready, 1)
            for k in FIRST_PE:
                first_slice(k)
            turn_vectors()
            turn_x(range(6))
            pe.wait_ge(first_summed, 1)
            for m in range(2 * KD):
                last = M(bank_of(0, "ada01")[:, m:m + 1], first_sum[:, m * P:(m + 1) * P], one_col,
                         start=False, stop=True, skip_group_check=True)
            last.then_inc(chunk_done[chunk(0, "ada01") % 2], 1)

            def sum_ada(before_l, name):
                if not ada_before(before_l, name):
                    return
                l, j = ada_before(before_l, name)
                bank = take_bank(l, f"ada{j}")
                g = ADA_GROUPS.index((l, j))
                pe.wait_ge(ada_summed, g + 1)
                for m in range(KD):
                    last = M(bank[:, m:m + 1], ada_acc[:, m * P:(m + 1) * P], one_col, start=True, stop=True)
                done(l, f"ada{j}", last)

            def take_bank(l, name):
                n = chunk(l, name)
                if n >= 2:
                    pe.wait_ge(chunk_saved[n % 2], n // 2)
                return proj[:, n % 2, :]

            def take_split(l, name):
                pe.wait_ge(split_lo, split_job(l, name) + 1)
                return split_slot(l, name)

            def product(bank, w, src, k, at, start, stop):
                (wh, wl), (sh, sl) = w, src
                block = slice(at * P, (at + 1) * P)
                M(bank, wh[:, block], sh[:, k, :], start=start, stop=False)
                M(bank, wh[:, block], sl[:, k, :], start=False, stop=False)
                return M(bank, wl[:, block], sh[:, k, :], start=False, stop=stop)

            def done(l, name, ins):
                ins.then_inc(chunk_done[chunk(l, name) % 2], 1)

            def project(l, name, src=(u_hi, u_lo)):
                w = take_split(l, name)
                bank = take_bank(l, name)
                for k in range(KD):
                    last = product(bank, w, src, k, k, k == 0, k == KD - 1)
                done(l, name, last)

            def project_first(l, names, src, ready, count):
                w = [take_split(l, name) for name in names]
                out = [take_bank(l, name) for name in names]
                for k in range(KD):
                    pe.wait_ge(ready, count + k + 1)
                    if names[0] == "kc" and l == 0 and k + 6 < KD:
                        turn_x([k + 6])
                    for i, name in enumerate(names):
                        last = product(out[i], w[i], src, k, k, k == 0, k == KD - 1)
                        if k == KD - 1:
                            done(l, name, last)

            def turn_tokens(l, name):
                n, r = TOKEN.index(name), RAW.index(name)
                wait_saved(pe, l, name)
                if n >= 2:
                    pe.wait_ge(token_saved, l * len(TOKEN) + n - 1)
                for i in range(TT):
                    last = nc.tensor.transpose(turned[:, n % 2, i * P:(i + 1) * P],
                                               raw[:, r % 2, i * P:(i + 1) * P], ident)
                last.then_inc(token_turned, 1)

            def score(l, i, j):
                s = score_step(l, i, j)
                if s >= 1:
                    pe.wait_ge(exp_done, s)
                tile = slice(i * P, (i + 1) * P)
                if j == 0:
                    for h in range(2):
                        M(scores[:, h, 0:P], ident_b[:, :], mask_b[:, P + i * P:2 * P + i * P],
                          start=True, stop=True)
                    for c in range(4):
                        for h in range(2):
                            rows = slice(64 * h, 64 * h + 64)
                            last = M(scores[:, h, NCP * c:NCP * (c + 1)], q_raw[rows, c, tile],
                                     k_cmpT[rows, NCP * (c // 2):NCP * (c // 2 + 1)],
                                     start=False, stop=True, skip_group_check=True)
                    last.then_inc(scored, 1)
                    return
                N = (i + 1) * P
                for h in range(2):
                    rows = slice(64 * h, 64 * h + 64)
                    if j <= 8:
                        c = (j - 1) % 4
                        q, k = q_rot[rows, c, tile], k_dup[rows, (j - 1) // 4, c // 2, 0:N]
                    else:
                        q, k = qdT[rows, j - 9, tile], kdT[rows, j - 9, 0:N]
                    M(scores[:, h, 0:N], q, k, start=True, stop=True)
                for h in range(2):
                    last = M(scores[:, h, i * P:N], ident_b[:, :], mask_b[:, 0:P], start=False, stop=True,
                             skip_group_check=True)
                last.then_inc(scored, 1)

            def free_turned(l, i, j):
                if (i, j) == (0, 0):
                    if l:
                        pe.wait_ge(turn_dve, turned_by_dve(l, 0, -1))
                    return
                if j == 0:
                    i, j = i - 1, STEPS + 1
                pe.wait_ge(turn_act, turned_by_act(l, i, j - 1))
                pe.wait_ge(turn_dve, turned_by_dve(l, i, j - 1))

            def turn(l, i, j):
                s = score_step(l, i, j)
                free_turned(l, i, j)
                if j < STEPS:
                    pe.wait_ge(exp_done, s + 1)
                if 9 <= j < STEPS:
                    pe.wait_ge(mix_done, (l * TT + i) * 4 + j - 8)
                if j == STEPS:
                    pe.wait_ge(nsa_ready, l * TT + i + 1)
                    blocks = [(0, c, o_nsa[:, c * P:(c + 1) * P]) for c in range(4)]
                elif j == 0:
                    blocks = [(0, g, probs[:, s % 2, 0, g * P:(g + 1) * P]) for g in range(2)]
                else:
                    blocks = [(h, b, probs[:, s % 2, h, b * P:(b + 1) * P])
                              for h in range(2 if j <= 8 else 1) for b in range(i + 1)]
                for h, b, src in blocks:
                    last = nc.tensor.transpose(turned[:, h, b * P:(b + 1) * P], src, ident)
                last.then_inc(turn_done, 1)

            def values(l, i, j):
                s = score_step(l, i, j)
                q = out_bank(l, i, j)
                bank = outs[:, q % 2, :]
                if j in (0, 1, 5, 9) and q >= 2:
                    pe.wait_ge(out_saved, q - 1)
                if j <= 8:
                    pe.wait_ge(turn_dve, turned_by_dve(l, i, j))
                if j >= 1:
                    pe.wait_ge(turn_act, turned_by_act(l, i, j))
                if j == 0:
                    for g in range(2):
                        last = M(bank[:, 256 * g:256 * (g + 1)], probsT[:, s % 2, 0, g * P:(g + 1) * P],
                                 v_cmp[:, g, :], start=True, stop=True)
                elif j <= 8:
                    br, c = (j - 1) // 4, (j - 1) % 4
                    for h in range(2):
                        head = 2 * c + h
                        v = slice(128 * br + 64 * (c // 2), 128 * br + 64 * (c // 2) + 64)
                        for b in range(i + 1):
                            last = M(bank[:, 64 * head:64 * head + 64], probsT[:, s % 2, h, b * P:(b + 1) * P],
                                     v_tok[:, b, v], start=b == 0, stop=b == i)
                else:
                    hd = j - 9
                    for b in range(i + 1):
                        last = M(bank[:, P * hd:P * (hd + 1)], probsT[:, s % 2, 0, b * P:(b + 1) * P],
                                 vd_tok[:, b, P * hd:P * (hd + 1)], start=b == 0, stop=b == i)
                if j in (0, 4, 8, 12):
                    last.then_inc(out_done, 1)
                    pe.wait_ge(out_done, q + 1)
                    pe.sem_inc(pv_done, 1)
                else:
                    last.then_inc(pv_done, 1)

            def merge_gate(l, m, k):
                name = f"gm{m}"
                if k == 0:
                    take_split(l, name)
                    take_bank(l, name)
                ins = product(bank_of(l, name), split_slot(l, name), (u_hi, u_lo), k, k, k == 0, k == KD - 1)
                if k == KD - 1:
                    done(l, name, ins)

            def mean_and_variance(l, which):
                n = 2 * l + which
                pe.wait_ge(y_summed, n + 1)
                M(mean_ps, ones[:, :], t2, start=True, stop=False)
                wait_saved(pe, l, ("wo", "fo")[which] + str(KD - 1))
                M(mean_ps, ones[:, :], yT[:, KD - 1, :], start=False, stop=True).then_inc(mean_done, 1)
                for m in (0, 1, 2, 3, 4, 6):
                    if m < 4:
                        pe.wait_ge(squared, n * KD + m + 1)
                    else:
                        pe.wait_ge(paired, 2 * n + (m - 4) // 2 + 1)
                    ins = M(var_ps, ones[:, :], squares[:, m, :], start=m == 0, stop=m == 6)
                ins.then_inc(var_done, 1)

            for l in range(DEPTH):
                project_first(l, ("kc", "vc"), (u_hi, u_lo), u_ready, 2 * l * KD)
                project(l, "ksl")
                project(l, "kwn")
                for name in ("vs", "vw", "g"):
                    project(l, name)
                    if name != "vs":
                        turn_tokens(l, TOKEN[TOKEN.index(name) - 1])
                for i in range(4):
                    sum_ada(l, f"qn{i}")
                    project(l, f"qn{i}")
                    if i == 0:
                        turn_tokens(l, "g")
                for w, name in enumerate(("hk", "hv")):
                    bank = take_bank(l, name)
                    pe.wait_ge(flat_ready, 2 * l + 2)
                    for m in range(2):
                        dst = bank[:, 2 * NCP * m:2 * NCP * (m + 1)].rearrange("p (g n) -> p g n", g=2)[:, :, 0:NC]
                        for j in range(KJ):
                            if j % KD == 0:
                                slot = weights_in(pe, l, f"w1{name[1]}{2 * m + j // KD}")
                            last = M(dst, slot[:, (j % KD) * P:(j % KD + 1) * P],
                                     flat[:, w, j, :].rearrange("p (g n) -> p g n", g=2)[:, :, 0:NC],
                                     start=j == 0, stop=j == KJ - 1)
                            if j % KD == KD - 1 and (m, j) != (1, KJ - 1):
                                last.then_inc(w1_read, 1)
                    done(l, name, last)
                bank = take_bank(l, "kv2")
                wait_saved(pe, l, "hk")
                for m in range(2):
                    M(bank[:, 0:2 * NCP], w2k[:, l, m].rearrange("p a d -> p (a d)"), hid[:, 0, m, :],
                      start=m == 0, stop=m == 1)
                pe.wait_ge(rep_ready, l + 1)
                for g in range(2):
                    for m in range(2):
                        last = M(bank[:, 64 + 64 * g:128 + 64 * g],
                                 hid_rep[:, m, g].rearrange("p r n -> p (r n)"), w2v[:, l, m, :],
                                 start=m == 0, stop=m == 1)
                done(l, "kv2", last)
                for name in [f"{a}{i}" for a in ("kd", "qd") for i in range(4)]:
                    sum_ada(l, name)
                    project(l, name)
                for i in range(4):
                    sum_ada(l, f"vd{i}")
                    project(l, f"vd{i}")
                    if i:
                        turn_tokens(l, f"vd{i - 1}")
                first_gates = gate_units(0)
                for m, k in first_gates:
                    merge_gate(l, m, k)
                turn_tokens(l, "vd3")

                pe.wait_ge(rope_done, 14 * (l + 1))
                wait_saved(pe, l, "kv2")
                pe.wait_ge(token_saved, len(TOKEN) * (l + 1))
                pe.wait_ge(setup_done, 1)
                for t in range(len(SEQUENCE) + 2):
                    if t < len(SEQUENCE) and SEQUENCE[t][1] < STEPS:
                        score(l, *SEQUENCE[t])
                    units = gate_units(t) if 0 < t < len(SEQUENCE) else []
                    for m, k in units[:1]:
                        merge_gate(l, m, k)
                    if 1 <= t <= len(SEQUENCE):
                        turn(l, *SEQUENCE[t - 1])
                    for m, k in units[1:]:
                        merge_gate(l, m, k)
                    if t >= 2 and SEQUENCE[t - 2][1] < STEPS:
                        values(l, *SEQUENCE[t - 2])
                sum_ada(l, f"gm{GM_IN}")
                def turn_diff(i):
                    pe.wait_ge(dnorm_ready, l * TT + i + 1)
                    if i >= 2:
                        pe.wait_ge(turn_dve, turned_by_dve(l, TT, -1) + i - 1)
                    for c in range(4):
                        last = nc.tensor.transpose(turned[:, i % 2, c * P:(c + 1) * P],
                                                   q_raw[:, c, i * P:(i + 1) * P], ident)
                    last.then_inc(turn_done, 1)

                for n in range(GM_IN * KD, 16 * KD):
                    if n == 15 * KD:
                        pe.wait_ge(turn_act, turned_by_act(l, TT - 1, STEPS))
                        turn_diff(0)
                        turn_diff(1)
                    elif n == 16 * KD - 2:
                        turn_diff(2)
                        turn_diff(3)
                    merge_gate(l, *divmod(n, KD))
                for m in range(KD):
                    w = take_split(l, f"br{m}")
                    for a, first in (("n", 0), ("d", 4)):
                        bank = take_bank(l, f"y{a}{m}")
                        for k in range(first, first + 4):
                            if m == 0:
                                pe.wait_ge(mix_ready, l * KD + k + 1)
                            last = product(bank, w, (mix_hi, mix_lo), k, k, k == first, k == first + 3)
                        done(l, f"y{a}{m}", last)
                project_first(l, ("wo0", "wo1"), (merged_hi, merged_lo), merged, l * KD)
                for m in range(2, KD):
                    project(l, f"wo{m}", (merged_hi, merged_lo))
                mean_and_variance(l, 0)
                for f in range(KF):
                    sum_ada(l, f"fa{f}")
                    if f == 0:
                        project_first(l, ("fa0", "fb0"), (u_hi, u_lo), u_ready, (2 * l + 1) * KD)
                    else:
                        project(l, f"fa{f}")
                        project(l, f"fb{f}")
                for m in range(KD):
                    bank = take_bank(l, f"fo{m}")
                    for part in range(FO_PARTS):
                        w = take_split(l, f"fo{FO_PARTS * m + part}")
                        for k in range(FO_AT[part], FO_AT[part + 1]):
                            if m == 0:
                                pe.wait_ge(h_ready, l * KF + k + 1)
                            last = product(bank, w, (h_hi, h_lo), k, k - FO_AT[part], k == 0, k == KF - 1)
                        if part < FO_PARTS - 1:
                            last.then_inc(part_read, 1)
                    done(l, f"fo{m}", last)
                mean_and_variance(l, 1)
            for k in range(KD):
                pe.wait_ge(u_high, 2 * DEPTH * KD + k + 1)
                for i in range(TT):
                    last = nc.tensor.transpose(banks[:, 2 * i + k // 4, (k % 4) * P:(k % 4 + 1) * P],
                                               res[:, k, i * P:(i + 1) * P], ident)
                if k in (3, 7):
                    last.then_inc(out_turned, 1)


def constants():
    c = np.zeros((P, C_COLS), np.float32)
    rot = HEAD_DIM // ROPE_FRACTION
    half = rot // 2
    inv = np.float32(ROPE_THETA) ** (-np.arange(half, dtype=np.float32) * np.float32(2.0) / np.float32(rot))
    ang = (np.arange(SEQ, dtype=np.float32)[:, None] * inv.astype(np.float32)[None, :]).T
    c[:, C_COS:C_COS + SEQ] = 1.0
    for base in (0, 64):
        c[base:base + half, C_COS:C_COS + SEQ] = np.cos(ang)
        c[base + half:base + rot, C_COS:C_COS + SEQ] = np.cos(ang)
        c[base:base + half, C_SIN:C_SIN + SEQ] = -np.sin(ang)
        c[base + half:base + rot, C_SIN:C_SIN + SEQ] = np.sin(ang)
    c[:, C_ID:C_ID + P] = np.eye(P)
    q = np.arange(P)
    c[:, C_MASKS:C_MASKS + P] = np.where(q[None, :] <= q[:, None], 0.0, NEG_INF)
    ends = np.arange(NCP) * CMP_STRIDE + CMP_BLOCK - 1
    for i in range(TT):
        m = np.where(ends[None, :] <= (i * P + q)[:, None], 0.0, NEG_INF)
        c[:, C_MASKS + (i + 1) * P:C_MASKS + (i + 2) * P] = np.tile(m, (1, 4))
    c[:, C_ANY] = (q >= CMP_BLOCK - 1)
    c[:, C_ANY + 1] = 1.0
    c[:, C_LAM:C_LAM + DEPTH] = np.array(LAMBDA_INIT)[None, :]
    return c


_INS = ["x", "w_ada", "b_ada", "c", "w_in", "cmp_pe_k", "cmp_w1_k", "cmp_w2_k", "cmp_pe_v", "cmp_w1_v",
        "cmp_w2_v", "diff_lambda", "diff_norm_g", "w_branch_nsa", "w_branch_diff", "w_out", "ln1_g",
        "ln1_b", "w_ffn_in", "w_ffn_out", "ln2_g", "ln2_b"]


def kernel(**inputs):
    import numpy as _np
    import concourse.bacc as _bacc
    from concourse import mybir as _mybir
    from concourse.bass_utils import run_bass_kernel_spmd as _run

    nc = _bacc.Bacc("TRN2", target_bir_lowering=False, num_devices=1)
    arrays, args = {}, []
    for name in _INS + ["consts"]:
        a = _np.ascontiguousarray(inputs[name]) if name != "consts" else constants()
        arrays[f"in_{name}_dram"] = a
        args.append(nc.dram_tensor(f"in_{name}_dram", a.shape, _mybir.dt.from_np(a.dtype),
                                   kind="ExternalInput").ap())
    args.append(nc.dram_tensor("out_0_dram", (1, SEQ, D_MODEL), _mybir.dt.float32,
                               kind="ExternalOutput").ap())
    build(nc, *args)
    r = _run(nc, [arrays], core_ids=[0])
    return r.results[0]["out_0_dram"]
```
